# Optimizing a Trainium2 kernel written in Bass

```python
import math
import jax, jax.numpy as jnp
from jax import lax
import numpy as np

D_MODEL = 1024
BATCH = 1
SEQ = 1024
DEPTH = 1

HEAD_DIM = 64
NSA_HEADS = 8
NSA_KV_GROUPS = 2
NSA_HPG = NSA_HEADS // NSA_KV_GROUPS
FOX_HEADS = 8
CMP_LEN = 32
CMP_STRIDE = 16
SEL_LEN = 64
N_SEL = 16
WINDOW = 512
Q_BLOCK = 128
N_EXPERT_GROUPS = 4
EXPERTS_PER_GROUP = 8
N_EXPERTS = N_EXPERT_GROUPS * EXPERTS_PER_GROUP
EXPERT_TOP_K = 2
D_EXPERT = D_MODEL // 2
MOE_BLOCK = 128
NORM_EPS = 1e-6
NEG = -1e30
FORCE = 1e9

NSA_W = NSA_HEADS * HEAD_DIM
NSA_KV_W = NSA_KV_GROUPS * HEAD_DIM
FOX_W = FOX_HEADS * HEAD_DIM
IN_SIZES = (NSA_W, 6 * NSA_KV_W, 3 * NSA_HEADS, 3 * FOX_W, FOX_HEADS, 2 * D_MODEL)
D_IN = sum(IN_SIZES)
IN_SPLITS = tuple(int(v) for v in np.cumsum(IN_SIZES)[:-1])

kernel_name = "hybrid_nsa_fox_hmoe_block"

def rmsnorm(x, g):
    xf = x.astype(jnp.float32)
    y = xf * lax.rsqrt(jnp.mean(xf * xf, axis=-1, keepdims=True) + NORM_EPS)
    return (y * g.astype(jnp.float32)).astype(x.dtype)

def masked_softmax(logits, mask):
    l = jnp.where(mask, logits.astype(jnp.float32), NEG)
    m = jnp.max(l, axis=-1, keepdims=True)
    e = jnp.where(mask, jnp.exp(l - m), 0.0)
    return e / jnp.maximum(jnp.sum(e, axis=-1, keepdims=True), 1e-30)

def alibi_slopes(n):
    return jnp.exp2(-8.0 * jnp.arange(1, n + 1, dtype=jnp.float32) / n)

def compress_blocks(kv, pe, w1, w2):
    S = kv.shape[2]
    n_cmp = (S - CMP_LEN) // CMP_STRIDE + 1
    idx = jnp.arange(n_cmp)[:, None] * CMP_STRIDE + jnp.arange(CMP_LEN)[None, :]
    blocks = kv[:, :, idx] + pe
    hid = jax.nn.gelu(jnp.einsum('bgnld,lde->bgne', blocks, w1))
    return hid @ w2

def nsa_attention(q, k_cmp, v_cmp, k_slc, v_slc, k_win, v_win, gates,
                  pe_k, w1_k, w2_k, pe_v, w1_v, w2_v):
    B, S = q.shape[0], q.shape[1]
    G, HPG, dh = NSA_KV_GROUPS, NSA_HPG, HEAD_DIM
    n_cmp = (S - CMP_LEN) // CMP_STRIDE + 1
    n_slc = S // SEL_LEN
    n_sel = min(N_SEL, n_slc)
    scale = HEAD_DIM ** -0.5
    tr = lambda a: a.transpose(0, 2, 1, 3)
    kc = compress_blocks(tr(k_cmp), pe_k, w1_k, w2_k)
    vc = compress_blocks(tr(v_cmp), pe_v, w1_v, w2_v)
    cmp_start = jnp.arange(n_cmp) * CMP_STRIDE
    cmp_end = cmp_start + CMP_LEN - 1
    slc_start = jnp.arange(n_slc) * SEL_LEN
    overlap = ((cmp_start[:, None] < slc_start[None, :] + SEL_LEN)
               & (cmp_end[:, None] >= slc_start[None, :])).astype(jnp.float32)
    ks_blocks = tr(k_slc).reshape(B, G, n_slc, SEL_LEN * dh)
    vs_blocks = tr(v_slc).reshape(B, G, n_slc, SEL_LEN * dh)
    pad = ((0, 0), (0, 0), (WINDOW, 0), (0, 0))
    kw = jnp.pad(tr(k_win), pad)
    vw = jnp.pad(tr(v_win), pad)
    qg = q.reshape(B, S, G, HPG, dh).transpose(0, 2, 3, 1, 4)
    gt = gates.reshape(B, S, G, HPG, 3).transpose(0, 2, 3, 1, 4)
    slopes = alibi_slopes(NSA_HEADS).reshape(G, HPG)[None, :, :, None, None]
    j_idx = jnp.arange(n_slc)

    def block(i):
        q0 = i * Q_BLOCK
        qb = lax.dynamic_slice_in_dim(qg, q0, Q_BLOCK, axis=3)
        gb = lax.dynamic_slice_in_dim(gt, q0, Q_BLOCK, axis=3)
        t = q0 + jnp.arange(Q_BLOCK)
        dc = (t[:, None] - cmp_end[None, :]).astype(jnp.float32)
        lc = jnp.einsum('bghqd,bgnd->bghqn', qb, kc).astype(jnp.float32) * scale - slopes * dc
        pc = masked_softmax(lc, dc >= 0)
        oc = jnp.einsum('bghqn,bgnd->bghqd', pc.astype(vc.dtype), vc)
        imp = jnp.einsum('bghqn,nj->bgqj', pc, overlap)
        cur = (t // SEL_LEN)[:, None]
        forced = (j_idx[None] == 0) | (j_idx[None] == cur) | (j_idx[None] == cur - 1)
        imp = jnp.where(j_idx[None] > cur, -FORCE, jnp.where(forced, FORCE, imp))
        _, sel = lax.top_k(imp, n_sel)
        flat = sel.reshape(B, G, Q_BLOCK * n_sel, 1)
        ks = jnp.take_along_axis(ks_blocks, flat, axis=2).reshape(B, G, Q_BLOCK, n_sel * SEL_LEN, dh)
        vs = jnp.take_along_axis(vs_blocks, flat, axis=2).reshape(B, G, Q_BLOCK, n_sel * SEL_LEN, dh)
        pos = (sel[..., None] * SEL_LEN + jnp.arange(SEL_LEN)).reshape(B, G, Q_BLOCK, n_sel * SEL_LEN)
        ds = (t[:, None] - pos)[:, :, None]
        ls = jnp.einsum('bghqd,bgqkd->bghqk', qb, ks).astype(jnp.float32) * scale - slopes * ds.astype(jnp.float32)
        ps = masked_softmax(ls, ds >= 0)
        osel = jnp.einsum('bghqk,bgqkd->bghqd', ps.astype(vs.dtype), vs)
        kwb = lax.dynamic_slice_in_dim(kw, q0, WINDOW + Q_BLOCK, axis=2)
        vwb = lax.dynamic_slice_in_dim(vw, q0, WINDOW + Q_BLOCK, axis=2)
        s = q0 - WINDOW + jnp.arange(WINDOW + Q_BLOCK)
        dw = t[:, None] - s[None, :]
        mw = (dw >= 0) & (dw < WINDOW) & (s[None, :] >= 0)
        lw = jnp.einsum('bghqd,bgkd->bghqk', qb, kwb).astype(jnp.float32) * scale - slopes * dw.astype(jnp.float32)
        pw = masked_softmax(lw, mw)
        ow = jnp.einsum('bghqk,bgkd->bghqd', pw.astype(vwb.dtype), vwb)
        return gb[..., 0:1] * oc + gb[..., 1:2] * osel + gb[..., 2:3] * ow

    out = lax.map(block, jnp.arange(S // Q_BLOCK))
    return out.transpose(1, 0, 4, 2, 3, 5).reshape(B, S, NSA_W)

def forgetting_attention(q, k, v, f_logit):
    B, S = q.shape[0], q.shape[1]
    scale = HEAD_DIM ** -0.5
    F = jnp.cumsum(jax.nn.log_sigmoid(f_logit.astype(jnp.float32)), axis=1).transpose(0, 2, 1)
    qh, kh, vh = (a.transpose(0, 2, 1, 3) for a in (q, k, v))
    outs = []
    for i in range(S // Q_BLOCK):
        q0, kend = i * Q_BLOCK, (i + 1) * Q_BLOCK
        l = (jnp.einsum('bhqd,bhkd->bhqk', qh[:, :, q0:kend], kh[:, :, :kend]).astype(jnp.float32) * scale
             + F[:, :, q0:kend, None] - F[:, :, None, :kend])
        mask = jnp.arange(kend)[None, :] <= jnp.arange(q0, kend)[:, None]
        p = masked_softmax(l, mask)
        outs.append(jnp.einsum('bhqk,bhkd->bhqd', p.astype(vh.dtype), vh[:, :, :kend]))
    o = jnp.concatenate(outs, axis=2)
    return o.transpose(0, 2, 1, 3).reshape(B, S, FOX_W)

def hierarchical_moe(h, w_rg, b_rg, w_re, b_re, w_gate, w_up, w_down):
    T, D = h.shape
    pg = jax.nn.softmax((h @ w_rg + b_rg).astype(jnp.float32), axis=-1)
    pg_top, g_idx = lax.top_k(pg, 1)
    le = (h @ w_re + b_re).astype(jnp.float32).reshape(T, N_EXPERT_GROUPS, EXPERTS_PER_GROUP)
    le = jnp.take_along_axis(le, g_idx[:, :, None], axis=1)[:, 0]
    top_l, e_local = lax.top_k(le, EXPERT_TOP_K)
    weight = pg_top * jax.nn.softmax(top_l, axis=-1)
    expert = g_idx * EXPERTS_PER_GROUP + e_local
    A = T * EXPERT_TOP_K
    e_flat = expert.reshape(A)
    w_flat = weight.reshape(A)
    tok = jnp.arange(A, dtype=jnp.int32) // EXPERT_TOP_K
    order = jnp.argsort(e_flat)
    e_s, tok_s, w_s = e_flat[order], tok[order], w_flat[order]
    counts = jnp.bincount(e_flat, length=N_EXPERTS)
    padded = (counts + MOE_BLOCK - 1) // MOE_BLOCK * MOE_BLOCK
    pad_end = jnp.cumsum(padded)
    pad_start = pad_end - padded
    raw_start = jnp.cumsum(counts) - counts
    dest = pad_start[e_s] + jnp.arange(A) - raw_start[e_s]
    cap = -(-(A + N_EXPERTS * (MOE_BLOCK - 1)) // MOE_BLOCK) * MOE_BLOCK
    n_blocks = cap // MOE_BLOCK
    buf_tok = jnp.zeros((cap,), jnp.int32).at[dest].set(tok_s)
    buf_w = jnp.zeros((cap,), jnp.float32).at[dest].set(w_s)
    block_expert = jnp.minimum(jnp.searchsorted(pad_end, jnp.arange(n_blocks) * MOE_BLOCK, side='right'), N_EXPERTS - 1)
    xb = h[buf_tok].reshape(n_blocks, MOE_BLOCK, D)

    def expert_block(args):
        xe, e = args
        return (jax.nn.silu(xe @ w_gate[e]) * (xe @ w_up[e])) @ w_down[e]

    yb = lax.map(expert_block, (xb, block_expert)).reshape(cap, D)
    return jnp.zeros((T, D), h.dtype).at[buf_tok].add(yb * buf_w[:, None].astype(h.dtype))

def setup_inputs(seed: int = 0) -> dict:
    key = jax.random.key(seed)
    ks = jax.random.split(key, 26)
    f32 = jnp.float32
    L = DEPTH
    nrm = lambda k, shape, fan: jax.random.normal(k, shape, f32) * fan ** -0.5
    gain = lambda k: 1.0 + 0.05 * jax.random.normal(k, (L, D_MODEL), f32)
    return {
        "x": jax.random.normal(ks[0], (BATCH, SEQ, D_MODEL), f32),
        "c": jax.random.normal(ks[1], (BATCH, D_MODEL), f32),
        "w_ada": 0.5 * nrm(ks[2], (L, D_MODEL, 6 * D_MODEL), D_MODEL),
        "b_ada": 0.02 * jax.random.normal(ks[3], (L, 6 * D_MODEL), f32),
        "g_pre_mix": gain(ks[4]),
        "g_post_mix": gain(ks[5]),
        "g_pre_ffn": gain(ks[6]),
        "g_post_ffn": gain(ks[7]),
        "w_in": nrm(ks[8], (L, D_MODEL, D_IN), D_MODEL),
        "b_forget": jax.random.uniform(ks[9], (L, FOX_HEADS), f32, 1.0, 6.0),
        "cmp_pe_k": 0.1 * jax.random.normal(ks[10], (L, CMP_LEN, HEAD_DIM), f32),
        "cmp_w1_k": nrm(ks[11], (L, CMP_LEN, HEAD_DIM, HEAD_DIM), CMP_LEN * HEAD_DIM),
        "cmp_w2_k": nrm(ks[12], (L, HEAD_DIM, HEAD_DIM), HEAD_DIM),
        "cmp_pe_v": 0.1 * jax.random.normal(ks[13], (L, CMP_LEN, HEAD_DIM), f32),
        "cmp_w1_v": nrm(ks[14], (L, CMP_LEN, HEAD_DIM, HEAD_DIM), CMP_LEN * HEAD_DIM),
        "cmp_w2_v": nrm(ks[15], (L, HEAD_DIM, HEAD_DIM), HEAD_DIM),
        "w_o_nsa": nrm(ks[16], (L, NSA_W, D_MODEL), NSA_W),
        "w_o_fox": nrm(ks[17], (L, FOX_W, D_MODEL), FOX_W),
        "w_out": nrm(ks[18], (L, D_MODEL, D_MODEL), D_MODEL),
        "w_router_group": nrm(ks[19], (L, D_MODEL, N_EXPERT_GROUPS), D_MODEL),
        "b_router_group": 0.01 * jax.random.normal(ks[20], (L, N_EXPERT_GROUPS), f32),
        "w_router_expert": nrm(ks[21], (L, D_MODEL, N_EXPERTS), D_MODEL),
        "b_router_expert": 0.01 * jax.random.normal(ks[22], (L, N_EXPERTS), f32),
        "w_exp_gate": nrm(ks[23], (L, N_EXPERTS, D_MODEL, D_EXPERT), D_MODEL),
        "w_exp_up": nrm(ks[24], (L, N_EXPERTS, D_MODEL, D_EXPERT), D_MODEL),
        "w_exp_down": nrm(ks[25], (L, N_EXPERTS, D_EXPERT, D_MODEL), D_EXPERT),
    }

def reference(x, c, w_ada, b_ada, g_pre_mix, g_post_mix, g_pre_ffn, g_post_ffn, w_in, b_forget,
              cmp_pe_k, cmp_w1_k, cmp_w2_k, cmp_pe_v, cmp_w1_v, cmp_w2_v,
              w_o_nsa, w_o_fox, w_out, w_router_group, b_router_group, w_router_expert, b_router_expert,
              w_exp_gate, w_exp_up, w_exp_down):
    B, S, D = x.shape
    for l in range(DEPTH):
        mod = jax.nn.silu(c) @ w_ada[l] + b_ada[l]
        sh_m, sc_m, gt_m, sh_f, sc_f, gt_f = (m[:, None, :] for m in jnp.split(mod, 6, axis=-1))
        h = rmsnorm(x, g_pre_mix[l]) * (1 + sc_m) + sh_m
        proj = h @ w_in[l]
        q_a, kv_a, gl_a, qkv_b, f_b, mg = jnp.split(proj, IN_SPLITS, axis=-1)
        q_a = q_a.reshape(B, S, NSA_HEADS, HEAD_DIM)
        kcmp, vcmp, kslc, vslc, kwin, vwin = (a.reshape(B, S, NSA_KV_GROUPS, HEAD_DIM)
                                              for a in jnp.split(kv_a, 6, axis=-1))
        g_a = jax.nn.sigmoid(gl_a).reshape(B, S, NSA_HEADS, 3)
        y_a = nsa_attention(q_a, kcmp, vcmp, kslc, vslc, kwin, vwin, g_a,
                            cmp_pe_k[l], cmp_w1_k[l], cmp_w2_k[l], cmp_pe_v[l], cmp_w1_v[l], cmp_w2_v[l])
        q_b, k_b, v_b = (a.reshape(B, S, FOX_HEADS, HEAD_DIM) for a in jnp.split(qkv_b, 3, axis=-1))
        y_b = forgetting_attention(q_b, k_b, v_b, f_b + b_forget[l])
        g_merge_a, g_merge_b = jnp.split(jax.nn.sigmoid(mg), 2, axis=-1)
        mixed = (g_merge_a * (y_a @ w_o_nsa[l]) + g_merge_b * (y_b @ w_o_fox[l])) @ w_out[l]
        x = x + gt_m * rmsnorm(mixed, g_post_mix[l])
        h2 = rmsnorm(x, g_pre_ffn[l]) * (1 + sc_f) + sh_f
        y = hierarchical_moe(h2.reshape(B * S, D), w_router_group[l], b_router_group[l],
                             w_router_expert[l], b_router_expert[l],
                             w_exp_gate[l], w_exp_up[l], w_exp_down[l]).reshape(B, S, D)
        x = x + gt_f * rmsnorm(y, g_post_ffn[l])
    return x


_drawn_inputs = setup_inputs


def setup_inputs(seed=0):
    import zlib

    import numpy as np

    out = dict(_drawn_inputs(seed))
    spreads = {}
    factors = {'g_post_ffn': 4.124, 'cmp_pe_k': 5.979, 'b_router_group': 3.826, 'b_router_expert': 3.504}
    for name, (base, spread) in spreads.items():
        noise = np.random.default_rng([zlib.crc32(name.encode()), seed]).standard_normal(out[name].shape)
        drawn = base * np.exp(spread * noise) if base else spread * noise
        out[name] = __import__('jax').numpy.asarray(drawn.astype(out[name].dtype))
    for name, factor in factors.items():
        out[name] = (out[name] * factor).astype(out[name].dtype)
    return out
```

```python
from contextlib import ExitStack

import concourse.bass as bass
from concourse import mybir

ALU = mybir.AluOpType
ACT = mybir.ActivationFunctionType
AX = mybir.AxisListType
F32 = mybir.dt.float32
F32R = mybir.dt.float32r
I32 = mybir.dt.int32
U32 = mybir.dt.uint32

P = 128
S = 1024
D = 1024
NT = S // P
ND = D // P
HD = 64
NSA_HEADS, NSA_GROUPS, FOX_HEADS = 8, 2, 8
CMP_LEN, CMP_STRIDE = 32, 16
N_CMP = (S - CMP_LEN) // CMP_STRIDE + 1
WINDOW = 512
EPS = 1e-6
BIG = 1e30
N_GRP, PER_GRP = 4, 8
N_EXP = N_GRP * PER_GRP
D_EXP = D // 2
NEG_SCALE = -(HD ** -0.5)

C_QA = 0
C_KCMP, C_VCMP, C_KSLC, C_VSLC, C_KWIN, C_VWIN = (512 + 128 * i for i in range(6))
C_GL = 1280
C_QB, C_KB, C_VB = 1304, 1816, 2328
C_F = 2840
C_MG = 2848

N_OVF = 2 * S // (P + 1)
N_COL = N_EXP + N_OVF + 1

Q_SLOTS = 2


class Chain:

    def __init__(self, eng, sem, base=0):
        self.eng, self.sem, self.base, self.n = eng, sem, base, 0

    def link(self, instruction):
        instruction.then_inc(self.sem, 1)
        self.n += 1
        self.eng.wait_ge(self.sem, self.base + self.n)


def allocator(nc, ctx):
    def sb(name, shape, dt=F32):
        return ctx.enter_context(nc.sbuf_tensor(name, shape, dt))

    def ps(name, shape, dt=F32):
        return ctx.enter_context(nc.psum_tensor(name, shape, dt))

    def sem(name):
        return ctx.enter_context(nc.semaphore(name))

    return sb, ps, sem



class Constants:
    def __init__(self, sb):
        self.ident, self.ident_r = sb("ident", [P, P]), sb("ident_r", [P, P], F32R)
        self.ones, self.eps = sb("ones", [P, P]), sb("eps", [P, 1])
        self.csilu = sb("csilu", [P, ND])


def constants(nc, g, d):
    with ExitStack() as ctx:
        sb, ps, sem = allocator(nc, ctx)
        crow = sb("crow", [ND, P])
        ccol = sb("ccol", [P, ND])
        cexp = sb("cexp", [P, ND])
        cden = sb("cden", [P, ND])
        cps = ps("cps", [P, ND])
        loaded, made, turned, copied, exped, step = (
            sem(n) for n in ("c_loaded", "c_made", "c_turned", "c_copied", "c_exped", "c_step"))
        block = ctx.enter_context(nc.Block())

        @block.sync
        def _(sp):
            sp.dma_start(crow[:, :], d["c"].rearrange("a (k p) -> (a k) p", p=P)).then_inc(loaded, 16)

        @block.gpsimd
        def _(pool):
            pool.memset(g.ident[:, :], 0.0).then_inc(step, 1)
            pool.memset(g.ones[:, :], 1.0).then_inc(step, 1)
            pool.memset(g.eps[:, :], EPS).then_inc(step, 1)
            pool.wait_ge(step, 3)
            pool.affine_select(out=g.ident[:, :], in_=g.ident[:, :], compare_op=ALU.not_equal, fill=1.0,
                               base=0, pattern=[[-1, P]], channel_multiplier=1).then_inc(made, 1)

        @block.tensor
        def _(pe):
            pe.wait_ge(loaded, 16)
            pe.wait_ge(made, 1)
            pe.transpose(cps[:, :], crow[:, :], g.ident[0:ND, 0:ND]).then_inc(turned, 1)

        @block.scalar
        def _(act):
            act.wait_ge(turned, 1)
            act.activation(cexp[:, :], cps[:, :], ACT.Exp, scale=-1.0).then_inc(exped, 1)

        @block.vector
        def _(dve):
            dve.wait_ge(exped, 1)
            chain = Chain(dve, copied)
            chain.link(dve.tensor_copy(ccol[:, :], cps[:, :]))
            chain.link(dve.tensor_scalar_add(cden[:, :], cexp[:, :], 1.0))
            chain.link(dve.reciprocal(cexp[:, :], cden[:, :]))
            dve.tensor_tensor(g.csilu[:, :], ccol[:, :], cexp[:, :], ALU.mult).then_inc(copied, 1)


def modulation(nc, g, d, first, count, out):
    W = 512
    with ExitStack() as ctx:
        sb, ps, sem = allocator(nc, ctx)
        wada = [sb(f"wada{s}_{first}", [P, ND, W]) for s in range(2)]
        bias = [sb(f"bada{s}_{first}", [P, W]) for s in range(2)]
        part = [sb(f"mpart{s}_{first}", [P, W]) for s in range(2)]
        total = [ps(f"mtotal{s}_{first}", [P, W]) for s in range(2)]
        loaded = [sem(f"m_loaded{s}_{first}") for s in range(2)]
        step, summed, free = (sem(f"{n}_{first}") for n in ("m_step", "m_summed", "m_free"))
        STEPS = ND + 1
        block = ctx.enter_context(nc.Block())

        @block.sync
        def _(sp):
            with sp.Fori(0, count // 2) as r:
                for s in range(2):
                    n = r * 2 + s
                    sp.wait_ge(free, n + 1)
                    sp.dma_start(wada[s][:, :, :], d["w_ada"][0, :, bass.ds(n * W + first * W, W)]
                                 .rearrange("(k p) n -> p k n", p=P)).then_inc(loaded[s], 16)
                    sp.dma_start(bias[s][:, :], d["b_ada"][0:1, bass.ds(n * W + first * W, W)]
                                 .to_broadcast([P, W])).then_inc(loaded[s], 16)

        @block.tensor
        def _(pe):
            with pe.Fori(0, count // 2) as r:
                for s in range(2):
                    n = r * 2 + s
                    pe.wait_ge(step, n * STEPS + ND)
                    pe.matmul(total[s][:, :], g.ones[:, :], part[s][:, :], start=True, stop=True).then_inc(summed, 1)

        @block.vector
        def _(dve):
            dve.sem_inc(free, 2)
            with dve.Fori(0, count // 2) as r:
                for s in range(2):
                    n = r * 2 + s
                    dve.wait_ge(loaded[s], r * 32 + 32)
                    chain = Chain(dve, step, n * STEPS)
                    chain.link(dve.tensor_scalar(part[s][:, :], wada[s][:, 0, :], g.csilu[:, 0:1], None, ALU.mult))
                    for k in range(1, ND):
                        chain.link(dve.scalar_tensor_tensor(
                            out=part[s][:, :], in0=wada[s][:, k, :], scalar=g.csilu[:, k:k + 1],
                            in1=part[s][:, :], op0=ALU.mult, op1=ALU.add))
                    dve.wait_ge(summed, n + 1)
                    chain.link(dve.tensor_tensor(out[:, bass.ds(n * W, W)], total[s][:, :], bias[s][:, :], ALU.add))
                    dve.sem_inc(free, 1)



def normalise_input(nc, g, d, mod, hT):
    with ExitStack() as ctx:
        sb, ps, sem = allocator(nc, ctx)
        gain = sb("gain_pre", [P, D])
        scale = sb("scale_mix", [P, D])
        x = [sb(f"xt{s}", [P, D]) for s in range(2)]
        h = [sb(f"ht{s}", [P, D]) for s in range(2)]
        junk = sb("junk", [P, D])
        ms = [sb(f"ms{s}", [P, 1]) for s in range(2)]
        rstd = [sb(f"rstd{s}", [P, 1]) for s in range(2)]
        tps = [[ps(f"tps{s}{b}", [P, 512]) for b in range(2)] for s in range(2)]
        loaded = [sem(f"n_loaded{s}") for s in range(2)]
        gained, squared, pstep, scaled, shifted, turned, out_a, out_d = (
            sem(n) for n in ("n_gained", "n_squared", "n_pstep", "n_scaled", "n_shifted",
                             "n_turned", "n_out_a", "n_out_d"))
        block = ctx.enter_context(nc.Block())

        @block.sync
        def _(sp):
            sp.dma_start(gain[:, :], d["g_pre_mix"][0:1, :].to_broadcast([P, D])).then_inc(gained, 16)
            with sp.Fori(0, NT // 2) as r:
                for s in range(2):
                    i = r * 2 + s
                    sp.wait_ge(scaled, i + 1)
                    sp.dma_start(x[s][:, :], d["x"][0, bass.ds(i * P, P), :]).then_inc(loaded[s], 16)

        @block.scalar
        def _(act):
            with act.Fori(0, NT // 2) as r:
                for s in range(2):
                    i = r * 2 + s
                    act.wait_ge(loaded[s], r * 16 + 16)
                    act.wait_ge(scaled, i + 1)
                    act.activation(junk[:, :], x[s][:, :], ACT.Square, scale=D ** -0.5,
                                   accum_out=ms[s][:, :]).then_inc(squared, 1)
                    act.wait_ge(squared, i * 2 + 1)
                    act.activation(ms[s][:, :], ms[s][:, :], ACT.Sqrt, bias=g.eps[:, :]).then_inc(squared, 1)
                    act.wait_ge(turned, i + 1)
                    act.activation(hT[:, 0:4, bass.ds(i * P, P)],
                                   tps[s][0][:, :].rearrange("p (k t) -> p k t", t=P), ACT.Copy).then_inc(out_a, 1)

        @block.gpsimd
        def _(pool):
            with pool.Fori(0, NT // 2) as r:
                for s in range(2):
                    i = r * 2 + s
                    pool.wait_ge(scaled, i + 3)
                    pool.tensor_tensor(h[s][:, :], h[s][:, :], mod[:, 0:D], ALU.add).then_inc(shifted, 1)

        @block.vector
        def _(dve):
            dve.wait_ge(gained, 16)
            dve.scalar_tensor_tensor(out=scale[:, :], in0=mod[:, D:2 * D], scalar=1.0, in1=gain[:, :],
                                     op0=ALU.add, op1=ALU.mult).then_inc(scaled, 1)
            dve.wait_ge(scaled, 1)
            dve.sem_inc(scaled, 1)
            with dve.Fori(0, NT // 2) as r:
                for s in range(2):
                    i = r * 2 + s
                    dve.wait_ge(squared, i * 2 + 2)
                    dve.reciprocal(rstd[s][:, :], ms[s][:, :]).then_inc(pstep, 1)
                    dve.wait_ge(pstep, i + 1)
                    dve.wait_ge(out_d, i + 1)
                    dve.scalar_tensor_tensor(out=h[s][:, :], in0=x[s][:, :], scalar=rstd[s][:, :], in1=scale[:, :],
                                             op0=ALU.mult, op1=ALU.mult).then_inc(scaled, 1)
                    dve.wait_ge(turned, i + 1)
                    dve.tensor_copy(hT[:, 4:8, bass.ds(i * P, P)],
                                    tps[s][1][:, :].rearrange("p (k t) -> p k t", t=P)).then_inc(out_d, 1)

        @block.tensor
        def _(pe):
            pe.sem_inc(out_d, 2)
            pe.sem_inc(out_a, 2)
            with pe.Fori(0, NT // 2) as r:
                for s in range(2):
                    i = r * 2 + s
                    pe.wait_ge(shifted, i + 1)
                    pe.wait_ge(out_a, i + 1)
                    pe.wait_ge(out_d, i + 1)
                    for k in range(ND):
                        last = pe.transpose(tps[s][k // 4][:, (k % 4) * P:(k % 4 + 1) * P],
                                            h[s][:, k * P:(k + 1) * P], g.ident[:, :])
                    last.then_inc(turned, 1)



def gates_and_forget(nc, g, d, hT, gates, fsum_dram):
    NG = 3 * NSA_HEADS
    with ExitStack() as ctx:
        sb, ps, sem = allocator(nc, ctx)
        w = sb("w_small", [P, ND, NG + FOX_HEADS])
        bf = sb("b_forget_all", [P, FOX_HEADS])
        zero = sb("zero_f", [FOX_HEADS, S])
        f = sb("f_logit", [P, NT, FOX_HEADS])
        fneg = sb("f_neg", [P, NT, FOX_HEADS])
        fln = sb("f_ln", [P, NT, FOX_HEADS])
        gexp = sb("gate_exp", [P, NT, NG])
        fT = sb("f_turned", [FOX_HEADS, S])
        valid = sb("cmp_valid", [P, 1])
        logits = ps("small_logits", [P, NT, NG + FOX_HEADS])
        fps = [ps(f"fps{b}", [FOX_HEADS, 512]) for b in range(2)]
        loaded, made, multiplied, aexp, step, turned, stored = (
            sem(n) for n in ("g_loaded", "g_made", "g_multiplied", "g_exp", "g_step", "g_turned", "g_stored"))
        block = ctx.enter_context(nc.Block())

        @block.sync
        def _(sp):
            sp.dma_start(w[:, :, 0:NG], d["w_in"][0, :, C_GL:C_GL + NG].rearrange("(k p) n -> p k n", p=P)
                         ).then_inc(loaded, 16)
            sp.dma_start(w[:, :, NG:], d["w_in"][0, :, C_F:C_F + FOX_HEADS].rearrange("(k p) n -> p k n", p=P)
                         ).then_inc(loaded, 16)
            sp.dma_start(bf[:, :], d["b_forget"][0:1, :].to_broadcast([P, FOX_HEADS])).then_inc(loaded, 16)
            sp.wait_ge(step, 9)
            sp.dma_start(fsum_dram, fT[:, :]).then_inc(stored, 16)
            sp.wait_ge(stored, 16)

        @block.gpsimd
        def _(pool):
            pool.memset(valid[:, :], 1.0).then_inc(made, 1)
            pool.memset(zero[:, :], 0.0).then_inc(made, 1)
            pool.wait_ge(made, 2)
            pool.affine_select(out=valid[:, :], in_=valid[:, :], compare_op=ALU.is_ge, fill=0.0,
                               base=-(CMP_LEN - 1), pattern=[[0, 1]], channel_multiplier=1).then_inc(made, 1)

        @block.tensor
        def _(pe):
            pe.wait_ge(loaded, 48)
            for i in range(NT):
                for k in range(ND):
                    last = pe.matmul(logits[:, i, :], hT[:, k, i * P:(i + 1) * P], w[:, k, :],
                                     start=(k == 0), stop=(k == ND - 1))
            last.then_inc(multiplied, 1)
            pe.wait_ge(step, 7)
            for i in range(NT):
                last = pe.transpose(fps[i // 4][:, (i % 4) * P:(i % 4 + 1) * P], fln[:, i, :], g.ident[:, :])
            last.then_inc(turned, 1)

        @block.scalar
        def _(act):
            act.wait_ge(multiplied, 1)
            act.activation(gexp[:, :, :], logits[:, :, 0:NG], ACT.Exp, scale=-1.0).then_inc(aexp, 1)
            act.wait_ge(step, 3)
            act.activation(fln[:, :, :], fneg[:, :, :], ACT.Exp).then_inc(aexp, 1)
            act.wait_ge(aexp, 2)
            act.activation(fln[:, :, :], fln[:, :, :], ACT.Ln, bias=1.0).then_inc(aexp, 1)

        @block.vector
        def _(dve):
            dve.wait_ge(loaded, 48)
            dve.wait_ge(aexp, 1)
            chain = Chain(dve, step)
            chain.link(dve.tensor_tensor(f[:, :, :], logits[:, :, NG:],
                                         bf[:, :].unsqueeze(1).to_broadcast([P, NT, FOX_HEADS]), ALU.add))
            chain.link(dve.tensor_scalar(fneg[:, :, :], f[:, :, :], -1.0, None, ALU.mult))
            chain.link(dve.tensor_tensor(fneg[:, :, :], f[:, :, :], fneg[:, :, :], ALU.min))
            chain.link(dve.tensor_scalar_add(gexp[:, :, :], gexp[:, :, :], 1.0))
            chain.link(dve.reciprocal(gates[:, :, :], gexp[:, :, :]))
            dve.wait_ge(aexp, 3)
            chain.link(dve.tensor_scalar(f[:, :, :], f[:, :, :], 0.0, None, ALU.min))
            chain.link(dve.tensor_tensor(fln[:, :, :], f[:, :, :], fln[:, :, :], ALU.subtract))
            dve.wait_ge(made, 3)
            cmp_gates = gates[:, 0, :].rearrange("p (h b) -> p h b", b=3)[:, :, 0]
            chain.link(dve.tensor_scalar(cmp_gates, cmp_gates, valid[:, 0:1], None, ALU.mult))
            dve.wait_ge(turned, 1)
            dve.tensor_tensor_scan(fT[:, 0:512], fps[0][:, :], zero[:, 0:512], 0.0, ALU.add, ALU.add
                                   ).then_inc(turned, 1)
            dve.wait_ge(turned, 2)
            dve.tensor_tensor_scan(fT[:, 512:S], fps[1][:, :], zero[:, 512:S], fT[:, 511:512], ALU.add, ALU.add
                                   ).then_inc(step, 1)



CR_SCORE = 2
CR_TURN = 6
CR_LO = 2
CR_PV = 2
CR_COMB = 4
CR_FAC = 4
Y_CHUNKS = 2


class Unit:

    def __init__(self, h, i, k0, nk, br, first):
        self.h, self.i, self.k0, self.nk, self.br, self.first = h, i, k0, nk, br, first

    @property
    def chunks(self):
        return [(a, min(a + 512, self.nk)) for a in range(0, self.nk, 512)]


def n_chunks(units):
    return sum(len(u.chunks) for u in units)


class AttentionBuffers:

    def __init__(self, nc, ctx, tag):
        sb, ps, sem = allocator(nc, ctx)
        self.tag, self.counts = tag, {}
        self.S = [ps(f"{tag}_S{s}", [P, S]) for s in range(2)]
        self.T = [ps(f"{tag}_T{s}", [P, 512]) for s in range(2)]
        self.O = [ps(f"{tag}_O{s}", [P, 512]) for s in range(2)]
        self.X = [sb(f"{tag}_X{s}", [P, S]) for s in range(2)]
        self.PTh = [sb(f"{tag}_PTh{s}", [P, S], F32R) for s in range(2)]
        self.PTl = [sb(f"{tag}_PTl{s}", [P, S], F32R) for s in range(2)]
        self.low = sb(f"{tag}_low", [P, 4])
        self.rsum = sb(f"{tag}_rsum", [P, 4])
        self.rmax = sb(f"{tag}_rmax", [P, 4])
        self.inv = sb(f"{tag}_inv", [P, 4])
        self.fac = sb(f"{tag}_fac", [P, 4])
        self.y = sb(f"{tag}_y", [P, NT, P])
        self.scored, self.score_read = sem(f"{tag}_scored"), sem(f"{tag}_score_read")
        self.probs, self.turned = sem(f"{tag}_probs"), sem(f"{tag}_turned")
        self.hi_done, self.lo_done = sem(f"{tag}_hi_done"), sem(f"{tag}_lo_done")
        self.pv_done, self.sum_used = sem(f"{tag}_pv_done"), sem(f"{tag}_sum_used")
        self.inv_done, self.fac_ready = sem(f"{tag}_inv_done"), sem(f"{tag}_fac_ready")
        self.comb_step, self.combined = sem(f"{tag}_comb_step"), sem(f"{tag}_combined")
        self.proj_done, self.proj_a, self.proj_d = (sem(f"{tag}_proj_{n}") for n in ("done", "a", "d"))
        self.w_loaded, self.cleared = sem(f"{tag}_w_loaded"), sem(f"{tag}_cleared")


def in_register(eng, a, value):
    if eng.engine not in a.counts:
        a.counts[eng.engine] = eng.alloc_register(f"{a.tag}_count")
    eng.reg_mov(a.counts[eng.engine], value)
    return a.counts[eng.engine]


def attend_pe(pe, g, a, units, t, operands):
    N, C = len(units), n_chunks(units)
    before = [n_chunks(units[:n]) for n in range(N + 1)]
    u0, c0 = t * N, t * (C + Y_CHUNKS)

    def scores(n):
        u = units[n]
        q, ks, _, mask = operands(u)
        pe.wait_ge(a.score_read, u0 + n + 1)
        for lo, hi in u.chunks:
            out = a.S[n % 2][:, lo:hi]
            pe.matmul(out, q, ks[0][:, u.k0 + lo:u.k0 + hi], start=True, stop=False)
            if mask is not None and hi == u.nk:
                pe.matmul(a.S[n % 2][:, hi - P:hi], g.ident_r[:, :], mask, start=False, stop=False)
            last = pe.matmul(out, q, ks[1][:, u.k0 + lo:u.k0 + hi], start=False, stop=True)
        last.then_inc(a.scored, 1)

    def turn(n):
        u = units[n]
        pe.wait_ge(a.probs, u0 + n + 1)
        for j, (lo, hi) in enumerate(u.chunks):
            c = before[n] + j
            pe.wait_ge(a.lo_done, c0 + c + 1)
            for b in range(lo, hi, P):
                last = pe.transpose(a.T[c % 2][:, b - lo:b - lo + P], a.X[n % 2][:, b:b + P], g.ident[:, :])
            last.then_inc(a.turned, 1)

    def weigh(n):
        u = units[n]
        v = operands(u)[2]
        pe.wait_ge(a.lo_done, c0 + before[n + 1] + CR_LO)
        pe.wait_ge(a.combined, u0 + n + CR_COMB - 1)
        out = a.O[n % 2][:, 0:P]
        for b in range(0, u.nk, P):
            w = min(P, u.nk - b)
            pe.matmul(out, a.PTh[n % 2][0:w, b:b + P], v(b // P), start=(b == 0), stop=False)
            last = pe.matmul(out, a.PTl[n % 2][0:w, b:b + P], v(b // P), start=False, stop=(b + P >= u.nk))
        last.then_inc(a.pv_done, 1)

    scores(0)
    scores(1)
    for n in range(N):
        turn(n)
        if n + 2 < N:
            scores(n + 2)
        if n >= 1:
            weigh(n - 1)
    weigh(N - 1)
    pe.wait_ge(a.combined, u0 + N + CR_COMB)
    for half in range(2):
        pe.wait_ge(a.lo_done, c0 + C + half + 1)
        for i in range(4):
            last = pe.transpose(a.T[half][:, i * P:(i + 1) * P], a.y[:, 4 * half + i, :], g.ident[:, :])
        last.then_inc(a.turned, 1)


def attend_act(act, a, units, t):
    N, C = len(units), n_chunks(units)
    before = [n_chunks(units[:n]) for n in range(N + 1)]
    u0, c0, h0 = t * N, t * (C + Y_CHUNKS), t * C

    def exps(n):
        u = units[n]
        act.wait_ge(a.score_read, u0 + n + 1 + CR_SCORE)
        act.wait_ge(a.sum_used, u0 + n + 1)
        x = a.X[n % 2][:, 0:u.nk]
        act.activation(x, x, ACT.Exp, bias=a.low[:, n % 4:n % 4 + 1], scale=-1.0,
                       accum_out=a.rsum[:, n % 4:n % 4 + 1]).then_inc(a.probs, 1)

    def hi(n):
        u = units[n]
        act.wait_ge(a.pv_done, u0 + n + 1)
        for j, (lo, end) in enumerate(u.chunks):
            c = before[n] + j
            w = min(P, u.nk)
            cols = max(P, end - lo)
            act.wait_ge(a.turned, c0 + c + 1 + CR_TURN)
            act.activation(a.PTh[n % 2][0:w, lo:lo + cols], a.T[c % 2][0:w, 0:cols], ACT.Copy).then_inc(a.hi_done, 1)

    exps(0)
    exps(1)
    for n in range(N):
        hi(n)
        if n + 2 < N:
            exps(n + 2)


def attend_dve(dve, a, units, t, bias_of, gated, yT):
    N, C = len(units), n_chunks(units)
    before = [n_chunks(units[:n]) for n in range(N + 1)]
    u0, c0, h0 = t * N, t * (C + Y_CHUNKS), t * C

    def add_bias(n):
        u = units[n]
        dve.wait_ge(a.scored, u0 + n + 1)
        chunks = before[n - 1] if n >= 2 else before[N - 1 + n] - C - Y_CHUNKS
        count = in_register(dve, a, c0 + (chunks + CR_TURN))
        dve.wait_ge(a.score_read, CR_SCORE)
        dve.wait_ge(a.turned, count)
        dve.tensor_tensor_reduce(out=a.X[n % 2][:, 0:u.nk], in0=a.S[n % 2][:, 0:u.nk], in1=bias_of(u),
                                 scale=1.0, scalar=3e38, op0=ALU.add, op1=ALU.min,
                                 accum_out=a.low[:, n % 4:n % 4 + 1]).then_inc(a.score_read, 1)

    def lo(n):
        u = units[n]
        for j, (start, end) in enumerate(u.chunks):
            c = before[n] + j
            w = min(P, u.nk)
            cols = max(P, end - start)
            dve.wait_ge(a.hi_done, h0 + c + 1)
            dve.tensor_tensor(a.PTl[n % 2][0:w, start:start + cols], a.T[c % 2][0:w, 0:cols],
                              a.PTh[n % 2][0:w, start:start + cols].bitcast(F32), ALU.subtract
                              ).then_inc(a.lo_done, 1)

    def invert(n):
        c = slice(n % 4, n % 4 + 1)
        dve.wait_ge(a.sum_used, u0 + n + 1 + CR_FAC)
        dve.wait_ge(a.combined, u0 + n + 1)
        if gated:
            dve.reciprocal(a.inv[:, c], a.rmax[:, c]).then_inc(a.inv_done, 1)
        else:
            dve.reciprocal(a.fac[:, c], a.rmax[:, c]).then_inc(a.inv_done, 1)

    def combine(n):
        u = units[n]
        y = a.y[:, u.i, u.h * HD:(u.h + 1) * HD]
        f = a.fac[:, n % 4:n % 4 + 1]
        dve.wait_ge(a.pv_done, u0 + n + 1 + CR_PV)
        if gated:
            dve.wait_ge(a.fac_ready, u0 + n + 1)
        else:
            dve.wait_ge(a.inv_done, u0 + n + 1 + CR_FAC)
        dve.wait_ge(a.combined, u0 + n + CR_COMB)
        if u.first:
            dve.tensor_scalar(y, a.O[n % 2][:, 0:HD], f, None, ALU.mult).then_inc(a.comb_step, 1)
        else:
            dve.scalar_tensor_tensor(out=y, in0=a.O[n % 2][:, 0:HD], scalar=f, in1=y,
                                     op0=ALU.mult, op1=ALU.add).then_inc(a.comb_step, 1)
        dve.wait_ge(a.comb_step, u0 + n + 1)
        dve.scalar_tensor_tensor(out=y, in0=a.O[n % 2][:, HD:P], scalar=f, in1=y,
                                 op0=ALU.mult, op1=ALU.add).then_inc(a.combined, 1)

    add_bias(0)
    add_bias(1)
    for n in range(N):
        lo(n)
        if n + 2 < N:
            add_bias(n + 2)
        invert(n)
        if n >= 1:
            combine(n - 1)
    combine(N - 1)
    for half in range(2):
        dve.wait_ge(a.turned, c0 + C + half + 1 + CR_TURN)
        dve.tensor_copy(yT[:, bass.ds(t, 1), half * 512:(half + 1) * 512], a.T[half][:, :].unsqueeze(1)
                        ).then_inc(a.lo_done, 1)


def attend_pool(pool, a, units, t, gate_of):
    N = len(units)
    u0 = t * N

    def guard(n):
        c = slice(n % 4, n % 4 + 1)
        count = in_register(pool, a, u0 + n + 1)
        pool.wait_ge(a.sum_used, CR_FAC)
        pool.wait_ge(a.probs, count)
        pool.wait_ge(a.inv_done, count)
        pool.tensor_scalar(a.rmax[:, c], a.rsum[:, c], 1e-30, None, ALU.max).then_inc(a.sum_used, 1)

    def gate(n):
        c = slice(n % 4, n % 4 + 1)
        pool.wait_ge(a.inv_done, u0 + n + 1 + CR_FAC)
        pool.wait_ge(a.combined, u0 + n + 1)
        pool.tensor_tensor(a.fac[:, c], a.inv[:, c], gate_of(units[n]), ALU.mult).then_inc(a.fac_ready, 1)

    for n in range(N):
        guard(n)
        if gate_of is not None:
            gate(n)


def project_columns(pe, a, slot, w, hT):
    for half in range(2):
        for k in range(ND):
            last = pe.matmul(a.S[slot][:, half * 512:(half + 1) * 512], w[:, k, :],
                             hT[:, k, half * 512:(half + 1) * 512], start=(k == 0), stop=(k == ND - 1))
    last.then_inc(a.proj_done, 1)


def project_rows(pe, a, slot, w, hT):
    for i in range(NT):
        for k in range(ND):
            last = pe.matmul(a.S[slot][:, i * P:(i + 1) * P], hT[:, k, i * P:(i + 1) * P], w[:, k, :],
                             start=(k == 0), stop=(k == ND - 1))
    last.then_inc(a.proj_done, 1)


LOW, HIGH = slice(0, HD), slice(HD, P)


def queries_act(act, ps, q):
    act.activation(q[0][LOW, :], ps[LOW, :], ACT.Copy, scale=NEG_SCALE)
    return act.activation(q[1][LOW, :], ps[HIGH, :], ACT.Copy, scale=NEG_SCALE)


def queries_dve(dve, ps, q):
    for h, part in enumerate((LOW, HIGH)):
        last = dve.scalar_tensor_tensor(out=q[h][HIGH, :], in0=ps[part, :], scalar=NEG_SCALE,
                                        in1=q[h][LOW, :].bitcast(F32), op0=ALU.mult, op1=ALU.subtract)
    return last


def keys_act(act, ps, k_hi):
    for h, part in enumerate((LOW, HIGH)):
        act.activation(k_hi[h][LOW, :], ps[part, :], ACT.Copy)
        last = act.activation(k_hi[h][HIGH, :], ps[part, :], ACT.Copy)
    return last


def keys_dve(dve, ps, k_hi, k_lo):
    for h, part in enumerate((LOW, HIGH)):
        dve.tensor_tensor(k_lo[h][LOW, :], ps[part, :], k_hi[h][LOW, :].bitcast(F32), ALU.subtract)
        last = dve.tensor_tensor(k_lo[h][HIGH, :], ps[part, :], k_hi[h][LOW, :].bitcast(F32), ALU.subtract)
    return last


def values_act(act, ps, v):
    return act.activation(v[:, :, 0:HD], ps[:, :].rearrange("p (n e) -> p n e", e=HD), ACT.Copy)


def values_dve(dve, ps, v):
    return dve.tensor_tensor(v[:, :, HD:P], ps[:, :].rearrange("p (n e) -> p n e", e=HD),
                             v[:, :, 0:HD].bitcast(F32), ALU.subtract)


def fox(nc, g, d, hT, yT, fsum_dram, y_dram):
    units = [Unit(h=h, i=i, k0=0, nk=(i + 1) * P, br=0, first=True) for h in range(2) for i in range(NT)]
    N = len(units)
    PAIRS = FOX_HEADS // 2
    with ExitStack() as ctx:
        sb, ps, sem = allocator(nc, ctx)
        a = AttentionBuffers(nc, ctx, "fox")
        wq, wk, wv = (sb(f"fox_w{n}", [P, ND, P]) for n in "qkv")
        q = [sb(f"fox_q{h}", [P, S], F32R) for h in range(2)]
        k_hi = [sb(f"fox_kh{h}", [P, S], F32R) for h in range(2)]
        k_lo = [sb(f"fox_kl{h}", [P, S], F32R) for h in range(2)]
        v = sb("fox_v", [P, NT * 2, P], F32R)
        decay = sb("fox_decay", [P, 2, S])
        mask_f = sb("fox_mask_f", [P, P])
        mask = sb("fox_mask", [P, P], F32R)
        zero = sb("fox_zero", [P, D])
        masked, decayed, blank, blanked = (sem(f"fox_{n}") for n in ("masked", "decayed", "blank", "blanked"))
        block = ctx.enter_context(nc.Block())

        @block.sync
        def _(sp):
            with sp.Fori(0, PAIRS) as t:
                sp.wait_ge(a.proj_d, t * 3 + 1)
                for w, c in ((wq, C_QB), (wk, C_KB), (wv, C_VB)):
                    sp.dma_start(w[:, :, :], d["w_in"][0, :, bass.ds(t * P + c, P)].rearrange("(k p) n -> p k n", p=P)
                                 ).then_inc(a.w_loaded, 16)
                sp.wait_ge(a.score_read, t * N + CR_SCORE)
                for h in range(2):
                    sp.dma_start(decay[:, h, :], fsum_dram[bass.ds(t * 2 + h, 1), :].to_broadcast([P, S])
                                 ).then_inc(decayed, 16)
            sp.wait_ge(blank, 1)
            for j in range(N_OVF):
                sp.dma_start(y_dram[(N_EXP + j) * P:(N_EXP + j + 1) * P, :], zero[:, :]).then_inc(blanked, 16)
            sp.wait_ge(blanked, N_OVF * 16)

        def operands(u):
            return (q[u.h][:, u.i * P:(u.i + 1) * P], (k_hi[u.h], k_lo[u.h]),
                    lambda b: v[:, 2 * b + u.h, :], mask[:, :])

        @block.tensor
        def _(pe):
            pe.wait_ge(masked, 4)
            with pe.Fori(0, PAIRS) as t:
                pe.wait_ge(a.score_read, t * N + CR_SCORE)
                pe.wait_ge(a.w_loaded, t * 48 + 48)
                project_columns(pe, a, 0, wq, hT)
                project_columns(pe, a, 1, wk, hT)
                pe.wait_ge(a.proj_d, t * 3 + 2)
                project_rows(pe, a, 0, wv, hT)
                pe.wait_ge(a.proj_d, t * 3 + 4)
                attend_pe(pe, g, a, units, t, operands)

        @block.scalar
        def _(act):
            with act.Fori(0, PAIRS) as t:
                act.wait_ge(a.proj_done, t * 3 + 1)
                queries_act(act, a.S[0], q).then_inc(a.proj_a, 1)
                act.wait_ge(a.proj_done, t * 3 + 2)
                keys_act(act, a.S[1], k_hi).then_inc(a.proj_a, 1)
                act.wait_ge(a.proj_done, t * 3 + 3)
                values_act(act, a.S[0], v).then_inc(a.proj_a, 1)
                attend_act(act, a, units, t)

        @block.gpsimd
        def _(pool):
            pool.sem_inc(a.sum_used, CR_FAC)
            pool.memset(mask_f[:, :], 0.0).then_inc(masked, 1)
            pool.memset(zero[:, :], 0.0).then_inc(blank, 1)
            pool.wait_ge(masked, 1)
            pool.affine_select(out=mask_f[:, :], in_=mask_f[:, :], compare_op=ALU.is_ge, fill=2.0 ** 99, base=0,
                               pattern=[[-1, P]], channel_multiplier=1).then_inc(masked, 1)
            with pool.Fori(0, PAIRS) as t:
                attend_pool(pool, a, units, t, None)

        @block.vector
        def _(dve):
            dve.sem_inc(a.score_read, CR_SCORE)
            dve.sem_inc(a.lo_done, CR_LO)
            dve.sem_inc(a.combined, CR_COMB)
            dve.sem_inc(a.pv_done, CR_PV)
            dve.sem_inc(a.turned, CR_TURN)
            dve.sem_inc(a.proj_d, 1)
            dve.sem_inc(a.inv_done, CR_FAC)
            dve.wait_ge(masked, 2)
            dve.tensor_copy(mask[:, :], mask_f[:, :]).then_inc(masked, 1)
            dve.tensor_copy(g.ident_r[:, :], g.ident[:, :]).then_inc(masked, 1)
            with dve.Fori(0, PAIRS) as t:
                dve.wait_ge(a.proj_a, t * 3 + 1)
                queries_dve(dve, a.S[0], q).then_inc(a.proj_d, 1)
                dve.wait_ge(a.proj_a, t * 3 + 2)
                keys_dve(dve, a.S[1], k_hi, k_lo).then_inc(a.proj_d, 1)
                dve.wait_ge(a.proj_a, t * 3 + 3)
                values_dve(dve, a.S[0], v).then_inc(a.proj_d, 1)
                dve.wait_ge(decayed, t * 32 + 32)
                attend_dve(dve, a, units, t, lambda u: decay[:, u.h, 0:u.nk], False, yT)


def compression_constants(nc, g, d, w1, w2, pec):
    with ExitStack() as ctx:
        sb, ps, sem = allocator(nc, ctx)
        pe_rows = sb("pe_rows", [CMP_LEN, P])
        pe_cols = sb("pe_cols", [P, CMP_LEN])
        pe_ps = ps("pe_ps", [P, CMP_LEN])
        pec_ps = ps("pec_ps", [P, 1])
        cleared, loaded, multiplied, copied = (
            sem(n) for n in ("k_cleared", "k_loaded", "k_multiplied", "k_copied"))
        block = ctx.enter_context(nc.Block())

        @block.gpsimd
        def _(pool):
            pool.memset(w1[LOW, :, HIGH], 0.0).then_inc(cleared, 1)
            pool.memset(w1[HIGH, :, LOW], 0.0).then_inc(cleared, 1)
            pool.memset(w2[LOW, HIGH], 0.0).then_inc(cleared, 1)
            pool.memset(w2[HIGH, LOW], 0.0).then_inc(cleared, 1)

        @block.sync
        def _(sp):
            for part, x, y, z in ((LOW, d["cmp_w1_k"], d["cmp_w2_k"], d["cmp_pe_k"]), (HIGH, d["cmp_w1_v"], d["cmp_w2_v"], d["cmp_pe_v"])):
                sp.dma_start(w1[part, :, part], x[0].rearrange("l d e -> d l e")).then_inc(loaded, 16)
                sp.dma_start(w2[part, part], y[0]).then_inc(loaded, 16)
                sp.dma_start(pe_rows[:, part], z[0]).then_inc(loaded, 16)

        @block.tensor
        def _(pe):
            pe.wait_ge(loaded, 96)
            pe.wait_ge(cleared, 4)
            pe.transpose(pe_ps[:, :], pe_rows[:, :], g.ident[0:CMP_LEN, 0:CMP_LEN]).then_inc(multiplied, 1)
            pe.wait_ge(copied, 1)
            for l in range(CMP_LEN):
                last = pe.matmul(pec_ps[:, :], w1[:, l, :], pe_cols[:, l:l + 1], start=(l == 0), stop=(l == CMP_LEN - 1))
            last.then_inc(multiplied, 1)

        @block.vector
        def _(dve):
            dve.wait_ge(multiplied, 1)
            dve.tensor_copy(pe_cols[:, :], pe_ps[:, :]).then_inc(copied, 1)
            dve.wait_ge(multiplied, 2)
            dve.tensor_copy(pec[:, :], pec_ps[:, :]).then_inc(copied, 1)


def nsa(nc, g, d, hT, yT, gates, room):
    CMP, SEL, WIN = range(3)
    units = []
    for h in range(2):
        for i in range(NT):
            k0 = max(0, i * P - WINDOW)
            units += [Unit(h=h, i=i, br=CMP, k0=0, nk=HD, first=True),
                      Unit(h=h, i=i, br=SEL, k0=0, nk=(i + 1) * P, first=False),
                      Unit(h=h, i=i, br=WIN, k0=k0, nk=(i + 1) * P - k0, first=False)]
    N = len(units)
    W_CMP = NT * HD
    W_WIN = WINDOW + P
    X_SEL, X_WIN, X_CMP = 0, S, S + W_WIN
    W_TAB = S + W_WIN + W_CMP
    PPG = NSA_HEADS // NSA_GROUPS // 2
    G_TILES = 3 + PPG
    GELU_A, GELU_B = 0.044715, 2 * (2 / 3.141592653589793) ** 0.5
    with ExitStack() as ctx:
        sb, ps, sem = allocator(nc, ctx)
        w1 = sb("cmp_w1", [P, CMP_LEN, P])
        w2 = sb("cmp_w2", [P, P])
        pec = sb("cmp_pec", [P, 1])
        compression_constants(nc, g, d, w1, w2, pec)
        a = AttentionBuffers(nc, ctx, "nsa")
        wq, wk, wv, wc = (sb(f"nsa_w{n}", [P, ND, P]) for n in "qkvc")
        q = [sb(f"nsa_q{h}", [P, S], F32R) for h in range(2)]
        k_hi = [sb(f"nsa_kh{b}", [P, S], F32R) for b in range(2)]
        k_lo = [sb(f"nsa_kl{b}", [P, S], F32R) for b in range(2)]
        v = sb("nsa_v", [P, NT * 2, P], F32R)
        kvc = sb("nsa_kvc", [P, S])
        hid = sb("cmp_hid", [P, N_CMP])
        cube = sb("cmp_cube", [P, N_CMP])
        act_out = sb("cmp_exp", [P, N_CMP])
        hidT = sb("cmp_hidT", [P, HD])
        kc_hi = sb("cmp_kh", [P, HD], F32R)
        kc_lo = sb("cmp_kl", [P, HD], F32R)
        vc = sb("cmp_v", [HD, P], F32R)
        dist = room[:, 0:W_TAB]
        bias = room[:, W_TAB:3 * W_TAB].rearrange("p (h n) -> p h n", h=2)
        pair_gates = sb("pair_gates", [P, NT, 6])
        w_group, cmp_pe, cmp_act, cmp_dve, tables, made = (
            sem(n) for n in ("nsa_w_group", "cmp_pe", "cmp_act", "cmp_dve", "tables", "dist_made"))
        C_DVE, C_ACT, C_PE = 9, 4, 2
        block = ctx.enter_context(nc.Block())

        @block.sync
        def _(sp):
            with sp.Fori(0, NSA_GROUPS) as grp:
                sp.wait_ge(a.proj_d, grp * G_TILES + 1)
                for w, half, c in ((wc, LOW, C_KCMP), (wc, HIGH, C_VCMP), (wk, LOW, C_KSLC), (wk, HIGH, C_KWIN),
                                   (wv, LOW, C_VSLC), (wv, HIGH, C_VWIN)):
                    sp.dma_start(w[:, :, half], d["w_in"][0, :, bass.ds(grp * HD + c, HD)].rearrange("(k p) n -> p k n", p=P)
                                 ).then_inc(w_group, 16)
                with sp.Fori(0, PPG) as pr:
                    t = grp * PPG + pr
                    sp.wait_ge(a.proj_d, grp * G_TILES + pr * 4 + 1)
                    sp.dma_start(wq[:, :, :], d["w_in"][0, :, bass.ds(t * P + C_QA, P)].rearrange("(k p) n -> p k n", p=P)
                                 ).then_inc(a.w_loaded, 16)

        def operands(u):
            tile = slice(u.i * P, (u.i + 1) * P)
            if u.br == CMP:
                return q[u.h][:, tile], (kc_hi, kc_lo), lambda b: vc[:, :], None
            b = u.br - SEL
            return (q[u.h][:, tile], (k_hi[b], k_lo[b]),
                    lambda n: v[:, 2 * (u.k0 // P + n) + b, :], None)

        def bias_of(u):
            if u.br == CMP:
                lo = X_CMP + u.i * HD
            elif u.br == SEL:
                lo = X_SEL + S - u.nk
            else:
                lo = X_WIN + W_WIN - u.nk
            return bias[:, u.h, lo:lo + u.nk]

        @block.tensor
        def _(pe):
            with pe.Fori(0, NSA_GROUPS) as grp:
                pe.wait_ge(a.score_read, grp * (PPG * N) + CR_SCORE)
                pe.wait_ge(w_group, grp * 96 + 96)
                project_columns(pe, a, 0, wc, hT)
                project_columns(pe, a, 1, wk, hT)
                pe.wait_ge(a.proj_d, grp * G_TILES + 2)
                project_rows(pe, a, 0, wv, hT)
                pe.wait_ge(a.combined, grp * (PPG * N) + CR_COMB)
                for l in range(CMP_LEN):
                    last = pe.matmul(a.O[0][:, 0:N_CMP], w1[:, l, :],
                                     kvc[:, l:l + CMP_STRIDE * (N_CMP - 1) + 1:CMP_STRIDE],
                                     start=(l == 0), stop=(l == CMP_LEN - 1))
                last.then_inc(cmp_pe, 1)
                pe.wait_ge(cmp_dve, grp * C_DVE + 7)
                pe.matmul(a.O[1][:, 0:HD], w2[:, :], hidT[:, :], start=True, stop=True)
                pe.matmul(a.O[1][0:HD, HD:P], hidT[:, :], w2[:, HIGH], start=True, stop=True).then_inc(cmp_pe, 1)
                with pe.Fori(0, PPG) as pr:
                    t = grp * PPG + pr
                    pe.wait_ge(cmp_dve, grp * C_DVE + C_DVE)
                    pe.wait_ge(a.score_read, t * N + CR_SCORE)
                    pe.wait_ge(a.proj_d, grp * G_TILES + pr + 4)
                    pe.wait_ge(a.w_loaded, t * 16 + 16)
                    project_columns(pe, a, 1, wq, hT)
                    pe.wait_ge(a.proj_d, grp * G_TILES + pr + 5)
                    attend_pe(pe, g, a, units, t, operands)

        @block.scalar
        def _(act):
            with act.Fori(0, NSA_GROUPS) as grp:
                act.wait_ge(a.proj_done, grp * G_TILES + 1)
                act.activation(kvc[:, 0:512], a.S[0][:, 0:512], ACT.Copy).then_inc(a.proj_a, 1)
                act.wait_ge(a.proj_done, grp * G_TILES + 2)
                keys_act(act, a.S[1], k_hi).then_inc(a.proj_a, 1)
                act.wait_ge(a.proj_done, grp * G_TILES + 3)
                values_act(act, a.S[0], v).then_inc(a.proj_a, 1)
                act.wait_ge(cmp_dve, grp * C_DVE + 4)
                act.activation(act_out[:, :], cube[:, :], ACT.Exp, scale=-GELU_B).then_inc(cmp_act, 1)
                act.wait_ge(cmp_pe, grp * C_PE + 2)
                act.activation(kc_hi[LOW, :], a.O[1][LOW, 0:HD], ACT.Copy).then_inc(cmp_act, 1)
                act.activation(kc_hi[HIGH, :], a.O[1][LOW, 0:HD], ACT.Copy).then_inc(cmp_act, 1)
                act.activation(vc[:, 0:HD], a.O[1][LOW, HD:P], ACT.Copy).then_inc(cmp_act, 1)
                with act.Fori(0, PPG) as pr:
                    t = grp * PPG + pr
                    act.wait_ge(a.proj_done, grp * G_TILES + pr + 4)
                    queries_act(act, a.S[1], q).then_inc(a.proj_a, 1)
                    attend_act(act, a, units, t)

        @block.gpsimd
        def _(pool):
            pool.sem_inc(a.sum_used, CR_FAC)
            for s in range(2):
                pool.memset(a.X[s][:, 0:P], 0.0).then_inc(a.cleared, 1)
            pool.memset(hidT[:, :], 0.0).then_inc(made, 1)
            tab = dict(allow_small_or_imprecise_dtypes=True, channel_multiplier=1)
            pool.iota(dist[:, X_SEL:X_SEL + S], pattern=[[-1, S]], base=S - P, **tab).then_inc(made, 1)
            pool.iota(dist[:, X_WIN:X_WIN + W_WIN], pattern=[[-1, W_WIN]], base=WINDOW, **tab).then_inc(made, 1)
            pool.iota(dist[:, X_CMP:], pattern=[[P, NT], [-CMP_STRIDE, HD]], base=1 - CMP_LEN, **tab).then_inc(made, 1)
            pool.wait_ge(made, 4)

            def keep(lo, hi, pattern, base, mult):
                pool.affine_select(out=dist[:, lo:hi], in_=dist[:, lo:hi], compare_op=ALU.is_ge, fill=BIG,
                                   base=base, pattern=pattern, channel_multiplier=mult).then_inc(made, 1)

            keep(X_SEL, X_SEL + S, [[-1, S]], S - P, 1)
            keep(X_WIN, X_WIN + W_WIN, [[-1, W_WIN]], WINDOW, 1)
            keep(X_CMP, W_TAB, [[P, NT], [-CMP_STRIDE, HD]], 1 - CMP_LEN, 1)
            pool.wait_ge(made, 6)
            keep(X_WIN, X_WIN + W_WIN, [[1, W_WIN]], -1, -1)
            pool.wait_ge(made, 8)
            with pool.Fori(0, NSA_GROUPS) as grp:
                with pool.Fori(0, PPG) as pr:
                    t = grp * PPG + pr
                    count = in_register(pool, a, t * N + CR_SCORE)
                    pool.wait_ge(made, 7)
                    pool.wait_ge(a.score_read, count)
                    pool.tensor_scalar(bias[:, 0, :], dist[:, :], 0.5, None, ALU.mult).then_inc(tables, 1)
                    pool.tensor_scalar(bias[:, 1, :], dist[:, :], 0.25, None, ALU.mult).then_inc(tables, 1)
                    pool.wait_ge(a.combined, t * N + CR_COMB)
                    pool.tensor_copy(pair_gates[:, :, :], gates[:, :, bass.ds(t * 6, 6)]).then_inc(tables, 1)
                    count = in_register(pool, a, t * 4 + 3)
                    pool.wait_ge(made, 7)
                    pool.wait_ge(tables, count)
                    pool.tensor_scalar(dist[:, :], dist[:, :], 0.25, None, ALU.mult).then_inc(tables, 1)
                    attend_pool(pool, a, units, t, lambda u: pair_gates[:, u.i, 3 * u.h + u.br:3 * u.h + u.br + 1])
                    pool.wait_ge(tables, t * 4 + 4)

        @block.vector
        def _(dve):
            dve.sem_inc(a.score_read, CR_SCORE)
            dve.sem_inc(a.lo_done, CR_LO)
            dve.sem_inc(a.combined, CR_COMB)
            dve.sem_inc(a.pv_done, CR_PV)
            dve.sem_inc(a.turned, CR_TURN)
            dve.sem_inc(a.proj_d, 1)
            dve.sem_inc(a.inv_done, CR_FAC)
            dve.wait_ge(a.cleared, 2)
            dve.wait_ge(made, 1)
            with dve.Fori(0, NSA_GROUPS) as grp:
                dve.wait_ge(a.proj_done, grp * G_TILES + 1)
                dve.wait_ge(a.proj_a, grp * G_TILES + 1)
                dve.tensor_copy(kvc[:, 512:S], a.S[0][:, 512:S]).then_inc(a.proj_d, 1)
                dve.wait_ge(a.proj_a, grp * G_TILES + 2)
                keys_dve(dve, a.S[1], k_hi, k_lo).then_inc(a.proj_d, 1)
                dve.wait_ge(a.proj_a, grp * G_TILES + 3)
                values_dve(dve, a.S[0], v).then_inc(a.proj_d, 1)
                dve.wait_ge(cmp_pe, grp * C_PE + 1)
                chain = Chain(dve, cmp_dve, grp * C_DVE)
                chain.link(dve.tensor_scalar(hid[:, :], a.O[0][:, 0:N_CMP], pec[:, 0:1], None, ALU.add))
                chain.link(dve.tensor_tensor(cube[:, :], hid[:, :], hid[:, :], ALU.mult))
                chain.link(dve.tensor_scalar(cube[:, :], cube[:, :], GELU_A, 1.0, ALU.mult, ALU.add))
                chain.link(dve.tensor_tensor(cube[:, :], cube[:, :], hid[:, :], ALU.mult))
                dve.wait_ge(cmp_act, grp * C_ACT + 1)
                chain.link(dve.tensor_scalar_add(act_out[:, :], act_out[:, :], 1.0))
                chain.link(dve.reciprocal(act_out[:, :], act_out[:, :]))
                chain.link(dve.tensor_tensor(hidT[:, 0:N_CMP], hid[:, :], act_out[:, :], ALU.mult))
                dve.wait_ge(cmp_act, grp * C_ACT + 4)
                dve.tensor_tensor(kc_lo[LOW, :], a.O[1][LOW, 0:HD], kc_hi[LOW, :].bitcast(F32), ALU.subtract)
                chain.link(dve.tensor_tensor(kc_lo[HIGH, :], a.O[1][LOW, 0:HD], kc_hi[LOW, :].bitcast(F32), ALU.subtract))
                dve.tensor_tensor(vc[:, HD:P], a.O[1][LOW, HD:P], vc[:, 0:HD].bitcast(F32), ALU.subtract
                                  ).then_inc(cmp_dve, 1)
                with dve.Fori(0, PPG) as pr:
                    t = grp * PPG + pr
                    dve.wait_ge(a.proj_a, grp * G_TILES + pr + 4)
                    queries_dve(dve, a.S[1], q).then_inc(a.proj_d, 1)
                    dve.wait_ge(tables, t * 4 + 2)
                    attend_dve(dve, a, units, t, bias_of, True, yT)



def merge(nc, g, d, hT, yaT, ybT, mixT):
    NY = yaT.shape[1]
    with ExitStack() as ctx:
        sb, ps, sem = allocator(nc, ctx)
        w_gate = [[sb(f"w_mg{s}{m}", [P, ND, P]) for m in range(2)] for s in range(2)]
        w_o = [[sb(f"w_o{s}{m}", [P, NY, P]) for m in range(2)] for s in range(2)]
        e = [sb(f"mg_e{h}", [P, 2, 512]) for h in range(2)]
        prod = [sb(f"mg_p{h}", [P, 2, 512]) for h in range(2)]
        bank = [[ps(f"mg_ps{h}{m}", [P, 512]) for m in range(4)] for h in range(2)]
        loaded = [sem(f"mg_loaded{s}") for s in range(2)]
        multiplied, exped, plus1, step, used, mixed = (
            sem(n) for n in ("mg_multiplied", "mg_exped", "mg_plus1", "mg_step", "mg_used", "mg_mixed"))
        block = ctx.enter_context(nc.Block())
        halves = [slice(0, 512), slice(512, S)]

        @block.sync
        def _(sp):
            with sp.Fori(0, ND // 2) as r:
                for s in range(2):
                    c = r * 2 + s
                    sp.wait_ge(multiplied, c * 2 + 2)
                    for m in range(2):
                        sp.dma_start(w_gate[s][m][:, :, :], d["w_in"][0, :, bass.ds(c * P + (C_MG + m * D), P)]
                                     .rearrange("(k p) n -> p k n", p=P)).then_inc(loaded[s], 16)
                        w = (d["w_o_nsa"], d["w_o_fox"])[m]
                        sp.dma_start(w_o[s][m][:, :, :], w[0, :, bass.ds(c * P, P)]
                                     .rearrange("(k p) n -> p k n", p=P)).then_inc(loaded[s], 16)

        @block.tensor
        def _(pe):
            pe.sem_inc(multiplied, 4)
            with pe.Fori(0, ND // 2) as r:
                for s in range(2):
                    c = r * 2 + s
                    pe.wait_ge(loaded[s], r * 64 + 64)
                    for h in range(2):
                        pe.wait_ge(used, c * 2 + h + 1)
                        for m in range(2):
                            for k in range(ND):
                                pe.matmul(bank[h][m][:, :], w_gate[s][m][:, k, :], hT[:, k, halves[h]],
                                          start=(k == 0), stop=(k == ND - 1))
                        for m, y in enumerate((yaT, ybT)):
                            for k in range(NY):
                                last = pe.matmul(bank[h][2 + m][:, :], w_o[s][m][:, k, :], y[:, k, halves[h]],
                                                 start=(k == 0), stop=(k == NY - 1))
                        last.then_inc(multiplied, 1)

        @block.scalar
        def _(act):
            with act.Fori(0, ND) as c:
                for h in range(2):
                    n = c * 2 + h
                    act.wait_ge(multiplied, n + 5)
                    act.wait_ge(used, n + 1)
                    act.activation(e[h][:, 0, :], bank[h][0][:, :], ACT.Exp, scale=-1.0)
                    act.activation(e[h][:, 1, :], bank[h][1][:, :], ACT.Exp, scale=-1.0).then_inc(exped, 1)

        @block.vector
        def _(dve):
            dve.sem_inc(used, 2)
            with dve.Fori(0, ND) as c:
                for h in range(2):
                    n = c * 2 + h
                    dve.wait_ge(exped, n + 1)
                    dve.wait_ge(mixed, n + 1)
                    chain = Chain(dve, step, n * 2)
                    chain.link(dve.tensor_scalar_add(e[h][:, :, :], e[h][:, :, :], 1.0))
                    chain.link(dve.reciprocal(e[h][:, :, :], e[h][:, :, :]))
                    dve.tensor_tensor(prod[h][:, 0, :], e[h][:, 0, :], bank[h][2][:, :], ALU.mult)
                    dve.tensor_tensor(prod[h][:, 1, :], e[h][:, 1, :], bank[h][3][:, :], ALU.mult).then_inc(used, 1)

        @block.gpsimd
        def _(pool):
            pool.sem_inc(mixed, 2)
            with pool.Fori(0, ND) as c:
                for h in range(2):
                    pool.wait_ge(used, c * 2 + h + 3)
                    pool.tensor_tensor(mixT[:, bass.ds(c, 1), halves[h]], prod[h][:, 0, :].unsqueeze(1),
                                       prod[h][:, 1, :].unsqueeze(1), ALU.add).then_inc(mixed, 1)



def project_out(nc, g, d, mixT, mod, x1, logits, h2_dram):
    GT_M, SH_F, SC_F, GT_F = (slice(i * D, (i + 1) * D) for i in range(4))
    NL = N_GRP + N_EXP
    with ExitStack() as ctx:
        sb, ps, sem = allocator(nc, ctx)
        w = sb("w_out_sb", [P, ND, D])
        wr = sb("w_router", [P, ND, NL])
        br = sb("b_router", [P, NL])
        gain = sb("gains", [P, D])
        mt = [sb(f"mt{s}", [P, ND, P]) for s in range(2)]
        x = [sb(f"xo{s}", [P, D]) for s in range(2)]
        scaled = [sb(f"scaled{s}", [P, D]) for s in range(2)]
        h2 = [sb(f"h2{s}", [P, D]) for s in range(2)]
        h2T = sb("h2T", [P, ND, P])
        ms = [sb(f"oms{s}", [P, 2]) for s in range(2)]
        rstd = [sb(f"orstd{s}", [P, 2]) for s in range(2)]
        junk = sb("ojunk", [P, D])
        M = [ps(f"oM{s}", [P, D]) for s in range(2)]
        TP = ps("oT", [P, D])
        LG = ps("oL", [P, NL])
        x_loaded = [sem(f"o_x_loaded{s}") for s in range(2)]
        stored = [sem(f"o_stored{s}") for s in range(2)]
        w_loaded, gains, gain_used, staged, mixed, astep, dstep, shifted, turned, out_a, out_d, routed, logit = (
            sem(f"o_{n}") for n in ("w_loaded", "gains", "gain_used", "staged", "mixed", "astep", "dstep", "shifted",
                                    "turned", "out_a", "out_d", "routed", "logit"))
        A_STEPS, D_STEPS, CREDIT = 4, 5, 10
        block = ctx.enter_context(nc.Block())

        def over_tiles(eng, first, tile):
            first(0, 0)
            with eng.Fori(0, NT // 2 - 1) as r:
                for s in range(2):
                    first(r * 2 + s + 1, 1 - s)
                    tile(r * 2 + s, s)
            first(NT - 1, 1)
            tile(NT - 2, 0)
            tile(NT - 1, 1)

        @block.sync
        def _(sp):
            sp.dma_start(gain[:, :], d["g_post_mix"][0:1, :].to_broadcast([P, D])).then_inc(gains, 16)
            sp.dma_start(w[:, :, :], d["w_out"][0].rearrange("(k p) n -> p k n", p=P)).then_inc(w_loaded, 16)
            sp.dma_start(wr[:, :, 0:N_GRP], d["w_router_group"][0].rearrange("(k p) n -> p k n", p=P)).then_inc(w_loaded, 16)
            sp.dma_start(wr[:, :, N_GRP:], d["w_router_expert"][0].rearrange("(k p) n -> p k n", p=P)).then_inc(w_loaded, 16)
            sp.dma_start(br[:, 0:N_GRP], d["b_router_group"][0:1, :].to_broadcast([P, N_GRP])).then_inc(w_loaded, 16)
            sp.dma_start(br[:, N_GRP:], d["b_router_expert"][0:1, :].to_broadcast([P, N_EXP])).then_inc(w_loaded, 16)
            for n, gd in enumerate((d["g_pre_ffn"], d["g_post_ffn"])):
                sp.wait_ge(gain_used, n + 1)
                sp.dma_start(gain[:, :], gd[0:1, :].to_broadcast([P, D])).then_inc(gains, 16)

            def load(i, s):
                sp.wait_ge(dstep, i * D_STEPS + 3)
                sp.dma_start(x[s][:, :], d["x"][0, bass.ds(i * P, P), :]).then_inc(x_loaded[s], 16)

            def store(i, s):
                sp.wait_ge(shifted, i + 1)
                sp.dma_start(h2_dram[bass.ds(i * P, P), :], h2[s][:, :]).then_inc(stored[s], 16)

            for s in range(2):
                sp.sem_inc(stored[s], 16)
            over_tiles(sp, load, store)
            for s in range(2):
                sp.wait_ge(stored[s], (NT // 2 + 1) * 16)

        @block.tensor
        def _(pe):
            def project(i, s):
                pe.wait_ge(staged, i + 1)
                pe.wait_ge(dstep, i * D_STEPS + 2)
                for half in range(2):
                    cols = slice(half * 512, (half + 1) * 512)
                    for k in range(ND):
                        last = pe.matmul(M[s][:, cols], mt[s][:, k, :], w[:, k, cols], start=(k == 0), stop=(k == ND - 1))
                last.then_inc(mixed, 1)

            def route(i, s):
                pe.wait_ge(shifted, i + 1)
                pe.wait_ge(out_a, i + 1)
                pe.wait_ge(out_d, i + 1)
                for k in range(ND):
                    last = pe.transpose(TP[:, k * P:(k + 1) * P], h2[s][:, k * P:(k + 1) * P], g.ident[:, :])
                last.then_inc(turned, 1)
                pe.wait_ge(out_a, i + 2)
                pe.wait_ge(out_d, i + 2)
                pe.wait_ge(logit, i + 1)
                for k in range(ND):
                    last = pe.matmul(LG[:, :], h2T[:, k, :], wr[:, k, :], start=(k == 0), stop=(k == ND - 1))
                last.then_inc(routed, 1)

            pe.wait_ge(w_loaded, 80)
            over_tiles(pe, project, route)

        @block.scalar
        def _(act):
            def stage(i, s):
                act.wait_ge(mixed, i + 1)
                act.activation(mt[s][:, :, :], mixT[:, :, bass.ds(i * P, P)], ACT.Copy).then_inc(staged, 1)

            def norms(i, s):
                chain = Chain(act, astep, i * A_STEPS)
                act.wait_ge(mixed, i + 3)
                act.wait_ge(dstep, i * D_STEPS + 4)
                chain.link(act.activation(junk[:, :], M[s][:, :], ACT.Square, scale=D ** -0.5, accum_out=ms[s][:, 0:1]))
                chain.link(act.activation(ms[s][:, 0:1], ms[s][:, 0:1], ACT.Sqrt, bias=g.eps[:, :]))
                act.wait_ge(dstep, i * D_STEPS + (CREDIT + 3))
                chain.link(act.activation(junk[:, :], x1[:, bass.ds(i, 1), :].rearrange("p a n -> p (a n)"), ACT.Square,
                                          scale=D ** -0.5, accum_out=ms[s][:, 1:2]))
                chain.link(act.activation(ms[s][:, 1:2], ms[s][:, 1:2], ACT.Sqrt, bias=g.eps[:, :]))
                act.wait_ge(turned, i + 1)
                act.wait_ge(routed, i + 1)
                act.activation(h2T[:, 0:4, :], TP[:, 0:512].rearrange("p (k t) -> p k t", t=P), ACT.Copy).then_inc(out_a, 1)

            act.sem_inc(mixed, 2)
            over_tiles(act, stage, norms)

        @block.gpsimd
        def _(pool):
            with pool.Fori(0, NT // 2) as r:
                for s in range(2):
                    i = r * 2 + s
                    pool.wait_ge(dstep, i * D_STEPS + (CREDIT + 5))
                    pool.tensor_tensor(h2[s][:, :], h2[s][:, :], mod[:, SH_F], ALU.add).then_inc(shifted, 1)

        @block.vector
        def _(dve):
            dve.sem_inc(dstep, CREDIT)
            dve.sem_inc(out_d, 1)
            dve.sem_inc(out_a, 1)
            dve.sem_inc(logit, 1)
            dve.sem_inc(routed, 1)
            for n, (part, plus) in enumerate(((GT_M, 0.0), (SC_F, 1.0), (GT_F, 0.0))):
                dve.wait_ge(gains, n * 16 + 16)
                dve.scalar_tensor_tensor(out=mod[:, part], in0=mod[:, part], scalar=plus, in1=gain[:, :],
                                         op0=ALU.add, op1=ALU.mult).then_inc(gain_used, 1)
            dve.wait_ge(gain_used, 3)
            dve.wait_ge(w_loaded, 80)
            with dve.Fori(0, NT // 2) as r:
                for s in range(2):
                    i = r * 2 + s
                    x1_i = x1[:, bass.ds(i, 1), :].rearrange("p a n -> p (a n)")
                    chain = Chain(dve, dstep, i * D_STEPS + CREDIT)
                    dve.wait_ge(astep, i * A_STEPS + 2)
                    chain.link(dve.reciprocal(rstd[s][:, 0:1], ms[s][:, 0:1]))
                    chain.link(dve.scalar_tensor_tensor(out=scaled[s][:, :], in0=M[s][:, :], scalar=rstd[s][:, 0:1],
                                                        in1=mod[:, GT_M], op0=ALU.mult, op1=ALU.mult))
                    dve.wait_ge(x_loaded[s], r * 16 + 16)
                    chain.link(dve.tensor_tensor(x1_i, scaled[s][:, :], x[s][:, :], ALU.add))
                    dve.wait_ge(astep, i * A_STEPS + 4)
                    chain.link(dve.reciprocal(rstd[s][:, 1:2], ms[s][:, 1:2]))
                    dve.wait_ge(stored[s], r * 16 + 16)
                    chain.link(dve.scalar_tensor_tensor(out=h2[s][:, :], in0=x1_i, scalar=rstd[s][:, 1:2],
                                                        in1=mod[:, SC_F], op0=ALU.mult, op1=ALU.mult))
                    dve.wait_ge(turned, i + 1)
                    dve.wait_ge(routed, i + 1)
                    dve.tensor_copy(h2T[:, 4:8, :], TP[:, 512:D].rearrange("p (k t) -> p k t", t=P)).then_inc(out_d, 1)
                    dve.wait_ge(routed, i + 2)
                    dve.tensor_tensor(logits[:, bass.ds(i, 1), :], LG[:, :].unsqueeze(1), br[:, :].unsqueeze(1), ALU.add
                                      ).then_inc(logit, 1)



def route(nc, g, logits, slots, rows, weights, ids, ids_dram, overflow):
    with ExitStack() as ctx:
        sb, ps, sem = allocator(nc, ctx)
        E, T2 = N_EXP, 2 * NT
        gpad = sb("gpad", [P, NT, 8])
        gtop = sb("gtop", [P, NT, 8])
        gidx = sb("gidx", [P, NT, 8], U32)
        gsub = sb("gsub", [P, NT, N_GRP])
        gsum = sb("gsum", [P, NT])
        pg = sb("pg", [P, NT])
        gif = sb("gif", [P, NT])
        grp_of = sb("grp_of", [P, E])
        exp_no = sb("exp_no", [P, E])
        in_grp = sb("in_grp", [P, NT, E])
        outside = sb("outside", [P, NT, E])
        masked = sb("masked", [P, NT, E])
        etop = sb("etop", [P, NT, 8])
        eidx = sb("eidx", [P, NT, 8], U32)
        ef = sb("ef", [P, 2, NT])
        diff = sb("diff", [P, NT])
        den = sb("den", [P, NT])
        one_hot = sb("one_hot", [P, 2, NT, E])
        prefix = sb("prefix", [P, NT + 1, E])
        both = sb("both", [P, NT, E])
        before = sb("before_me", [P, P])
        rank_all = sb("rank_all", [P, NT, E])
        picked = sb("picked", [P, 2, NT, E])
        rank = sb("rank", [P, 2, NT])
        over = sb("over_no", [P, 2, NT])
        start = sb("over_start", [P, 2, NT])
        n_over = sb("n_over", [P, E])
        over_end = sb("over_end", [P, E])
        over_beg = sb("over_beg", [P, E])
        zero = sb("rzero", [P, E])
        place = sb("place", [P, 2, NT])
        col = sb("colno", [P, 2, NT])
        tmp = sb("rtmp", [P, 2, NT])
        block_no = sb("block_no", [P, N_OVF + 1])
        cmpb = sb("cmpb", [P, N_OVF + 1, E])
        bexp = sb("bexp", [P, N_OVF + 1])
        token = sb("token_no", [P, NT], I32)
        zeros_i = sb("zeros_i", [P, N_COL], I32)
        R = ps("rank_ps", [P, NT * E])
        C = ps("count_ps", [P, E])
        made, step, ranked, aexp, cleared, scattered, loaded = (
            sem(f"r_{n}") for n in ("made", "step", "ranked", "aexp", "cleared", "scattered", "loaded"))
        counted = {}
        block = ctx.enter_context(nc.Block())

        def per_token(ap):
            return ap.unsqueeze(2).to_broadcast([P, NT, E])

        def per_expert(ap):
            return ap.unsqueeze(1).to_broadcast([P, NT, E])

        @block.vector
        def _(dve):
            chain = Chain(dve, step)
            link = chain.link
            dve.wait_ge(made, 9)
            link(dve.tensor_copy(gpad[:, :, 0:N_GRP], logits[:, :, 0:N_GRP]))
            for i in range(NT):
                last = dve.max(gtop[:, i, :], gpad[:, i, :])
            link(last)
            for i in range(NT):
                last = dve.max_index(gidx[:, i, :], gtop[:, i, :], gpad[:, i, :])
            link(last)
            link(dve.tensor_tensor(gsub[:, :, :], logits[:, :, 0:N_GRP],
                                   gtop[:, :, 0:1].to_broadcast([P, NT, N_GRP]), ALU.subtract))
            counted["gsub"] = chain.n
            link(dve.tensor_copy(gif[:, :], gidx[:, :, 0]))
            link(dve.tensor_tensor(in_grp[:, :, :], per_expert(grp_of[:, :]), per_token(gif[:, :]), ALU.is_equal))
            link(dve.tensor_scalar(outside[:, :, :], in_grp[:, :, :], BIG, -BIG, ALU.mult, ALU.add))
            link(dve.tensor_tensor(masked[:, :, :], logits[:, :, N_GRP:], in_grp[:, :, :], ALU.mult))
            link(dve.tensor_tensor(masked[:, :, :], masked[:, :, :], outside[:, :, :], ALU.add))
            for i in range(NT):
                last = dve.max(etop[:, i, :], masked[:, i, :])
            link(last)
            for i in range(NT):
                last = dve.max_index(eidx[:, i, :], etop[:, i, :], masked[:, i, :])
            link(last)
            link(dve.tensor_tensor(diff[:, :], etop[:, :, 1], etop[:, :, 0], ALU.subtract))
            counted["diff"] = chain.n
            for k in range(2):
                last = dve.tensor_copy(ef[:, k, :], eidx[:, :, k])
            link(last)
            for k in range(2):
                last = dve.tensor_tensor(one_hot[:, k, :, :], per_expert(exp_no[:, :]), per_token(ef[:, k, :]), ALU.is_equal)
            link(last)
            link(dve.tensor_tensor(both[:, :, :], one_hot[:, 0, :, :], one_hot[:, 1, :, :], ALU.add))
            for i in range(NT):
                link(dve.tensor_tensor(prefix[:, i + 1, :], prefix[:, i, :], both[:, i, :], ALU.add))
            counted["prefix"] = chain.n
            dve.wait_ge(aexp, 2)
            link(dve.tensor_reduce(gsum[:, :], gsub[:, :, :], AX.X, ALU.add))
            link(dve.reciprocal(pg[:, :], gsum[:, :]))
            link(dve.tensor_scalar_add(den[:, :], diff[:, :], 1.0))
            link(dve.reciprocal(den[:, :], den[:, :]))
            link(dve.tensor_tensor(weights[:, 0, :], pg[:, :], den[:, :], ALU.mult))
            link(dve.tensor_tensor(weights[:, 1, :], weights[:, 0, :], diff[:, :], ALU.mult))
            dve.wait_ge(ranked, 1)
            link(dve.tensor_copy(rank_all[:, :, :], R[:, :].rearrange("p (t e) -> p t e", e=E)))
            for k in range(2):
                last = dve.tensor_tensor(picked[:, k, :, :], one_hot[:, k, :, :], rank_all[:, :, :], ALU.mult)
            link(last)
            link(dve.tensor_reduce(rank[:, :, :], picked[:, :, :, :], AX.X, ALU.add))
            link(dve.tensor_scalar(n_over[:, :], C[:, :], float(P), None, ALU.is_gt))
            for m in range(2, S // P):
                link(dve.scalar_tensor_tensor(out=n_over[:, :], in0=C[:, :], scalar=float(m * P), in1=n_over[:, :],
                                              op0=ALU.is_gt, op1=ALU.add))
            link(dve.tensor_tensor_scan(over_end[:, :], n_over[:, :], zero[:, :], 0.0, ALU.add, ALU.add))
            link(dve.tensor_tensor(over_beg[:, :], over_end[:, :], n_over[:, :], ALU.subtract))
            for k in range(2):
                last = dve.tensor_tensor(picked[:, k, :, :], one_hot[:, k, :, :], per_expert(over_beg[:, :]), ALU.mult)
            link(last)
            link(dve.tensor_reduce(start[:, :, :], picked[:, :, :, :], AX.X, ALU.add))
            link(dve.tensor_scalar(over[:, :, :], rank[:, :, :], float(P), None, ALU.is_ge))
            for m in range(2, S // P):
                link(dve.scalar_tensor_tensor(out=over[:, :, :], in0=rank[:, :, :], scalar=float(m * P),
                                              in1=over[:, :, :], op0=ALU.is_ge, op1=ALU.add))
            link(dve.scalar_tensor_tensor(out=place[:, :, :], in0=over[:, :, :], scalar=-float(P), in1=rank[:, :, :],
                                          op0=ALU.mult, op1=ALU.add))
            link(dve.scalar_tensor_tensor(out=tmp[:, :, :], in0=over[:, :, :], scalar=float(E - 1), in1=start[:, :, :],
                                          op0=ALU.add, op1=ALU.add))
            link(dve.tensor_tensor(tmp[:, :, :], tmp[:, :, :], ef[:, :, :], ALU.subtract))
            link(dve.scalar_tensor_tensor(out=tmp[:, :, :], in0=over[:, :, :], scalar=1.0, in1=tmp[:, :, :],
                                          op0=ALU.min, op1=ALU.mult))
            link(dve.tensor_tensor(col[:, :, :], tmp[:, :, :], ef[:, :, :], ALU.add))
            link(dve.scalar_tensor_tensor(out=slots[:, :, :], in0=place[:, :, :], scalar=float(N_COL), in1=col[:, :, :],
                                          op0=ALU.mult, op1=ALU.add))
            counted["slots"] = chain.n
            link(dve.scalar_tensor_tensor(out=rows[:, :, :], in0=col[:, :, :], scalar=float(P), in1=place[:, :, :],
                                          op0=ALU.mult, op1=ALU.add))
            link(dve.tensor_tensor(cmpb[:, :, :], over_end[:, :].unsqueeze(1).to_broadcast([P, N_OVF + 1, E]),
                                   block_no[:, :].unsqueeze(2).to_broadcast([P, N_OVF + 1, E]), ALU.is_le))
            link(dve.tensor_reduce(bexp[:, :], cmpb[:, :, :], AX.X, ALU.add))
            link(dve.tensor_scalar(overflow[:, 1:], bexp[:, :], float(E - 1), None, ALU.min))
            link(dve.tensor_copy(overflow[:, 0:1], over_end[:, E - 1:E]))

        @block.scalar
        def _(act):
            act.wait_ge(step, counted["gsub"])
            act.activation(gsub[:, :, :], gsub[:, :, :], ACT.Exp).then_inc(aexp, 1)
            act.wait_ge(step, counted["diff"])
            act.activation(diff[:, :], diff[:, :], ACT.Exp).then_inc(aexp, 1)

        @block.tensor
        def _(pe):
            pe.wait_ge(step, counted["prefix"])
            pe.wait_ge(made, 9)
            pe.matmul(R[:, :], before[:, :], both[:, :, :].rearrange("p t e -> p (t e)"), start=True, stop=False)
            pe.matmul(R[:, :], g.ones[:, :], prefix[:, 0:NT, :].rearrange("p t e -> p (t e)"), start=False, stop=True)
            pe.matmul(C[:, :], g.ones[:, :], prefix[:, NT, :], start=True, stop=True).then_inc(ranked, 1)

        @block.gpsimd
        def _(pool):
            flt = dict(allow_small_or_imprecise_dtypes=True)
            pool.memset(zeros_i[:, :], 0).then_inc(cleared, 1)
            pool.memset(gpad[:, :, :], -BIG).then_inc(made, 1)
            pool.memset(prefix[:, 0, :], 0.0).then_inc(made, 1)
            pool.memset(zero[:, :], 0.0).then_inc(made, 1)
            pool.memset(before[:, :], 1.0).then_inc(made, 1)
            pool.iota(grp_of[:, :], pattern=[[1, N_GRP], [0, PER_GRP]], base=0, channel_multiplier=0, **flt).then_inc(made, 1)
            pool.iota(exp_no[:, :], pattern=[[1, E]], base=0, channel_multiplier=0, **flt).then_inc(made, 1)
            pool.iota(block_no[:, :], pattern=[[1, N_OVF + 1]], base=0, channel_multiplier=0, **flt).then_inc(made, 1)
            pool.iota(token[:, :], pattern=[[P, NT]], base=0, channel_multiplier=1).then_inc(made, 1)
            pool.wait_ge(made, 8)
            pool.affine_select(out=before[:, :], in_=before[:, :], compare_op=ALU.is_gt, fill=0.0, base=0,
                               pattern=[[1, P]], channel_multiplier=-1).then_inc(made, 1)
            pool.wait_ge(made, 9)
            pool.wait_ge(cleared, 17)
            pool.wait_ge(step, counted["slots"])
            for k in range(2):
                for i in range(NT):
                    pool.indirect_dma_start(
                        out=ids_dram, out_offset=bass.IndirectOffsetOnAxis(ap=slots[:, k, i:i + 1], axis=0),
                        in_=token[:, i:i + 1], in_offset=None).then_inc(scattered, 16)
            pool.wait_ge(scattered, 16 * T2)

        @block.sync
        def _(sp):
            table = ids_dram.rearrange("(p c) a -> p (c a)", c=N_COL)
            sp.wait_ge(cleared, 1)
            sp.dma_start(table, zeros_i[:, :]).then_inc(cleared, 16)
            sp.wait_ge(scattered, 16 * T2)
            sp.dma_start(ids[:, :], table).then_inc(loaded, 16)
            sp.wait_ge(loaded, 16)



def experts(nc, g, d, ids, overflow, h2_dram, y_dram, room):
    KD = D_EXP // P
    with ExitStack() as ctx:
        sb, ps, sem = allocator(nc, ctx)
        wg, wu = ([sb(f"w{n}{s}", [P, ND, D_EXP]) for s in range(2)] for n in ("gate", "up"))
        wd = [room[:, s * KD * D:(s + 1) * KD * D].rearrange("p (k n) -> p k n", n=D) for s in range(2)]
        idx = [sb(f"idx{s}", [P, 1], I32) for s in range(2)]
        xb = [sb(f"xb{s}", [P, D]) for s in range(2)]
        xT = [sb(f"xT{s}", [P, ND, P]) for s in range(2)]
        sig = sb("sig", [P, D_EXP])
        prod = sb("gu", [P, D_EXP])
        aT = sb("aT", [P, KD, P])
        y = [sb(f"yb{s}", [P, D]) for s in range(2)]
        TX = ps("TX", [P, D])
        GP = ps("GP", [P, D_EXP])
        UP = ps("UP", [P, D_EXP])
        TA = ps("TA", [P, D_EXP])
        YP = ps("YP", [P, D])
        gu_loaded = [sem(f"e_gu_loaded{s}") for s in range(2)]
        d_loaded = [sem(f"e_d_loaded{s}") for s in range(2)]
        x_loaded = [sem(f"e_x_loaded{s}") for s in range(2)]
        y_stored = [sem(f"e_y_stored{s}") for s in range(2)]
        names = ("copied", "x_turned", "x_out_a", "x_out_d", "gu_done", "exped", "step", "a_turned", "a_out",
                 "down_done", "y_out")
        (copied, x_turned, x_out_a, x_out_d, gu_done, exped, step, a_turned, a_out, down_done, y_out) = (
            sem(f"e_{n}") for n in names)
        block = ctx.enter_context(nc.Block())
        LAST = N_EXP - 1

        def over_blocks(eng, body):
            with eng.Fori(0, N_EXP // 2 - 1) as r:
                body(r * 2, 0, r, False)
                body(r * 2 + 1, 1, r, False)
            body(N_EXP - 2, 0, N_EXP // 2 - 1, False)
            body(N_EXP - 1, 1, N_EXP // 2 - 1, True)

        def over_overflow(eng, body):
            used = eng.value_load(overflow[0:1, 0:1], min_val=0, max_val=N_OVF)
            with eng.Fori(0, N_OVF) as j:
                with eng.If(used > j):
                    body(j)

        @block.sync
        def _(sp):
            def load(e, b, s, r):
                sp.wait_ge(gu_done, b + 1)
                sp.dma_start(wg[s][:, :, :], d["w_exp_gate"][0, bass.ds(e, 1)].rearrange("a (k p) n -> p (a k) n", p=P)
                             ).then_inc(gu_loaded[s], 16)
                sp.dma_start(wu[s][:, :, :], d["w_exp_up"][0, bass.ds(e, 1)].rearrange("a (k p) n -> p (a k) n", p=P)
                             ).then_inc(gu_loaded[s], 16)
                sp.wait_ge(down_done, b + 1)
                sp.dma_start(wd[s][:, :, :], d["w_exp_down"][0, bass.ds(e, 1)].rearrange("a (k p) n -> p (a k) n", p=P)
                             ).then_inc(d_loaded[s], 16)

            over_blocks(sp, lambda b, s, r, last: load(b, b, s, r))

            def more(j):
                e = sp.value_load(overflow[0:1, bass.ds(j + 1, 1)], min_val=0, max_val=N_EXP - 1)
                sp.wait_ge(gu_done, j + (N_EXP + 2))
                sp.dma_start(wg[0][:, :, :], d["w_exp_gate"][0, bass.ds(e, 1)].rearrange("a (k p) n -> p (a k) n", p=P)
                             ).then_inc(gu_loaded[0], 16)
                sp.dma_start(wu[0][:, :, :], d["w_exp_up"][0, bass.ds(e, 1)].rearrange("a (k p) n -> p (a k) n", p=P)
                             ).then_inc(gu_loaded[0], 16)
                sp.wait_ge(down_done, j + (N_EXP + 2))
                sp.dma_start(wd[0][:, :, :], d["w_exp_down"][0, bass.ds(e, 1)].rearrange("a (k p) n -> p (a k) n", p=P)
                             ).then_inc(d_loaded[0], 16)

            over_overflow(sp, more)

        @block.gpsimd
        def _(pool):
            count = pool.alloc_register("e_count")

            def gather(b, s):
                pool.reg_mov(count, b + 1)
                pool.wait_ge(x_turned, count)
                pool.tensor_copy(idx[s][:, :], ids[:, bass.ds(b, 1)]).then_inc(copied, 1)
                pool.reg_mov(count, b + 1)
                pool.wait_ge(x_turned, 1)
                pool.wait_ge(copied, count)
                pool.indirect_dma_start(out=xb[s][:, :], out_offset=None, in_=h2_dram,
                                        in_offset=bass.IndirectOffsetOnAxis(ap=idx[s][:, :], axis=0)
                                        ).then_inc(x_loaded[s], 16)

            with pool.Fori(0, N_EXP // 2) as r:
                gather(r * 2, 0)
                gather(r * 2 + 1, 1)

            def more(j):
                gather_more(j)

            def gather_more(j):
                pool.reg_mov(count, j + (N_EXP + 2))
                pool.wait_ge(x_turned, count)
                pool.tensor_copy(idx[0][:, :], ids[:, bass.ds(j + N_EXP, 1)]).then_inc(copied, 1)
                pool.reg_mov(count, j + (N_EXP + 1))
                pool.wait_ge(x_turned, 1)
                pool.wait_ge(copied, count)
                pool.indirect_dma_start(out=xb[0][:, :], out_offset=None, in_=h2_dram,
                                        in_offset=bass.IndirectOffsetOnAxis(ap=idx[0][:, :], axis=0)
                                        ).then_inc(x_loaded[0], 16)

            over_overflow(pool, more)

        @block.tensor
        def _(pe):
            def turn_x(b, s, loads):
                pe.wait_ge(x_loaded[s], loads * 16)
                pe.wait_ge(x_out_a, b + 1)
                pe.wait_ge(x_out_d, b + 1)
                for k in range(ND):
                    last = pe.transpose(TX[:, k * P:(k + 1) * P], xb[s][:, k * P:(k + 1) * P], g.ident[:, :])
                last.then_inc(x_turned, 1)

            def gate_up(b, s, loads):
                pe.wait_ge(gu_loaded[s], loads * 32)
                pe.wait_ge(x_out_a, b + 2)
                pe.wait_ge(x_out_d, b + 2)
                pe.wait_ge(step, b * 4 + 4)
                for out, w in ((GP, wg[s]), (UP, wu[s])):
                    for k in range(ND):
                        last = pe.matmul(out[:, :], xT[s][:, k, :], w[:, k, :], start=(k == 0), stop=(k == ND - 1))
                last.then_inc(gu_done, 1)

            def down(b, s, loads):
                pe.wait_ge(step, b * 4 + 8)
                pe.wait_ge(a_out, b + 1)
                for k in range(KD):
                    last = pe.transpose(TA[:, k * P:(k + 1) * P], prod[:, k * P:(k + 1) * P], g.ident[:, :])
                last.then_inc(a_turned, 1)
                pe.wait_ge(a_out, b + 2)
                pe.wait_ge(d_loaded[s], loads * 16)
                pe.wait_ge(y_out, b + 1)
                for half in range(2):
                    cols = slice(half * 512, (half + 1) * 512)
                    for k in range(KD):
                        last = pe.matmul(YP[:, cols], aT[:, k, :], wd[s][:, k, cols], start=(k == 0), stop=(k == KD - 1))
                last.then_inc(down_done, 1)

            def body(b, s, r, last):
                gate_up(b, s, r + 1)
                if not last:
                    turn_x(b + 1, 1 - s, r + 1 + s)
                down(b, s, r + 1)

            pe.sem_inc(gu_done, 2)
            pe.sem_inc(down_done, 2)
            pe.sem_inc(x_turned, 2)
            turn_x(0, 0, 1)
            over_blocks(pe, body)

            def more(j):
                turn_x(j + N_EXP, 0, j + (N_EXP // 2 + 1))
                gate_up(j + N_EXP, 0, j + (N_EXP // 2 + 1))
                down(j + N_EXP, 0, j + (N_EXP // 2 + 1))

            over_overflow(pe, more)

        @block.scalar
        def _(act):
            def x_out(b, s):
                act.wait_ge(x_turned, b + 3)
                act.wait_ge(gu_done, b + 1)
                act.activation(xT[s][:, 0:4, :], TX[:, 0:512].rearrange("p (k t) -> p k t", t=P), ACT.Copy
                               ).then_inc(x_out_a, 1)

            def rest(b, s, stores):
                act.wait_ge(gu_done, b + 3)
                act.wait_ge(step, b * 4 + 4)
                act.activation(sig[:, :], GP[:, :], ACT.Exp, scale=-1.0).then_inc(exped, 1)
                act.wait_ge(down_done, b + 3)
                act.wait_ge(y_stored[s], stores * 16)
                act.activation(y[s][:, :], YP[:, :], ACT.Copy).then_inc(y_out, 1)
                act.wait_ge(y_out, b + 2)
                act.dma_start(y_dram[bass.ds(b * P, P), :], y[s][:, :]).then_inc(y_stored[s], 16)

            def body(b, s, r, last):
                act.wait_ge(gu_done, b + 3)
                act.wait_ge(step, b * 4 + 4)
                act.activation(sig[:, :], GP[:, :], ACT.Exp, scale=-1.0).then_inc(exped, 1)
                if not last:
                    x_out(b + 1, 1 - s)
                act.wait_ge(down_done, b + 3)
                act.wait_ge(y_stored[s], r * 16 + 16)
                act.activation(y[s][:, :], YP[:, :], ACT.Copy).then_inc(y_out, 1)
                act.wait_ge(y_out, b + 2)
                act.dma_start(y_dram[bass.ds(b * P, P), :], y[s][:, :]).then_inc(y_stored[s], 16)

            for s in range(2):
                act.sem_inc(y_stored[s], 16)
            act.sem_inc(x_out_a, 1)
            act.sem_inc(y_out, 1)
            x_out(0, 0)
            over_blocks(act, body)

            def more(j):
                x_out(j + N_EXP, 0)
                rest(j + N_EXP, 0, j + (N_EXP // 2 + 1))

            over_overflow(act, more)
            used = act.value_load(overflow[0:1, 0:1], min_val=0, max_val=N_OVF)
            act.wait_ge(y_stored[1], (N_EXP // 2 + 1) * 16)
            act.wait_ge(y_stored[0], used * 16 + (N_EXP // 2 + 1) * 16)
            act.activation(sig[:, 0:1], sig[:, 0:1], ACT.Copy).then_inc(exped, 1)

        @block.vector
        def _(dve):
            def x_out(b, s):
                dve.wait_ge(x_turned, b + 3)
                dve.wait_ge(gu_done, b + 1)
                dve.tensor_copy(xT[s][:, 4:8, :], TX[:, 512:D].rearrange("p (k t) -> p k t", t=P)).then_inc(x_out_d, 1)

            def activate(b):
                dve.wait_ge(exped, b + 1)
                dve.wait_ge(a_turned, b + 1)
                chain = Chain(dve, step, b * 4 + 4)
                chain.link(dve.tensor_scalar_add(sig[:, :], sig[:, :], 1.0))
                chain.link(dve.reciprocal(sig[:, :], sig[:, :]))
                chain.link(dve.tensor_tensor(prod[:, :], sig[:, :], GP[:, :], ALU.mult))
                chain.link(dve.tensor_tensor(prod[:, :], prod[:, :], UP[:, :], ALU.mult))

            def product_out(b):
                dve.wait_ge(a_turned, b + 2)
                dve.wait_ge(down_done, b + 2)
                dve.tensor_copy(aT[:, :, :], TA[:, :].rearrange("p (k t) -> p k t", t=P)).then_inc(a_out, 1)

            def body(b, s, r, last):
                activate(b)
                if not last:
                    x_out(b + 1, 1 - s)
                product_out(b)

            dve.sem_inc(x_out_d, 1)
            dve.sem_inc(step, 4)
            dve.sem_inc(a_out, 1)
            dve.sem_inc(a_turned, 1)
            x_out(0, 0)
            over_blocks(dve, body)

            def more(j):
                x_out(j + N_EXP, 0)
                activate(j + N_EXP)
                product_out(j + N_EXP)

            over_overflow(dve, more)


def combine(nc, g, d, rows, weights, x1, mod, y_dram, out):
    GT_F = slice(3 * D, 4 * D)
    with ExitStack() as ctx:
        sb, ps, sem = allocator(nc, ctx)
        idx = [[sb(f"c_idx{s}{k}", [P, 1], U32) for k in range(2)] for s in range(2)]
        yk = [[sb(f"c_y{s}{k}", [P, D]) for k in range(2)] for s in range(2)]
        wk = [sb(f"c_w{s}", [P, 2]) for s in range(2)]
        total = [sb(f"c_sum{s}", [P, D]) for s in range(2)]
        ms = [sb(f"c_ms{s}", [P, 1]) for s in range(2)]
        rstd = [sb(f"c_rstd{s}", [P, 1]) for s in range(2)]
        junk = sb("c_junk", [P, D])
        loaded = [sem(f"c_loaded{s}") for s in range(2)]
        stored = [sem(f"c_stored{s}") for s in range(2)]
        copied, step, astep, weighed = (sem(f"c_{n}") for n in ("copied", "step", "astep", "weighed"))
        D_STEPS, CREDIT = 5, 10
        block = ctx.enter_context(nc.Block())

        @block.gpsimd
        def _(pool):
            count = pool.alloc_register("c_count")
            with pool.Fori(0, NT // 2) as r:
                for s in range(2):
                    i = r * 2 + s
                    pool.reg_mov(count, i * D_STEPS + 2)
                    pool.wait_ge(step, count)
                    pool.tensor_copy(wk[s][:, :], weights[:, :, bass.ds(i, 1)].rearrange("p k a -> p (k a)")
                                     ).then_inc(weighed, 1)
                    for k in range(2):
                        pool.tensor_copy(idx[s][k][:, :], rows[:, k, bass.ds(i, 1)]).then_inc(copied, 1)
                    pool.reg_mov(count, i * 2 + 2)
                    for k in range(2):
                        pool.wait_ge(step, CREDIT)
                        pool.wait_ge(copied, count)
                        pool.indirect_dma_start(out=yk[s][k][:, :], out_offset=None, in_=y_dram,
                                                in_offset=bass.IndirectOffsetOnAxis(ap=idx[s][k][:, :], axis=0)
                                                ).then_inc(loaded[s], 16)

        @block.vector
        def _(dve):
            dve.sem_inc(step, CREDIT)
            with dve.Fori(0, NT // 2) as r:
                for s in range(2):
                    i = r * 2 + s
                    chain = Chain(dve, step, i * D_STEPS + CREDIT)
                    dve.wait_ge(loaded[s], r * 32 + 32)
                    dve.wait_ge(weighed, i + 1)
                    dve.wait_ge(stored[s], r * 16 + 16)
                    chain.link(dve.tensor_scalar(total[s][:, :], yk[s][0][:, :], wk[s][:, 0:1], None, ALU.mult))
                    chain.link(dve.scalar_tensor_tensor(out=total[s][:, :], in0=yk[s][1][:, :], scalar=wk[s][:, 1:2],
                                                        in1=total[s][:, :], op0=ALU.mult, op1=ALU.add))
                    dve.wait_ge(astep, i * 2 + 2)
                    chain.link(dve.reciprocal(rstd[s][:, :], ms[s][:, :]))
                    chain.link(dve.scalar_tensor_tensor(out=total[s][:, :], in0=total[s][:, :], scalar=rstd[s][:, :],
                                                        in1=mod[:, GT_F], op0=ALU.mult, op1=ALU.mult))
                    chain.link(dve.tensor_tensor(total[s][:, :], total[s][:, :],
                                                 x1[:, bass.ds(i, 1), :].rearrange("p a n -> p (a n)"), ALU.add))

        @block.scalar
        def _(act):
            with act.Fori(0, NT // 2) as r:
                for s in range(2):
                    i = r * 2 + s
                    chain = Chain(act, astep, i * 2)
                    act.wait_ge(step, i * D_STEPS + (CREDIT + 2))
                    chain.link(act.activation(junk[:, :], total[s][:, :], ACT.Square, scale=D ** -0.5, accum_out=ms[s][:, :]))
                    chain.link(act.activation(ms[s][:, :], ms[s][:, :], ACT.Sqrt, bias=g.eps[:, :]))

        @block.sync
        def _(sp):
            for s in range(2):
                sp.sem_inc(stored[s], 16)
            with sp.Fori(0, NT // 2) as r:
                for s in range(2):
                    i = r * 2 + s
                    sp.wait_ge(step, i * D_STEPS + (CREDIT + 5))
                    sp.dma_start(out[0, bass.ds(i * P, P), :], total[s][:, :]).then_inc(stored[s], 16)
            for s in range(2):
                sp.wait_ge(stored[s], (NT // 2 + 1) * 16)


def decoder_block(nc, d, out):
    fsum_dram = nc.dram_tensor("fsum", [FOX_HEADS, S], F32).ap()
    h2_dram = nc.dram_tensor("h2_rows", [S, D], F32).ap()
    ids_dram = nc.dram_tensor("token_ids", [P * N_COL, 1], I32).ap()
    y_dram = nc.dram_tensor("expert_rows", [(N_EXP + N_OVF) * P, D], F32).ap()
    with ExitStack() as ctx:
        sb, _, _ = allocator(nc, ctx)
        g = Constants(sb)
        room = sb("room", [P, ND * S])
        mixT = room[:, :].rearrange("p (k t) -> p k t", t=S)
        constants(nc, g, d)
        with ExitStack() as mixers:
            msb, _, _ = allocator(nc, mixers)
            hT = msb("hT", [P, ND, S])
            yaT, ybT = msb("yaT", [P, NSA_HEADS * HD // P, S]), msb("ybT", [P, FOX_HEADS * HD // P, S])
            gates = msb("gates", [P, NT, 3 * NSA_HEADS])
            with ExitStack() as first:
                mod = allocator(nc, first)[0]("mod_mix", [P, 2 * D])
                modulation(nc, g, d, 0, 4, mod)
                normalise_input(nc, g, d, mod, hT)
            gates_and_forget(nc, g, d, hT, gates, fsum_dram)
            fox(nc, g, d, hT, ybT, fsum_dram, y_dram)
            nsa(nc, g, d, hT, yaT, gates, room)
            merge(nc, g, d, hT, yaT, ybT, mixT)
        mod = sb("mod_ffn", [P, 4 * D])
        x1 = sb("x1", [P, NT, D])
        modulation(nc, g, d, 4, 8, mod)
        logits = sb("logits", [P, NT, N_GRP + N_EXP])
        rows, weights = sb("rows", [P, 2, NT], U32), sb("weights", [P, 2, NT])
        slots, ids = sb("slots", [P, 2, NT], U32), sb("ids", [P, N_COL], I32)
        overflow = sb("overflow", [P, 2 + N_OVF], I32)
        project_out(nc, g, d, mixT, mod, x1, logits, h2_dram)
        route(nc, g, logits, slots, rows, weights, ids, ids_dram, overflow)
        experts(nc, g, d, ids, overflow, h2_dram, y_dram, room)
        combine(nc, g, d, rows, weights, x1, mod, y_dram, out)


_INS = ['x', 'c', 'w_ada', 'b_ada', 'g_pre_mix', 'g_post_mix', 'g_pre_ffn', 'g_post_ffn', 'w_in', 'b_forget',
        'cmp_pe_k', 'cmp_w1_k', 'cmp_w2_k', 'cmp_pe_v', 'cmp_w1_v', 'cmp_w2_v', 'w_o_nsa', 'w_o_fox', 'w_out',
        'w_router_group', 'b_router_group', 'w_router_expert', 'b_router_expert',
        'w_exp_gate', 'w_exp_up', 'w_exp_down']


def kernel(**inputs):
    import numpy as _np
    import concourse.bacc as _bacc
    from concourse import mybir as _mybir
    from concourse.bass_utils import run_bass_kernel_spmd as _run

    nc = _bacc.Bacc("TRN2", target_bir_lowering=False, num_devices=1)
    arrays, d = {}, {}
    for name in _INS:
        a = _np.ascontiguousarray(inputs[name])
        arrays[f"in_{name}_dram"] = a
        d[name] = nc.dram_tensor(f"in_{name}_dram", a.shape, _mybir.dt.from_np(a.dtype),
                                          kind="ExternalInput").ap()
    out = nc.dram_tensor("out_0_dram", (1, S, D), F32, kind="ExternalOutput").ap()
    decoder_block(nc, d, out)
    r = _run(nc, [arrays], core_ids=[0])
    return r.results[0]["out_0_dram"]
```

```python
from contextlib import ExitStack

import concourse.bass as bass
from concourse import mybir

ALU = mybir.AluOpType
ACT = mybir.ActivationFunctionType
AX = mybir.AxisListType
F32 = mybir.dt.float32
F32R = mybir.dt.float32r
I32 = mybir.dt.int32
U32 = mybir.dt.uint32

P = 128
S = 1024
D = 1024
NT = S // P
ND = D // P
HD = 64
NSA_HEADS, NSA_GROUPS, FOX_HEADS = 8, 2, 8
CMP_LEN, CMP_STRIDE = 32, 16
N_CMP = (S - CMP_LEN) // CMP_STRIDE + 1
WINDOW = 512
EPS = 1e-6
BIG = 1e30
N_GRP, PER_GRP = 4, 8
N_EXP = N_GRP * PER_GRP
D_EXP = D // 2
NEG_SCALE = -(HD ** -0.5)

C_QA = 0
C_KCMP, C_VCMP, C_KSLC, C_VSLC, C_KWIN, C_VWIN = (512 + 128 * i for i in range(6))
C_GL = 1280
C_QB, C_KB, C_VB = 1304, 1816, 2328
C_F = 2840
C_MG = 2848

N_OVF = 2 * S // (P + 1)
N_COL = N_EXP + N_OVF + 1

Q_SLOTS = 2


class Chain:

    def __init__(self, eng, sem, base=0):
        self.eng, self.sem, self.base, self.n = eng, sem, base, 0

    def link(self, instruction):
        instruction.then_inc(self.sem, 1)
        self.n += 1
        self.eng.wait_ge(self.sem, self.base + self.n)


def allocator(nc, ctx):
    def sb(name, shape, dt=F32, side="left"):
        return ctx.enter_context(nc.sbuf_tensor(name, shape, dt, side=side))

    def ps(name, shape, dt=F32):
        return ctx.enter_context(nc.psum_tensor(name, shape, dt))

    def sem(name):
        return ctx.enter_context(nc.semaphore(name))

    return sb, ps, sem



class Constants:
    def __init__(self, sb):
        self.ident, self.ident_r = sb("ident", [P, P]), sb("ident_r", [P, P], F32R)
        self.ones, self.eps = sb("ones", [P, P]), sb("eps", [P, 1])
        self.csilu = sb("csilu", [P, ND])


def constants(nc, g, d):
    with ExitStack() as ctx:
        sb, ps, sem = allocator(nc, ctx)
        crow = sb("crow", [ND, P])
        ccol = sb("ccol", [P, ND])
        cexp = sb("cexp", [P, ND])
        cden = sb("cden", [P, ND])
        cps = ps("cps", [P, ND])
        loaded, made, turned, copied, exped, step = (
            sem(n) for n in ("c_loaded", "c_made", "c_turned", "c_copied", "c_exped", "c_step"))
        block = ctx.enter_context(nc.Block())

        @block.sync
        def _(sp):
            sp.dma_start(crow[:, :], d["c"].rearrange("a (k p) -> (a k) p", p=P)).then_inc(loaded, 16)

        @block.gpsimd
        def _(pool):
            pool.memset(g.ident[:, :], 0.0).then_inc(step, 1)
            pool.memset(g.ones[:, :], 1.0).then_inc(step, 1)
            pool.memset(g.eps[:, :], EPS).then_inc(step, 1)
            pool.wait_ge(step, 3)
            pool.affine_select(out=g.ident[:, :], in_=g.ident[:, :], compare_op=ALU.not_equal, fill=1.0,
                               base=0, pattern=[[-1, P]], channel_multiplier=1).then_inc(made, 1)

        @block.tensor
        def _(pe):
            pe.wait_ge(loaded, 16)
            pe.wait_ge(made, 1)
            pe.transpose(cps[:, :], crow[:, :], g.ident[0:ND, 0:ND]).then_inc(turned, 1)

        @block.scalar
        def _(act):
            act.wait_ge(turned, 1)
            act.activation(cexp[:, :], cps[:, :], ACT.Exp, scale=-1.0).then_inc(exped, 1)

        @block.vector
        def _(dve):
            dve.wait_ge(exped, 1)
            chain = Chain(dve, copied)
            chain.link(dve.tensor_copy(ccol[:, :], cps[:, :]))
            chain.link(dve.tensor_scalar_add(cden[:, :], cexp[:, :], 1.0))
            chain.link(dve.reciprocal(cexp[:, :], cden[:, :]))
            dve.tensor_tensor(g.csilu[:, :], ccol[:, :], cexp[:, :], ALU.mult).then_inc(copied, 1)


def modulation(nc, g, d, first, count, out):
    W = 512
    with ExitStack() as ctx:
        sb, ps, sem = allocator(nc, ctx)
        wada = [sb(f"wada{s}_{first}", [P, ND, W]) for s in range(2)]
        bias = [sb(f"bada{s}_{first}", [P, W]) for s in range(2)]
        part = [sb(f"mpart{s}_{first}", [P, W]) for s in range(2)]
        total = [ps(f"mtotal{s}_{first}", [P, W]) for s in range(2)]
        loaded = [sem(f"m_loaded{s}_{first}") for s in range(2)]
        step, summed, free = (sem(f"{n}_{first}") for n in ("m_step", "m_summed", "m_free"))
        STEPS = ND + 1
        block = ctx.enter_context(nc.Block())

        @block.sync
        def _(sp):
            with sp.Fori(0, count // 2) as r:
                for s in range(2):
                    n = r * 2 + s
                    sp.wait_ge(free, n + 1)
                    sp.dma_start(wada[s][:, :, :], d["w_ada"][0, :, bass.ds(n * W + first * W, W)]
                                 .rearrange("(k p) n -> p k n", p=P)).then_inc(loaded[s], 16)
                    sp.dma_start(bias[s][:, :], d["b_ada"][0:1, bass.ds(n * W + first * W, W)]
                                 .to_broadcast([P, W])).then_inc(loaded[s], 16)

        @block.tensor
        def _(pe):
            with pe.Fori(0, count // 2) as r:
                for s in range(2):
                    n = r * 2 + s
                    pe.wait_ge(step, n * STEPS + ND)
                    pe.matmul(total[s][:, :], g.ones[:, :], part[s][:, :], start=True, stop=True).then_inc(summed, 1)

        @block.vector
        def _(dve):
            dve.sem_inc(free, 2)
            with dve.Fori(0, count // 2) as r:
                for s in range(2):
                    n = r * 2 + s
                    dve.wait_ge(loaded[s], r * 32 + 32)
                    chain = Chain(dve, step, n * STEPS)
                    chain.link(dve.tensor_scalar(part[s][:, :], wada[s][:, 0, :], g.csilu[:, 0:1], None, ALU.mult))
                    for k in range(1, ND):
                        chain.link(dve.scalar_tensor_tensor(
                            out=part[s][:, :], in0=wada[s][:, k, :], scalar=g.csilu[:, k:k + 1],
                            in1=part[s][:, :], op0=ALU.mult, op1=ALU.add))
                    dve.wait_ge(summed, n + 1)
                    chain.link(dve.tensor_tensor(out[:, bass.ds(n * W, W)], total[s][:, :], bias[s][:, :], ALU.add))
                    dve.sem_inc(free, 1)



def normalise_input(nc, g, d, mod, hT):
    with ExitStack() as ctx:
        sb, ps, sem = allocator(nc, ctx)
        gain = sb("gain_pre", [P, D])
        scale = sb("scale_mix", [P, D])
        x = [sb(f"xt{s}", [P, D]) for s in range(2)]
        h = [sb(f"ht{s}", [P, D]) for s in range(2)]
        junk = sb("junk", [P, D])
        ms = [sb(f"ms{s}", [P, 1]) for s in range(2)]
        rstd = [sb(f"rstd{s}", [P, 1]) for s in range(2)]
        tps = [[ps(f"tps{s}{b}", [P, 512]) for b in range(2)] for s in range(2)]
        loaded = [sem(f"n_loaded{s}") for s in range(2)]
        gained, squared, pstep, scaled, shifted, turned, out_a, out_d = (
            sem(n) for n in ("n_gained", "n_squared", "n_pstep", "n_scaled", "n_shifted",
                             "n_turned", "n_out_a", "n_out_d"))
        block = ctx.enter_context(nc.Block())

        @block.sync
        def _(sp):
            sp.dma_start(gain[:, :], d["g_pre_mix"][0:1, :].to_broadcast([P, D])).then_inc(gained, 16)
            with sp.Fori(0, NT // 2) as r:
                for s in range(2):
                    i = r * 2 + s
                    sp.wait_ge(scaled, i + 1)
                    sp.dma_start(x[s][:, :], d["x"][0, bass.ds(i * P, P), :]).then_inc(loaded[s], 16)

        @block.scalar
        def _(act):
            with act.Fori(0, NT // 2) as r:
                for s in range(2):
                    i = r * 2 + s
                    act.wait_ge(loaded[s], r * 16 + 16)
                    act.wait_ge(scaled, i + 1)
                    act.activation(junk[:, :], x[s][:, :], ACT.Square, scale=D ** -0.5,
                                   accum_out=ms[s][:, :]).then_inc(squared, 1)
                    act.wait_ge(squared, i * 2 + 1)
                    act.activation(ms[s][:, :], ms[s][:, :], ACT.Sqrt, bias=g.eps[:, :]).then_inc(squared, 1)
                    act.wait_ge(turned, i + 1)
                    act.activation(hT[:, 0:4, bass.ds(i * P, P)],
                                   tps[s][0][:, :].rearrange("p (k t) -> p k t", t=P), ACT.Copy).then_inc(out_a, 1)

        @block.gpsimd
        def _(pool):
            with pool.Fori(0, NT // 2) as r:
                for s in range(2):
                    i = r * 2 + s
                    pool.wait_ge(scaled, i + 3)
                    pool.tensor_tensor(h[s][:, :], h[s][:, :], mod[:, 0:D], ALU.add).then_inc(shifted, 1)

        @block.vector
        def _(dve):
            dve.wait_ge(gained, 16)
            dve.scalar_tensor_tensor(out=scale[:, :], in0=mod[:, D:2 * D], scalar=1.0, in1=gain[:, :],
                                     op0=ALU.add, op1=ALU.mult).then_inc(scaled, 1)
            dve.wait_ge(scaled, 1)
            dve.sem_inc(scaled, 1)
            with dve.Fori(0, NT // 2) as r:
                for s in range(2):
                    i = r * 2 + s
                    dve.wait_ge(squared, i * 2 + 2)
                    dve.reciprocal(rstd[s][:, :], ms[s][:, :]).then_inc(pstep, 1)
                    dve.wait_ge(pstep, i + 1)
                    dve.wait_ge(out_d, i + 1)
                    dve.scalar_tensor_tensor(out=h[s][:, :], in0=x[s][:, :], scalar=rstd[s][:, :], in1=scale[:, :],
                                             op0=ALU.mult, op1=ALU.mult).then_inc(scaled, 1)
                    dve.wait_ge(turned, i + 1)
                    dve.tensor_copy(hT[:, 4:8, bass.ds(i * P, P)],
                                    tps[s][1][:, :].rearrange("p (k t) -> p k t", t=P)).then_inc(out_d, 1)

        @block.tensor
        def _(pe):
            pe.sem_inc(out_d, 2)
            pe.sem_inc(out_a, 2)
            with pe.Fori(0, NT // 2) as r:
                for s in range(2):
                    i = r * 2 + s
                    pe.wait_ge(shifted, i + 1)
                    pe.wait_ge(out_a, i + 1)
                    pe.wait_ge(out_d, i + 1)
                    for k in range(ND):
                        last = pe.transpose(tps[s][k // 4][:, (k % 4) * P:(k % 4 + 1) * P],
                                            h[s][:, k * P:(k + 1) * P], g.ident[:, :])
                    last.then_inc(turned, 1)



def gates_and_forget(nc, g, d, hT, gates, fsum_dram):
    NG = 3 * NSA_HEADS
    with ExitStack() as ctx:
        sb, ps, sem = allocator(nc, ctx)
        w = sb("w_small", [P, ND, NG + FOX_HEADS])
        bf = sb("b_forget_all", [P, FOX_HEADS])
        zero = sb("zero_f", [FOX_HEADS, S])
        f = sb("f_logit", [P, NT, FOX_HEADS])
        fneg = sb("f_neg", [P, NT, FOX_HEADS])
        fln = sb("f_ln", [P, NT, FOX_HEADS])
        gexp = sb("gate_exp", [P, NT, NG])
        fT = sb("f_turned", [FOX_HEADS, S])
        valid = sb("cmp_valid", [P, 1])
        logits = ps("small_logits", [P, NT, NG + FOX_HEADS])
        fps = [ps(f"fps{b}", [FOX_HEADS, 512]) for b in range(2)]
        loaded, made, multiplied, aexp, step, turned, stored = (
            sem(n) for n in ("g_loaded", "g_made", "g_multiplied", "g_exp", "g_step", "g_turned", "g_stored"))
        block = ctx.enter_context(nc.Block())

        @block.sync
        def _(sp):
            sp.dma_start(w[:, :, 0:NG], d["w_in"][0, :, C_GL:C_GL + NG].rearrange("(k p) n -> p k n", p=P)
                         ).then_inc(loaded, 16)
            sp.dma_start(w[:, :, NG:], d["w_in"][0, :, C_F:C_F + FOX_HEADS].rearrange("(k p) n -> p k n", p=P)
                         ).then_inc(loaded, 16)
            sp.dma_start(bf[:, :], d["b_forget"][0:1, :].to_broadcast([P, FOX_HEADS])).then_inc(loaded, 16)
            sp.wait_ge(step, 9)
            sp.dma_start(fsum_dram, fT[:, :]).then_inc(stored, 16)
            sp.wait_ge(stored, 16)

        @block.gpsimd
        def _(pool):
            pool.memset(valid[:, :], 1.0).then_inc(made, 1)
            pool.memset(zero[:, :], 0.0).then_inc(made, 1)
            pool.wait_ge(made, 2)
            pool.affine_select(out=valid[:, :], in_=valid[:, :], compare_op=ALU.is_ge, fill=0.0,
                               base=-(CMP_LEN - 1), pattern=[[0, 1]], channel_multiplier=1).then_inc(made, 1)

        @block.tensor
        def _(pe):
            pe.wait_ge(loaded, 48)
            for i in range(NT):
                for k in range(ND):
                    last = pe.matmul(logits[:, i, :], hT[:, k, i * P:(i + 1) * P], w[:, k, :],
                                     start=(k == 0), stop=(k == ND - 1))
            last.then_inc(multiplied, 1)
            pe.wait_ge(step, 7)
            for i in range(NT):
                last = pe.transpose(fps[i // 4][:, (i % 4) * P:(i % 4 + 1) * P], fln[:, i, :], g.ident[:, :])
            last.then_inc(turned, 1)

        @block.scalar
        def _(act):
            act.wait_ge(multiplied, 1)
            act.activation(gexp[:, :, :], logits[:, :, 0:NG], ACT.Exp, scale=-1.0).then_inc(aexp, 1)
            act.wait_ge(step, 3)
            act.activation(fln[:, :, :], fneg[:, :, :], ACT.Exp).then_inc(aexp, 1)
            act.wait_ge(aexp, 2)
            act.activation(fln[:, :, :], fln[:, :, :], ACT.Ln, bias=1.0).then_inc(aexp, 1)

        @block.vector
        def _(dve):
            dve.wait_ge(loaded, 48)
            dve.wait_ge(aexp, 1)
            chain = Chain(dve, step)
            chain.link(dve.tensor_tensor(f[:, :, :], logits[:, :, NG:],
                                         bf[:, :].unsqueeze(1).to_broadcast([P, NT, FOX_HEADS]), ALU.add))
            chain.link(dve.tensor_scalar(fneg[:, :, :], f[:, :, :], -1.0, None, ALU.mult))
            chain.link(dve.tensor_tensor(fneg[:, :, :], f[:, :, :], fneg[:, :, :], ALU.min))
            chain.link(dve.tensor_scalar_add(gexp[:, :, :], gexp[:, :, :], 1.0))
            chain.link(dve.reciprocal(gates[:, :, :], gexp[:, :, :]))
            dve.wait_ge(aexp, 3)
            chain.link(dve.tensor_scalar(f[:, :, :], f[:, :, :], 0.0, None, ALU.min))
            chain.link(dve.tensor_tensor(fln[:, :, :], f[:, :, :], fln[:, :, :], ALU.subtract))
            dve.wait_ge(made, 3)
            cmp_gates = gates[:, 0, :].rearrange("p (h b) -> p h b", b=3)[:, :, 0]
            chain.link(dve.tensor_scalar(cmp_gates, cmp_gates, valid[:, 0:1], None, ALU.mult))
            dve.wait_ge(turned, 1)
            dve.tensor_tensor_scan(fT[:, 0:512], fps[0][:, :], zero[:, 0:512], 0.0, ALU.add, ALU.add
                                   ).then_inc(turned, 1)
            dve.wait_ge(turned, 2)
            dve.tensor_tensor_scan(fT[:, 512:S], fps[1][:, :], zero[:, 512:S], fT[:, 511:512], ALU.add, ALU.add
                                   ).then_inc(step, 1)



CR_SCORE = 2
CR_TURN = 6
CR_LO = 2
CR_PV = 2
CR_COMB = 4
CR_FAC = 4
Y_CHUNKS = 2


class Unit:

    def __init__(self, h, i, k0, nk, br, first):
        self.h, self.i, self.k0, self.nk, self.br, self.first = h, i, k0, nk, br, first

    @property
    def chunks(self):
        return [(a, min(a + 512, self.nk)) for a in range(0, self.nk, 512)]


def n_chunks(units):
    return sum(len(u.chunks) for u in units)


class AttentionBuffers:

    def __init__(self, nc, ctx, tag):
        sb, ps, sem = allocator(nc, ctx)
        self.tag, self.counts = tag, {}
        self.S = [ps(f"{tag}_S{s}", [P, S]) for s in range(2)]
        self.T = [ps(f"{tag}_T{s}", [P, 512]) for s in range(2)]
        self.O = [ps(f"{tag}_O{s}", [P, 512]) for s in range(2)]
        self.X = [sb(f"{tag}_X{s}", [P, S]) for s in range(2)]
        self.PTh = [sb(f"{tag}_PTh{s}", [P, S], F32R) for s in range(2)]
        self.PTl = [sb(f"{tag}_PTl{s}", [P, S], F32R) for s in range(2)]
        self.low = sb(f"{tag}_low", [P, 4])
        self.rsum = sb(f"{tag}_rsum", [P, 4])
        self.rmax = sb(f"{tag}_rmax", [P, 4])
        self.inv = sb(f"{tag}_inv", [P, 4])
        self.fac = sb(f"{tag}_fac", [P, 4])
        self.y = sb(f"{tag}_y", [P, NT, P])
        self.scored, self.score_read = sem(f"{tag}_scored"), sem(f"{tag}_score_read")
        self.probs, self.turned = sem(f"{tag}_probs"), sem(f"{tag}_turned")
        self.hi_done, self.lo_done = sem(f"{tag}_hi_done"), sem(f"{tag}_lo_done")
        self.pv_done, self.sum_used = sem(f"{tag}_pv_done"), sem(f"{tag}_sum_used")
        self.inv_done, self.fac_ready = sem(f"{tag}_inv_done"), sem(f"{tag}_fac_ready")
        self.comb_step, self.combined = sem(f"{tag}_comb_step"), sem(f"{tag}_combined")
        self.proj_done, self.proj_a, self.proj_d = (sem(f"{tag}_proj_{n}") for n in ("done", "a", "d"))
        self.w_loaded, self.cleared = sem(f"{tag}_w_loaded"), sem(f"{tag}_cleared")


def in_register(eng, a, value):
    if eng.engine not in a.counts:
        a.counts[eng.engine] = eng.alloc_register(f"{a.tag}_count")
    eng.reg_mov(a.counts[eng.engine], value)
    return a.counts[eng.engine]


def attend_pe(pe, g, a, units, t, operands):
    N, C = len(units), n_chunks(units)
    before = [n_chunks(units[:n]) for n in range(N + 1)]
    u0, c0 = t * N, t * (C + Y_CHUNKS)

    def scores(n):
        u = units[n]
        q, ks, _, mask = operands(u)
        pe.wait_ge(a.score_read, u0 + n + 1)
        for lo, hi in u.chunks:
            out = a.S[n % 2][:, lo:hi]
            pe.matmul(out, q, ks[0][:, u.k0 + lo:u.k0 + hi], start=True, stop=False)
            if mask is not None and hi == u.nk:
                pe.matmul(a.S[n % 2][:, hi - P:hi], g.ident_r[:, :], mask, start=False, stop=False)
            last = pe.matmul(out, q, ks[1][:, u.k0 + lo:u.k0 + hi], start=False, stop=True)
        last.then_inc(a.scored, 1)

    def turn(n):
        u = units[n]
        pe.wait_ge(a.probs, u0 + n + 1)
        for j, (lo, hi) in enumerate(u.chunks):
            c = before[n] + j
            pe.wait_ge(a.lo_done, c0 + c + 1)
            for b in range(lo, hi, P):
                last = pe.transpose(a.T[c % 2][:, b - lo:b - lo + P], a.X[n % 2][:, b:b + P], g.ident[:, :])
            last.then_inc(a.turned, 1)

    def weigh(n):
        u = units[n]
        v = operands(u)[2]
        pe.wait_ge(a.lo_done, c0 + before[n + 1] + CR_LO)
        pe.wait_ge(a.combined, u0 + n + CR_COMB - 1)
        out = a.O[n % 2][:, 0:P]
        for b in range(0, u.nk, P):
            w = min(P, u.nk - b)
            pe.matmul(out, a.PTh[n % 2][0:w, b:b + P], v(b // P), start=(b == 0), stop=False)
            last = pe.matmul(out, a.PTl[n % 2][0:w, b:b + P], v(b // P), start=False, stop=(b + P >= u.nk))
        last.then_inc(a.pv_done, 1)

    scores(0)
    scores(1)
    for n in range(N):
        turn(n)
        if n + 2 < N:
            scores(n + 2)
        if n >= 1:
            weigh(n - 1)
    weigh(N - 1)
    pe.wait_ge(a.combined, u0 + N + CR_COMB)
    for half in range(2):
        pe.wait_ge(a.lo_done, c0 + C + half + 1)
        for i in range(4):
            last = pe.transpose(a.T[half][:, i * P:(i + 1) * P], a.y[:, 4 * half + i, :], g.ident[:, :])
        last.then_inc(a.turned, 1)


def attend_act(act, a, units, t):
    N, C = len(units), n_chunks(units)
    before = [n_chunks(units[:n]) for n in range(N + 1)]
    u0, c0, h0 = t * N, t * (C + Y_CHUNKS), t * C

    def exps(n):
        u = units[n]
        act.wait_ge(a.score_read, u0 + n + 1 + CR_SCORE)
        act.wait_ge(a.sum_used, u0 + n + 1)
        x = a.X[n % 2][:, 0:u.nk]
        act.activation(x, x, ACT.Exp, bias=a.low[:, n % 4:n % 4 + 1], scale=-1.0,
                       accum_out=a.rsum[:, n % 4:n % 4 + 1]).then_inc(a.probs, 1)

    def hi(n):
        u = units[n]
        act.wait_ge(a.pv_done, u0 + n + 1)
        for j, (lo, end) in enumerate(u.chunks):
            c = before[n] + j
            w = min(P, u.nk)
            cols = max(P, end - lo)
            act.wait_ge(a.turned, c0 + c + 1 + CR_TURN)
            act.activation(a.PTh[n % 2][0:w, lo:lo + cols], a.T[c % 2][0:w, 0:cols], ACT.Copy).then_inc(a.hi_done, 1)

    exps(0)
    for n in range(N):
        hi(n)
        if n + 1 < N:
            exps(n + 1)


def attend_dve(dve, a, units, t, bias_of, gated, yT):
    N, C = len(units), n_chunks(units)
    before = [n_chunks(units[:n]) for n in range(N + 1)]
    u0, c0, h0 = t * N, t * (C + Y_CHUNKS), t * C

    def add_bias(n):
        u = units[n]
        dve.wait_ge(a.scored, u0 + n + 1)
        chunks = before[n - 1] if n >= 2 else before[N - 1 + n] - C - Y_CHUNKS
        count = in_register(dve, a, c0 + (chunks + CR_TURN))
        dve.wait_ge(a.score_read, CR_SCORE)
        dve.wait_ge(a.turned, count)
        dve.tensor_tensor_reduce(out=a.X[n % 2][:, 0:u.nk], in0=a.S[n % 2][:, 0:u.nk], in1=bias_of(u),
                                 scale=1.0, scalar=3e38, op0=ALU.add, op1=ALU.min,
                                 accum_out=a.low[:, n % 4:n % 4 + 1]).then_inc(a.score_read, 1)

    def lo(n):
        u = units[n]
        for j, (start, end) in enumerate(u.chunks):
            c = before[n] + j
            w = min(P, u.nk)
            cols = max(P, end - start)
            dve.wait_ge(a.hi_done, h0 + c + 1)
            dve.tensor_tensor(a.PTl[n % 2][0:w, start:start + cols], a.T[c % 2][0:w, 0:cols],
                              a.PTh[n % 2][0:w, start:start + cols].bitcast(F32), ALU.subtract
                              ).then_inc(a.lo_done, 1)

    def invert(n):
        c = slice(n % 4, n % 4 + 1)
        dve.wait_ge(a.sum_used, u0 + n + 1 + CR_FAC)
        dve.wait_ge(a.combined, u0 + n + 1)
        if gated:
            dve.reciprocal(a.inv[:, c], a.rmax[:, c]).then_inc(a.inv_done, 1)
        else:
            dve.reciprocal(a.fac[:, c], a.rmax[:, c]).then_inc(a.inv_done, 1)

    def combine(n):
        u = units[n]
        y = a.y[:, u.i, u.h * HD:(u.h + 1) * HD]
        f = a.fac[:, n % 4:n % 4 + 1]
        dve.wait_ge(a.pv_done, u0 + n + 1 + CR_PV)
        if gated:
            dve.wait_ge(a.fac_ready, u0 + n + 1)
        else:
            dve.wait_ge(a.inv_done, u0 + n + 1 + CR_FAC)
        dve.wait_ge(a.combined, u0 + n + CR_COMB)
        if u.first:
            dve.tensor_scalar(y, a.O[n % 2][:, 0:HD], f, None, ALU.mult).then_inc(a.comb_step, 1)
        else:
            dve.scalar_tensor_tensor(out=y, in0=a.O[n % 2][:, 0:HD], scalar=f, in1=y,
                                     op0=ALU.mult, op1=ALU.add).then_inc(a.comb_step, 1)
        dve.wait_ge(a.comb_step, u0 + n + 1)
        dve.scalar_tensor_tensor(out=y, in0=a.O[n % 2][:, HD:P], scalar=f, in1=y,
                                 op0=ALU.mult, op1=ALU.add).then_inc(a.combined, 1)

    add_bias(0)
    add_bias(1)
    for n in range(N):
        lo(n)
        if n + 2 < N:
            add_bias(n + 2)
        invert(n)
        if n >= 1:
            combine(n - 1)
    combine(N - 1)
    for half in range(2):
        dve.wait_ge(a.turned, c0 + C + half + 1 + CR_TURN)
        dve.tensor_copy(yT[:, bass.ds(t, 1), half * 512:(half + 1) * 512], a.T[half][:, :].unsqueeze(1)
                        ).then_inc(a.lo_done, 1)


def attend_pool(pool, a, units, t, gate_of):
    N = len(units)
    u0 = t * N

    def guard(n):
        c = slice(n % 4, n % 4 + 1)
        count = in_register(pool, a, u0 + n + 1)
        pool.wait_ge(a.sum_used, CR_FAC)
        pool.wait_ge(a.probs, count)
        pool.wait_ge(a.inv_done, count)
        pool.tensor_scalar(a.rmax[:, c], a.rsum[:, c], 1e-30, None, ALU.max).then_inc(a.sum_used, 1)

    def gate(n):
        c = slice(n % 4, n % 4 + 1)
        pool.wait_ge(a.inv_done, u0 + n + 1 + CR_FAC)
        pool.wait_ge(a.combined, u0 + n + 1)
        pool.tensor_tensor(a.fac[:, c], a.inv[:, c], gate_of(units[n]), ALU.mult).then_inc(a.fac_ready, 1)

    for n in range(N):
        guard(n)
        if gate_of is not None:
            gate(n)


def project_columns(pe, a, slot, w, hT):
    for half in range(2):
        for k in range(ND):
            last = pe.matmul(a.S[slot][:, half * 512:(half + 1) * 512], w[:, k, :],
                             hT[:, k, half * 512:(half + 1) * 512], start=(k == 0), stop=(k == ND - 1))
    last.then_inc(a.proj_done, 1)


def project_rows(pe, a, slot, w, hT):
    for i in range(NT):
        for k in range(ND):
            last = pe.matmul(a.S[slot][:, i * P:(i + 1) * P], hT[:, k, i * P:(i + 1) * P], w[:, k, :],
                             start=(k == 0), stop=(k == ND - 1))
    last.then_inc(a.proj_done, 1)


LOW, HIGH = slice(0, HD), slice(HD, P)


def queries_act(act, ps, q):
    act.activation(q[0][LOW, :], ps[LOW, :], ACT.Copy, scale=NEG_SCALE)
    return act.activation(q[1][LOW, :], ps[HIGH, :], ACT.Copy, scale=NEG_SCALE)


def queries_dve(dve, ps, q):
    for h, part in enumerate((LOW, HIGH)):
        last = dve.scalar_tensor_tensor(out=q[h][HIGH, :], in0=ps[part, :], scalar=NEG_SCALE,
                                        in1=q[h][LOW, :].bitcast(F32), op0=ALU.mult, op1=ALU.subtract)
    return last


def keys_act(act, ps, k_hi):
    for h, part in enumerate((LOW, HIGH)):
        act.activation(k_hi[h][LOW, :], ps[part, :], ACT.Copy)
        last = act.activation(k_hi[h][HIGH, :], ps[part, :], ACT.Copy)
    return last


def keys_dve(dve, ps, k_hi, k_lo):
    for h, part in enumerate((LOW, HIGH)):
        dve.tensor_tensor(k_lo[h][LOW, :], ps[part, :], k_hi[h][LOW, :].bitcast(F32), ALU.subtract)
        last = dve.tensor_tensor(k_lo[h][HIGH, :], ps[part, :], k_hi[h][LOW, :].bitcast(F32), ALU.subtract)
    return last


def values_act(act, ps, v):
    return act.activation(v[:, :, 0:HD], ps[:, :].rearrange("p (n e) -> p n e", e=HD), ACT.Copy)


def values_dve(dve, ps, v):
    return dve.tensor_tensor(v[:, :, HD:P], ps[:, :].rearrange("p (n e) -> p n e", e=HD),
                             v[:, :, 0:HD].bitcast(F32), ALU.subtract)


def fox(nc, g, d, hT, yT, fsum_dram, y_dram):
    units = [Unit(h=h, i=i, k0=0, nk=(i + 1) * P, br=0, first=True) for h in range(2) for i in range(NT)]
    N = len(units)
    PAIRS = FOX_HEADS // 2
    with ExitStack() as ctx:
        sb, ps, sem = allocator(nc, ctx)
        a = AttentionBuffers(nc, ctx, "fox")
        wq, wk, wv = (sb(f"fox_w{n}", [P, ND, P]) for n in "qkv")
        q = [sb(f"fox_q{h}", [P, S], F32R) for h in range(2)]
        k_hi = [sb(f"fox_kh{h}", [P, S], F32R) for h in range(2)]
        k_lo = [sb(f"fox_kl{h}", [P, S], F32R) for h in range(2)]
        v = sb("fox_v", [P, NT * 2, P], F32R)
        decay = sb("fox_decay", [P, 2, S])
        mask_f = sb("fox_mask_f", [P, P])
        mask = sb("fox_mask", [P, P], F32R)
        zero = sb("fox_zero", [P, D])
        masked, decayed, blank, blanked = (sem(f"fox_{n}") for n in ("masked", "decayed", "blank", "blanked"))
        block = ctx.enter_context(nc.Block())

        @block.sync
        def _(sp):
            with sp.Fori(0, PAIRS) as t:
                sp.wait_ge(a.proj_d, t * 3 + 1)
                for w, c in ((wq, C_QB), (wk, C_KB), (wv, C_VB)):
                    sp.dma_start(w[:, :, :], d["w_in"][0, :, bass.ds(t * P + c, P)].rearrange("(k p) n -> p k n", p=P)
                                 ).then_inc(a.w_loaded, 16)
                sp.wait_ge(a.score_read, t * N + CR_SCORE)
                for h in range(2):
                    sp.dma_start(decay[:, h, :], fsum_dram[bass.ds(t * 2 + h, 1), :].to_broadcast([P, S])
                                 ).then_inc(decayed, 16)
            sp.wait_ge(blank, 1)
            for j in range(N_COL - N_EXP):
                sp.dma_start(y_dram[(N_EXP + j) * P:(N_EXP + j + 1) * P, :], zero[:, :]).then_inc(blanked, 16)
            sp.wait_ge(blanked, (N_COL - N_EXP) * 16)

        def operands(u):
            return (q[u.h][:, u.i * P:(u.i + 1) * P], (k_hi[u.h], k_lo[u.h]),
                    lambda b: v[:, 2 * b + u.h, :], mask[:, :])

        @block.tensor
        def _(pe):
            pe.wait_ge(masked, 4)
            with pe.Fori(0, PAIRS) as t:
                pe.wait_ge(a.score_read, t * N + CR_SCORE)
                pe.wait_ge(a.w_loaded, t * 48 + 48)
                project_columns(pe, a, 0, wq, hT)
                project_columns(pe, a, 1, wk, hT)
                pe.wait_ge(a.proj_d, t * 3 + 2)
                project_rows(pe, a, 0, wv, hT)
                pe.wait_ge(a.proj_d, t * 3 + 4)
                attend_pe(pe, g, a, units, t, operands)

        @block.scalar
        def _(act):
            with act.Fori(0, PAIRS) as t:
                act.wait_ge(a.proj_done, t * 3 + 1)
                queries_act(act, a.S[0], q).then_inc(a.proj_a, 1)
                act.wait_ge(a.proj_done, t * 3 + 2)
                keys_act(act, a.S[1], k_hi).then_inc(a.proj_a, 1)
                act.wait_ge(a.proj_done, t * 3 + 3)
                values_act(act, a.S[0], v).then_inc(a.proj_a, 1)
                attend_act(act, a, units, t)

        @block.gpsimd
        def _(pool):
            pool.sem_inc(a.sum_used, CR_FAC)
            pool.memset(mask_f[:, :], 0.0).then_inc(masked, 1)
            pool.memset(zero[:, :], 0.0).then_inc(blank, 1)
            pool.wait_ge(masked, 1)
            pool.affine_select(out=mask_f[:, :], in_=mask_f[:, :], compare_op=ALU.is_ge, fill=2.0 ** 99, base=0,
                               pattern=[[-1, P]], channel_multiplier=1).then_inc(masked, 1)
            with pool.Fori(0, PAIRS) as t:
                attend_pool(pool, a, units, t, None)

        @block.vector
        def _(dve):
            dve.sem_inc(a.score_read, CR_SCORE)
            dve.sem_inc(a.lo_done, CR_LO)
            dve.sem_inc(a.combined, CR_COMB)
            dve.sem_inc(a.pv_done, CR_PV)
            dve.sem_inc(a.turned, CR_TURN)
            dve.sem_inc(a.proj_d, 1)
            dve.sem_inc(a.inv_done, CR_FAC)
            dve.wait_ge(masked, 2)
            dve.tensor_copy(mask[:, :], mask_f[:, :]).then_inc(masked, 1)
            dve.tensor_copy(g.ident_r[:, :], g.ident[:, :]).then_inc(masked, 1)
            with dve.Fori(0, PAIRS) as t:
                dve.wait_ge(a.proj_a, t * 3 + 1)
                queries_dve(dve, a.S[0], q).then_inc(a.proj_d, 1)
                dve.wait_ge(a.proj_a, t * 3 + 2)
                keys_dve(dve, a.S[1], k_hi, k_lo).then_inc(a.proj_d, 1)
                dve.wait_ge(a.proj_a, t * 3 + 3)
                values_dve(dve, a.S[0], v).then_inc(a.proj_d, 1)
                dve.wait_ge(decayed, t * 32 + 32)
                attend_dve(dve, a, units, t, lambda u: decay[:, u.h, 0:u.nk], False, yT)


def compression_constants(nc, g, d, w1, w2, pec):
    with ExitStack() as ctx:
        sb, ps, sem = allocator(nc, ctx)
        pe_rows = sb("pe_rows", [CMP_LEN, P])
        pe_cols = sb("pe_cols", [P, CMP_LEN])
        pe_ps = ps("pe_ps", [P, CMP_LEN])
        pec_ps = ps("pec_ps", [P, 1])
        cleared, loaded, multiplied, copied = (
            sem(n) for n in ("k_cleared", "k_loaded", "k_multiplied", "k_copied"))
        block = ctx.enter_context(nc.Block())

        @block.gpsimd
        def _(pool):
            pool.memset(w1[LOW, :, HIGH], 0.0).then_inc(cleared, 1)
            pool.memset(w1[HIGH, :, LOW], 0.0).then_inc(cleared, 1)
            pool.memset(w2[LOW, HIGH], 0.0).then_inc(cleared, 1)
            pool.memset(w2[HIGH, LOW], 0.0).then_inc(cleared, 1)

        @block.sync
        def _(sp):
            for part, x, y, z in ((LOW, d["cmp_w1_k"], d["cmp_w2_k"], d["cmp_pe_k"]), (HIGH, d["cmp_w1_v"], d["cmp_w2_v"], d["cmp_pe_v"])):
                sp.dma_start(w1[part, :, part], x[0].rearrange("l d e -> d l e")).then_inc(loaded, 16)
                sp.dma_start(w2[part, part], y[0]).then_inc(loaded, 16)
                sp.dma_start(pe_rows[:, part], z[0]).then_inc(loaded, 16)

        @block.tensor
        def _(pe):
            pe.wait_ge(loaded, 96)
            pe.wait_ge(cleared, 4)
            pe.transpose(pe_ps[:, :], pe_rows[:, :], g.ident[0:CMP_LEN, 0:CMP_LEN]).then_inc(multiplied, 1)
            pe.wait_ge(copied, 1)
            for l in range(CMP_LEN):
                last = pe.matmul(pec_ps[:, :], w1[:, l, :], pe_cols[:, l:l + 1], start=(l == 0), stop=(l == CMP_LEN - 1))
            last.then_inc(multiplied, 1)

        @block.vector
        def _(dve):
            dve.wait_ge(multiplied, 1)
            dve.tensor_copy(pe_cols[:, :], pe_ps[:, :]).then_inc(copied, 1)
            dve.wait_ge(multiplied, 2)
            dve.tensor_copy(pec[:, :], pec_ps[:, :]).then_inc(copied, 1)


def nsa(nc, g, d, hT, yT, gates, room):
    CMP, SEL, WIN = range(3)
    units = []
    for h in range(2):
        for i in range(NT):
            k0 = max(0, i * P - WINDOW)
            units += [Unit(h=h, i=i, br=CMP, k0=0, nk=HD, first=True),
                      Unit(h=h, i=i, br=SEL, k0=0, nk=(i + 1) * P, first=False),
                      Unit(h=h, i=i, br=WIN, k0=k0, nk=(i + 1) * P - k0, first=False)]
    N = len(units)
    W_CMP = NT * HD
    W_WIN = WINDOW + P
    X_SEL, X_WIN, X_CMP = 0, S, S + W_WIN
    W_TAB = S + W_WIN + W_CMP
    PPG = NSA_HEADS // NSA_GROUPS // 2
    G_TILES = 3 + PPG
    GELU_A, GELU_B = 0.044715, 2 * (2 / 3.141592653589793) ** 0.5
    with ExitStack() as ctx:
        sb, ps, sem = allocator(nc, ctx)
        w1 = sb("cmp_w1", [P, CMP_LEN, P])
        w2 = sb("cmp_w2", [P, P])
        pec = sb("cmp_pec", [P, 1])
        compression_constants(nc, g, d, w1, w2, pec)
        a = AttentionBuffers(nc, ctx, "nsa")
        wq, wk, wv, wc = (sb(f"nsa_w{n}", [P, ND, P]) for n in "qkvc")
        q = [sb(f"nsa_q{h}", [P, S], F32R) for h in range(2)]
        k_hi = [sb(f"nsa_kh{b}", [P, S], F32R) for b in range(2)]
        k_lo = [sb(f"nsa_kl{b}", [P, S], F32R) for b in range(2)]
        v = sb("nsa_v", [P, NT * 2, P], F32R)
        kvc = sb("nsa_kvc", [P, S])
        hid = sb("cmp_hid", [P, N_CMP])
        cube = sb("cmp_cube", [P, N_CMP])
        act_out = sb("cmp_exp", [P, N_CMP])
        hidT = sb("cmp_hidT", [P, HD])
        kc_hi = sb("cmp_kh", [P, HD], F32R)
        kc_lo = sb("cmp_kl", [P, HD], F32R)
        vc = sb("cmp_v", [HD, P], F32R)
        dist = room[:, 0:W_TAB]
        bias = room[:, W_TAB:3 * W_TAB].rearrange("p (h n) -> p h n", h=2)
        pair_gates = sb("pair_gates", [P, NT, 6])
        w_group, cmp_pe, cmp_act, cmp_dve, tables, made = (
            sem(n) for n in ("nsa_w_group", "cmp_pe", "cmp_act", "cmp_dve", "tables", "dist_made"))
        C_DVE, C_ACT, C_PE = 9, 4, 2
        block = ctx.enter_context(nc.Block())

        @block.sync
        def _(sp):
            with sp.Fori(0, NSA_GROUPS) as grp:
                sp.wait_ge(a.proj_d, grp * G_TILES + 1)
                for w, half, c in ((wc, LOW, C_KCMP), (wc, HIGH, C_VCMP), (wk, LOW, C_KSLC), (wk, HIGH, C_KWIN),
                                   (wv, LOW, C_VSLC), (wv, HIGH, C_VWIN)):
                    sp.dma_start(w[:, :, half], d["w_in"][0, :, bass.ds(grp * HD + c, HD)].rearrange("(k p) n -> p k n", p=P)
                                 ).then_inc(w_group, 16)
                with sp.Fori(0, PPG) as pr:
                    t = grp * PPG + pr
                    sp.wait_ge(a.proj_d, grp * G_TILES + pr * 4 + 1)
                    sp.dma_start(wq[:, :, :], d["w_in"][0, :, bass.ds(t * P + C_QA, P)].rearrange("(k p) n -> p k n", p=P)
                                 ).then_inc(a.w_loaded, 16)

        def operands(u):
            tile = slice(u.i * P, (u.i + 1) * P)
            if u.br == CMP:
                return q[u.h][:, tile], (kc_hi, kc_lo), lambda b: vc[:, :], None
            b = u.br - SEL
            return (q[u.h][:, tile], (k_hi[b], k_lo[b]),
                    lambda n: v[:, 2 * (u.k0 // P + n) + b, :], None)

        def bias_of(u):
            if u.br == CMP:
                lo = X_CMP + u.i * HD
            elif u.br == SEL:
                lo = X_SEL + S - u.nk
            else:
                lo = X_WIN + W_WIN - u.nk
            return bias[:, u.h, lo:lo + u.nk]

        @block.tensor
        def _(pe):
            with pe.Fori(0, NSA_GROUPS) as grp:
                pe.wait_ge(a.score_read, grp * (PPG * N) + CR_SCORE)
                pe.wait_ge(w_group, grp * 96 + 96)
                project_columns(pe, a, 0, wc, hT)
                project_columns(pe, a, 1, wk, hT)
                pe.wait_ge(a.proj_d, grp * G_TILES + 2)
                project_rows(pe, a, 0, wv, hT)
                pe.wait_ge(a.combined, grp * (PPG * N) + CR_COMB)
                for l in range(CMP_LEN):
                    last = pe.matmul(a.O[0][:, 0:N_CMP], w1[:, l, :],
                                     kvc[:, l:l + CMP_STRIDE * (N_CMP - 1) + 1:CMP_STRIDE],
                                     start=(l == 0), stop=(l == CMP_LEN - 1))
                last.then_inc(cmp_pe, 1)
                pe.wait_ge(cmp_dve, grp * C_DVE + 7)
                pe.matmul(a.O[1][:, 0:HD], w2[:, :], hidT[:, :], start=True, stop=True)
                pe.matmul(a.O[1][0:HD, HD:P], hidT[:, :], w2[:, HIGH], start=True, stop=True).then_inc(cmp_pe, 1)
                with pe.Fori(0, PPG) as pr:
                    t = grp * PPG + pr
                    pe.wait_ge(cmp_dve, grp * C_DVE + C_DVE)
                    pe.wait_ge(a.score_read, t * N + CR_SCORE)
                    pe.wait_ge(a.proj_d, grp * G_TILES + pr + 4)
                    pe.wait_ge(a.w_loaded, t * 16 + 16)
                    project_columns(pe, a, 1, wq, hT)
                    pe.wait_ge(a.proj_d, grp * G_TILES + pr + 5)
                    attend_pe(pe, g, a, units, t, operands)

        @block.scalar
        def _(act):
            with act.Fori(0, NSA_GROUPS) as grp:
                act.wait_ge(a.proj_done, grp * G_TILES + 1)
                act.activation(kvc[:, 0:512], a.S[0][:, 0:512], ACT.Copy).then_inc(a.proj_a, 1)
                act.wait_ge(a.proj_done, grp * G_TILES + 2)
                keys_act(act, a.S[1], k_hi).then_inc(a.proj_a, 1)
                act.wait_ge(a.proj_done, grp * G_TILES + 3)
                values_act(act, a.S[0], v).then_inc(a.proj_a, 1)
                act.wait_ge(cmp_dve, grp * C_DVE + 4)
                act.activation(act_out[:, :], cube[:, :], ACT.Exp, scale=-GELU_B).then_inc(cmp_act, 1)
                act.wait_ge(cmp_pe, grp * C_PE + 2)
                act.activation(kc_hi[LOW, :], a.O[1][LOW, 0:HD], ACT.Copy).then_inc(cmp_act, 1)
                act.activation(kc_hi[HIGH, :], a.O[1][LOW, 0:HD], ACT.Copy).then_inc(cmp_act, 1)
                act.activation(vc[:, 0:HD], a.O[1][LOW, HD:P], ACT.Copy).then_inc(cmp_act, 1)
                with act.Fori(0, PPG) as pr:
                    t = grp * PPG + pr
                    act.wait_ge(a.proj_done, grp * G_TILES + pr + 4)
                    queries_act(act, a.S[1], q).then_inc(a.proj_a, 1)
                    attend_act(act, a, units, t)

        @block.gpsimd
        def _(pool):
            pool.sem_inc(a.sum_used, CR_FAC)
            for s in range(2):
                pool.memset(a.X[s][:, 0:P], 0.0).then_inc(a.cleared, 1)
            pool.memset(hidT[:, :], 0.0).then_inc(made, 1)
            tab = dict(allow_small_or_imprecise_dtypes=True, channel_multiplier=1)
            pool.iota(dist[:, X_SEL:X_SEL + S], pattern=[[-1, S]], base=S - P, **tab).then_inc(made, 1)
            pool.iota(dist[:, X_WIN:X_WIN + W_WIN], pattern=[[-1, W_WIN]], base=WINDOW, **tab).then_inc(made, 1)
            pool.iota(dist[:, X_CMP:], pattern=[[P, NT], [-CMP_STRIDE, HD]], base=1 - CMP_LEN, **tab).then_inc(made, 1)
            pool.wait_ge(made, 4)

            def keep(lo, hi, pattern, base, mult):
                pool.affine_select(out=dist[:, lo:hi], in_=dist[:, lo:hi], compare_op=ALU.is_ge, fill=BIG,
                                   base=base, pattern=pattern, channel_multiplier=mult).then_inc(made, 1)

            keep(X_SEL, X_SEL + S, [[-1, S]], S - P, 1)
            keep(X_WIN, X_WIN + W_WIN, [[-1, W_WIN]], WINDOW, 1)
            keep(X_CMP, W_TAB, [[P, NT], [-CMP_STRIDE, HD]], 1 - CMP_LEN, 1)
            pool.wait_ge(made, 6)
            keep(X_WIN, X_WIN + W_WIN, [[1, W_WIN]], -1, -1)
            pool.wait_ge(made, 8)
            with pool.Fori(0, NSA_GROUPS) as grp:
                with pool.Fori(0, PPG) as pr:
                    t = grp * PPG + pr
                    count = in_register(pool, a, t * N + CR_SCORE)
                    pool.wait_ge(made, 7)
                    pool.wait_ge(a.score_read, count)
                    pool.tensor_scalar(bias[:, 0, :], dist[:, :], 0.5, None, ALU.mult).then_inc(tables, 1)
                    pool.tensor_scalar(bias[:, 1, :], dist[:, :], 0.25, None, ALU.mult).then_inc(tables, 1)
                    pool.wait_ge(a.combined, t * N + CR_COMB)
                    pool.tensor_copy(pair_gates[:, :, :], gates[:, :, bass.ds(t * 6, 6)]).then_inc(tables, 1)
                    count = in_register(pool, a, t * 4 + 3)
                    pool.wait_ge(made, 7)
                    pool.wait_ge(tables, count)
                    pool.tensor_scalar(dist[:, :], dist[:, :], 0.25, None, ALU.mult).then_inc(tables, 1)
                    attend_pool(pool, a, units, t, lambda u: pair_gates[:, u.i, 3 * u.h + u.br:3 * u.h + u.br + 1])
                    pool.wait_ge(tables, t * 4 + 4)

        @block.vector
        def _(dve):
            dve.sem_inc(a.score_read, CR_SCORE)
            dve.sem_inc(a.lo_done, CR_LO)
            dve.sem_inc(a.combined, CR_COMB)
            dve.sem_inc(a.pv_done, CR_PV)
            dve.sem_inc(a.turned, CR_TURN)
            dve.sem_inc(a.proj_d, 1)
            dve.sem_inc(a.inv_done, CR_FAC)
            dve.wait_ge(a.cleared, 2)
            dve.wait_ge(made, 1)
            with dve.Fori(0, NSA_GROUPS) as grp:
                dve.wait_ge(a.proj_done, grp * G_TILES + 1)
                dve.wait_ge(a.proj_a, grp * G_TILES + 1)
                dve.tensor_copy(kvc[:, 512:S], a.S[0][:, 512:S]).then_inc(a.proj_d, 1)
                dve.wait_ge(a.proj_a, grp * G_TILES + 2)
                keys_dve(dve, a.S[1], k_hi, k_lo).then_inc(a.proj_d, 1)
                dve.wait_ge(a.proj_a, grp * G_TILES + 3)
                values_dve(dve, a.S[0], v).then_inc(a.proj_d, 1)
                dve.wait_ge(cmp_pe, grp * C_PE + 1)
                chain = Chain(dve, cmp_dve, grp * C_DVE)
                chain.link(dve.tensor_scalar(hid[:, :], a.O[0][:, 0:N_CMP], pec[:, 0:1], None, ALU.add))
                chain.link(dve.tensor_tensor(cube[:, :], hid[:, :], hid[:, :], ALU.mult))
                chain.link(dve.tensor_scalar(cube[:, :], cube[:, :], GELU_A, 1.0, ALU.mult, ALU.add))
                chain.link(dve.tensor_tensor(cube[:, :], cube[:, :], hid[:, :], ALU.mult))
                dve.wait_ge(cmp_act, grp * C_ACT + 1)
                chain.link(dve.tensor_scalar_add(act_out[:, :], act_out[:, :], 1.0))
                chain.link(dve.reciprocal(act_out[:, :], act_out[:, :]))
                chain.link(dve.tensor_tensor(hidT[:, 0:N_CMP], hid[:, :], act_out[:, :], ALU.mult))
                dve.wait_ge(cmp_act, grp * C_ACT + 4)
                dve.tensor_tensor(kc_lo[LOW, :], a.O[1][LOW, 0:HD], kc_hi[LOW, :].bitcast(F32), ALU.subtract)
                chain.link(dve.tensor_tensor(kc_lo[HIGH, :], a.O[1][LOW, 0:HD], kc_hi[LOW, :].bitcast(F32), ALU.subtract))
                dve.tensor_tensor(vc[:, HD:P], a.O[1][LOW, HD:P], vc[:, 0:HD].bitcast(F32), ALU.subtract
                                  ).then_inc(cmp_dve, 1)
                with dve.Fori(0, PPG) as pr:
                    t = grp * PPG + pr
                    dve.wait_ge(a.proj_a, grp * G_TILES + pr + 4)
                    queries_dve(dve, a.S[1], q).then_inc(a.proj_d, 1)
                    dve.wait_ge(tables, t * 4 + 2)
                    attend_dve(dve, a, units, t, bias_of, True, yT)



def merge(nc, g, d, hT, yaT, ybT, mixT, mod, w_out, w_out_loaded):
    NY = yaT.shape[1]
    W_ADA, CREDIT = 256, 2 * ND
    with ExitStack() as ctx:
        sb, ps, sem = allocator(nc, ctx)
        w_gate = [[sb(f"w_mg{s}{m}", [P, ND, P]) for m in range(2)] for s in range(2)]
        w_o = [[sb(f"w_o{s}{m}", [P, NY, P]) for m in range(2)] for s in range(2)]
        e = [sb(f"mg_e{h}", [P, 2, 512]) for h in range(2)]
        prod = [sb(f"mg_p{h}", [P, 2, 512]) for h in range(2)]
        w_ada = [sb(f"mg_wada{h}", [P, ND, W_ADA]) for h in range(2)]
        bank = [[ps(f"mg_ps{h}{m}", [P, 512]) for m in range(4)] for h in range(2)]
        loaded = [sem(f"mg_loaded{s}") for s in range(2)]
        ada_loaded = [sem(f"mg_ada_loaded{h}") for h in range(2)]
        weighed = sem("mg_weighed")
        multiplied, exped, plus1, step, used, mixed = (
            sem(n) for n in ("mg_multiplied", "mg_exped", "mg_plus1", "mg_step", "mg_used", "mg_mixed"))
        block = ctx.enter_context(nc.Block())
        halves = [slice(0, 512), slice(512, S)]

        @block.sync
        def _(sp):
            with sp.Fori(0, ND // 2) as r:
                for s in range(2):
                    c = r * 2 + s
                    sp.wait_ge(multiplied, c * 2 + 2)
                    for m in range(2):
                        sp.dma_start(w_gate[s][m][:, :, :], d["w_in"][0, :, bass.ds(c * P + (C_MG + m * D), P)]
                                     .rearrange("(k p) n -> p k n", p=P)).then_inc(loaded[s], 16)
                        w = (d["w_o_nsa"], d["w_o_fox"])[m]
                        sp.dma_start(w_o[s][m][:, :, :], w[0, :, bass.ds(c * P, P)]
                                     .rearrange("(k p) n -> p k n", p=P)).then_inc(loaded[s], 16)
                    for h in range(2):
                        n = c * 2 + h
                        sp.wait_ge(weighed, n * ND + ND)
                        sp.dma_start(w_ada[h][:, :, :], d["w_ada"][0, :, bass.ds(n * W_ADA + 2 * D, W_ADA)]
                                     .rearrange("(k p) n -> p k n", p=P)).then_inc(ada_loaded[h], 16)
            sp.dma_start(w_out[:, :, :], d["w_out"][0].rearrange("(k p) n -> p k n", p=P)).then_inc(w_out_loaded, 16)
            sp.wait_ge(w_out_loaded, 16)

        @block.tensor
        def _(pe):
            pe.sem_inc(multiplied, 4)
            with pe.Fori(0, ND // 2) as r:
                for s in range(2):
                    c = r * 2 + s
                    pe.wait_ge(loaded[s], r * 64 + 64)
                    for h in range(2):
                        pe.wait_ge(used, c * 2 + h + 1)
                        for m in range(2):
                            for k in range(ND):
                                pe.matmul(bank[h][m][:, :], w_gate[s][m][:, k, :], hT[:, k, halves[h]],
                                          start=(k == 0), stop=(k == ND - 1))
                        for m, y in enumerate((yaT, ybT)):
                            for k in range(NY):
                                last = pe.matmul(bank[h][2 + m][:, :], w_o[s][m][:, k, :], y[:, k, halves[h]],
                                                 start=(k == 0), stop=(k == NY - 1))
                        last.then_inc(multiplied, 1)

        @block.scalar
        def _(act):
            with act.Fori(0, ND) as c:
                for h in range(2):
                    n = c * 2 + h
                    act.wait_ge(multiplied, n + 5)
                    act.wait_ge(used, n + 1)
                    act.activation(e[h][:, 0, :], bank[h][0][:, :], ACT.Exp, scale=-1.0)
                    act.activation(e[h][:, 1, :], bank[h][1][:, :], ACT.Exp, scale=-1.0).then_inc(exped, 1)

        @block.vector
        def _(dve):
            dve.sem_inc(used, 2)
            dve.sem_inc(weighed, CREDIT)
            with dve.Fori(0, ND) as c:
                for h in range(2):
                    n = c * 2 + h
                    dve.wait_ge(exped, n + 1)
                    dve.wait_ge(mixed, n + 1)
                    chain = Chain(dve, step, n * 2)
                    chain.link(dve.tensor_scalar_add(e[h][:, :, :], e[h][:, :, :], 1.0))
                    chain.link(dve.reciprocal(e[h][:, :, :], e[h][:, :, :]))
                    dve.tensor_tensor(prod[h][:, 0, :], e[h][:, 0, :], bank[h][2][:, :], ALU.mult)
                    dve.tensor_tensor(prod[h][:, 1, :], e[h][:, 1, :], bank[h][3][:, :], ALU.mult).then_inc(used, 1)
                    dve.wait_ge(ada_loaded[h], c * 16 + 16)
                    part = mod[:, bass.ds(n * W_ADA, W_ADA)]
                    chain = Chain(dve, weighed, n * ND + CREDIT)
                    chain.link(dve.tensor_scalar(part, w_ada[h][:, 0, :], g.csilu[:, 0:1], None, ALU.mult))
                    for k in range(1, ND):
                        chain.link(dve.scalar_tensor_tensor(out=part, in0=w_ada[h][:, k, :], scalar=g.csilu[:, k:k + 1],
                                                            in1=part, op0=ALU.mult, op1=ALU.add))

        @block.gpsimd
        def _(pool):
            pool.sem_inc(mixed, 2)
            with pool.Fori(0, ND) as c:
                for h in range(2):
                    pool.wait_ge(used, c * 2 + h + 3)
                    pool.tensor_tensor(mixT[:, bass.ds(c, 1), halves[h]], prod[h][:, 0, :].unsqueeze(1),
                                       prod[h][:, 1, :].unsqueeze(1), ALU.add).then_inc(mixed, 1)



def project_out(nc, g, d, mixT, mod, w, w_out_loaded, x1, logits, h2_dram, expert_weights):
    GT_M, SH_F, SC_F, GT_F = (slice(i * D, (i + 1) * D) for i in range(4))
    NL = N_GRP + N_EXP
    with ExitStack() as ctx:
        sb, ps, sem = allocator(nc, ctx)
        b_ada = sb("b_ada_sb", [P, 4 * D])
        wr = sb("w_router", [P, ND, NL])
        br = sb("b_router", [P, NL])
        gain = sb("gains", [P, D])
        mt = [sb(f"mt{s}", [P, ND, P]) for s in range(2)]
        x = [sb(f"xo{s}", [P, D]) for s in range(2)]
        scaled = [sb(f"scaled{s}", [P, D]) for s in range(2)]
        h2 = [sb(f"h2{s}", [P, D]) for s in range(2)]
        h2T = sb("h2T", [P, ND, P])
        ms = [sb(f"oms{s}", [P, 2]) for s in range(2)]
        rstd = [sb(f"orstd{s}", [P, 2]) for s in range(2)]
        junk = b_ada[:, 0:D]
        M = [ps(f"oM{s}", [P, D]) for s in range(2)]
        TP = ps("oT", [P, D])
        LG = ps("oL", [P, NL])
        SUM = ps("oSum", [P, 512])
        b_loaded, summed, added = (sem(f"o_{n}") for n in ("b_loaded", "summed", "added"))
        x_loaded = [sem(f"o_x_loaded{s}") for s in range(2)]
        stored = [sem(f"o_stored{s}") for s in range(2)]
        w_loaded, gains, gain_used, staged, mixed, astep, dstep, shifted, turned, out_a, out_d, routed, logit = (
            sem(f"o_{n}") for n in ("w_loaded", "gains", "gain_used", "staged", "mixed", "astep", "dstep", "shifted",
                                    "turned", "out_a", "out_d", "routed", "logit"))
        A_STEPS, D_STEPS, CREDIT = 4, 5, 10
        block = ctx.enter_context(nc.Block())

        def over_tiles(eng, first, tile):
            first(0, 0)
            with eng.Fori(0, NT // 2 - 1) as r:
                for s in range(2):
                    first(r * 2 + s + 1, 1 - s)
                    tile(r * 2 + s, s)
            first(NT - 1, 1)
            tile(NT - 2, 0)
            tile(NT - 1, 1)

        @block.sync
        def _(sp):
            sp.dma_start(b_ada[:, :], d["b_ada"][0:1, 2 * D:].to_broadcast([P, 4 * D])).then_inc(b_loaded, 16)
            sp.dma_start(gain[:, :], d["g_post_mix"][0:1, :].to_broadcast([P, D])).then_inc(gains, 16)
            sp.dma_start(wr[:, :, 0:N_GRP], d["w_router_group"][0].rearrange("(k p) n -> p k n", p=P)).then_inc(w_loaded, 16)
            sp.dma_start(wr[:, :, N_GRP:], d["w_router_expert"][0].rearrange("(k p) n -> p k n", p=P)).then_inc(w_loaded, 16)
            sp.dma_start(br[:, 0:N_GRP], d["b_router_group"][0:1, :].to_broadcast([P, N_GRP])).then_inc(w_loaded, 16)
            sp.dma_start(br[:, N_GRP:], d["b_router_expert"][0:1, :].to_broadcast([P, N_EXP])).then_inc(w_loaded, 16)
            for n, gd in enumerate((d["g_pre_ffn"], d["g_post_ffn"])):
                sp.wait_ge(gain_used, n + 1)
                sp.dma_start(gain[:, :], gd[0:1, :].to_broadcast([P, D])).then_inc(gains, 16)

            def load(i, s):
                sp.wait_ge(dstep, i * D_STEPS + 3)
                sp.dma_start(x[s][:, :], d["x"][0, bass.ds(i * P, P), :]).then_inc(x_loaded[s], 16)

            def store(i, s):
                sp.wait_ge(shifted, i + 1)
                sp.dma_start(h2_dram[bass.ds(i * P, P), :], h2[s][:, :]).then_inc(stored[s], 16)

            for s in range(2):
                sp.sem_inc(stored[s], 16)
            expert_weights.load_gate_up(sp, d, 0, 0)
            over_tiles(sp, load, store)
            for s in range(2):
                sp.wait_ge(stored[s], (NT // 2 + 1) * 16)

        @block.tensor
        def _(pe):
            def project(i, s):
                pe.wait_ge(staged, i + 1)
                pe.wait_ge(dstep, i * D_STEPS + 2)
                for half in range(2):
                    cols = slice(half * 512, (half + 1) * 512)
                    for k in range(ND):
                        last = pe.matmul(M[s][:, cols], mt[s][:, k, :], w[:, k, cols], start=(k == 0), stop=(k == ND - 1))
                last.then_inc(mixed, 1)

            def route(i, s):
                pe.wait_ge(shifted, i + 1)
                pe.wait_ge(out_a, i + 1)
                pe.wait_ge(out_d, i + 1)
                for k in range(ND):
                    last = pe.transpose(TP[:, k * P:(k + 1) * P], h2[s][:, k * P:(k + 1) * P], g.ident[:, :])
                last.then_inc(turned, 1)
                pe.wait_ge(out_a, i + 2)
                pe.wait_ge(out_d, i + 2)
                pe.wait_ge(logit, i + 1)
                for k in range(ND):
                    last = pe.matmul(LG[:, :], h2T[:, k, :], wr[:, k, :], start=(k == 0), stop=(k == ND - 1))
                last.then_inc(routed, 1)

            with pe.Fori(0, 4 * D // 512) as n:
                pe.wait_ge(added, n + 1)
                pe.matmul(SUM[:, :], g.ones[:, :], mod[:, bass.ds(n * 512, 512)], start=True, stop=True
                          ).then_inc(summed, 1)
            pe.wait_ge(w_out_loaded, 16)
            pe.wait_ge(w_loaded, 64)
            over_tiles(pe, project, route)

        @block.scalar
        def _(act):
            def stage(i, s):
                act.wait_ge(mixed, i + 1)
                act.activation(mt[s][:, :, :], mixT[:, :, bass.ds(i * P, P)], ACT.Copy).then_inc(staged, 1)

            def norms(i, s):
                chain = Chain(act, astep, i * A_STEPS)
                act.wait_ge(mixed, i + 3)
                act.wait_ge(dstep, i * D_STEPS + 4)
                chain.link(act.activation(junk[:, :], M[s][:, :], ACT.Square, scale=D ** -0.5, accum_out=ms[s][:, 0:1]))
                chain.link(act.activation(ms[s][:, 0:1], ms[s][:, 0:1], ACT.Sqrt, bias=g.eps[:, :]))
                act.wait_ge(dstep, i * D_STEPS + (CREDIT + 3))
                chain.link(act.activation(junk[:, :], x1[:, bass.ds(i, 1), :].rearrange("p a n -> p (a n)"), ACT.Square,
                                          scale=D ** -0.5, accum_out=ms[s][:, 1:2]))
                chain.link(act.activation(ms[s][:, 1:2], ms[s][:, 1:2], ACT.Sqrt, bias=g.eps[:, :]))
                act.wait_ge(turned, i + 1)
                act.wait_ge(routed, i + 1)
                act.activation(h2T[:, 0:4, :], TP[:, 0:512].rearrange("p (k t) -> p k t", t=P), ACT.Copy).then_inc(out_a, 1)

            act.sem_inc(mixed, 2)
            act.wait_ge(added, 1 + 4 * D // 512)
            over_tiles(act, stage, norms)

        @block.gpsimd
        def _(pool):
            with pool.Fori(0, NT // 2) as r:
                for s in range(2):
                    i = r * 2 + s
                    pool.wait_ge(dstep, i * D_STEPS + (CREDIT + 5))
                    pool.tensor_tensor(h2[s][:, :], h2[s][:, :], mod[:, SH_F], ALU.add).then_inc(shifted, 1)

        @block.vector
        def _(dve):
            dve.sem_inc(dstep, CREDIT)
            dve.sem_inc(out_d, 1)
            dve.sem_inc(out_a, 1)
            dve.sem_inc(logit, 1)
            dve.sem_inc(routed, 1)
            dve.sem_inc(added, 1)
            dve.wait_ge(b_loaded, 16)
            with dve.Fori(0, 4 * D // 512) as n:
                part = mod[:, bass.ds(n * 512, 512)]
                dve.wait_ge(summed, n + 1)
                dve.tensor_tensor(part, SUM[:, :], b_ada[:, bass.ds(n * 512, 512)], ALU.add).then_inc(added, 1)
            dve.wait_ge(added, 1 + 4 * D // 512)
            for n, (part, plus) in enumerate(((GT_M, 0.0), (SC_F, 1.0), (GT_F, 0.0))):
                dve.wait_ge(gains, n * 16 + 16)
                dve.scalar_tensor_tensor(out=mod[:, part], in0=mod[:, part], scalar=plus, in1=gain[:, :],
                                         op0=ALU.add, op1=ALU.mult).then_inc(gain_used, 1)
            dve.wait_ge(gain_used, 3)
            dve.wait_ge(w_loaded, 64)
            with dve.Fori(0, NT // 2) as r:
                for s in range(2):
                    i = r * 2 + s
                    x1_i = x1[:, bass.ds(i, 1), :].rearrange("p a n -> p (a n)")
                    chain = Chain(dve, dstep, i * D_STEPS + CREDIT)
                    dve.wait_ge(astep, i * A_STEPS + 2)
                    chain.link(dve.reciprocal(rstd[s][:, 0:1], ms[s][:, 0:1]))
                    chain.link(dve.scalar_tensor_tensor(out=scaled[s][:, :], in0=M[s][:, :], scalar=rstd[s][:, 0:1],
                                                        in1=mod[:, GT_M], op0=ALU.mult, op1=ALU.mult))
                    dve.wait_ge(x_loaded[s], r * 16 + 16)
                    chain.link(dve.tensor_tensor(x1_i, scaled[s][:, :], x[s][:, :], ALU.add))
                    dve.wait_ge(astep, i * A_STEPS + 4)
                    chain.link(dve.reciprocal(rstd[s][:, 1:2], ms[s][:, 1:2]))
                    dve.wait_ge(stored[s], r * 16 + 16)
                    chain.link(dve.scalar_tensor_tensor(out=h2[s][:, :], in0=x1_i, scalar=rstd[s][:, 1:2],
                                                        in1=mod[:, SC_F], op0=ALU.mult, op1=ALU.mult))
                    dve.wait_ge(turned, i + 1)
                    dve.wait_ge(routed, i + 1)
                    dve.tensor_copy(h2T[:, 4:8, :], TP[:, 512:D].rearrange("p (k t) -> p k t", t=P)).then_inc(out_d, 1)
                    dve.wait_ge(routed, i + 2)
                    dve.tensor_tensor(logits[:, bass.ds(i, 1), :], LG[:, :].unsqueeze(1), br[:, :].unsqueeze(1), ALU.add
                                      ).then_inc(logit, 1)



def route(nc, g, logits, rows, weights, ids, overflow):
    with ExitStack() as ctx:
        sb, ps, sem = allocator(nc, ctx)
        E, T2 = N_EXP, 2 * NT
        gpad = sb("gpad", [P, NT, 8])
        gtop = sb("gtop", [P, NT, 8])
        gidx = sb("gidx", [P, NT, 8], U32)
        gsub = sb("gsub", [P, NT, N_GRP])
        gsum = sb("gsum", [P, NT])
        pg = sb("pg", [P, NT])
        gif = sb("gif", [P, NT])
        grp_of = sb("grp_of", [P, E])
        exp_no = sb("exp_no", [P, E])
        in_grp = sb("in_grp", [P, NT, E])
        outside = sb("outside", [P, NT, E])
        masked = sb("masked", [P, NT, E])
        etop = sb("etop", [P, NT, 8])
        eidx = sb("eidx", [P, NT, 8], U32)
        ef = sb("ef", [P, 2, NT])
        diff = sb("diff", [P, NT])
        den = sb("den", [P, NT])
        one_hot = sb("one_hot", [P, 2, NT, E])
        prefix = sb("prefix", [P, NT + 1, E])
        both = sb("both", [P, NT, E])
        before = sb("before_me", [P, P])
        rank_all = sb("rank_all", [P, NT, E])
        picked = sb("picked", [P, 2, NT, E])
        rank = sb("rank", [P, 2, NT])
        over = sb("over_no", [P, 2, NT])
        start = sb("over_start", [P, 2, NT])
        n_over = sb("n_over", [P, E])
        over_end = sb("over_end", [P, E])
        over_beg = sb("over_beg", [P, E])
        zero = sb("rzero", [P, E])
        place = sb("place", [P, 2, NT])
        col = sb("colno", [P, 2, NT])
        tmp = sb("rtmp", [P, 2, NT])
        block_no = sb("block_no", [P, N_OVF + 1])
        cmpb = sb("cmpb", [P, N_OVF + 1, E])
        bexp = sb("bexp", [P, N_OVF + 1])
        token = sb("token_no", [P, NT])
        slot_no = sb("slot_no", [P, P])
        col_no = sb("col_no", [P, N_COL])
        at_slot = sb("at_slot", [P, T2, P])
        at_block = sb("at_block", [P, T2, N_COL])
        R = ps("rank_ps", [P, NT * E])
        C = ps("count_ps", [P, E])
        ID = ps("ids_ps", [P, N_COL])
        made, step, ranked, aexp = (sem(f"r_{n}") for n in ("made", "step", "ranked", "aexp"))
        counted = {}
        block = ctx.enter_context(nc.Block())

        def per_token(ap):
            return ap.unsqueeze(2).to_broadcast([P, NT, E])

        def per_expert(ap):
            return ap.unsqueeze(1).to_broadcast([P, NT, E])

        @block.vector
        def _(dve):
            chain = Chain(dve, step)
            link = chain.link
            dve.wait_ge(made, 11)
            link(dve.tensor_copy(gpad[:, :, 0:N_GRP], logits[:, :, 0:N_GRP]))
            for i in range(NT):
                last = dve.max(gtop[:, i, :], gpad[:, i, :])
            link(last)
            for i in range(NT):
                last = dve.max_index(gidx[:, i, :], gtop[:, i, :], gpad[:, i, :])
            link(last)
            link(dve.tensor_tensor(gsub[:, :, :], logits[:, :, 0:N_GRP],
                                   gtop[:, :, 0:1].to_broadcast([P, NT, N_GRP]), ALU.subtract))
            counted["gsub"] = chain.n
            link(dve.tensor_copy(gif[:, :], gidx[:, :, 0]))
            link(dve.tensor_tensor(in_grp[:, :, :], per_expert(grp_of[:, :]), per_token(gif[:, :]), ALU.is_equal))
            link(dve.tensor_scalar(outside[:, :, :], in_grp[:, :, :], BIG, -BIG, ALU.mult, ALU.add))
            link(dve.tensor_tensor(masked[:, :, :], logits[:, :, N_GRP:], in_grp[:, :, :], ALU.mult))
            link(dve.tensor_tensor(masked[:, :, :], masked[:, :, :], outside[:, :, :], ALU.add))
            for i in range(NT):
                last = dve.max(etop[:, i, :], masked[:, i, :])
            link(last)
            for i in range(NT):
                last = dve.max_index(eidx[:, i, :], etop[:, i, :], masked[:, i, :])
            link(last)
            link(dve.tensor_tensor(diff[:, :], etop[:, :, 1], etop[:, :, 0], ALU.subtract))
            counted["diff"] = chain.n
            for k in range(2):
                last = dve.tensor_copy(ef[:, k, :], eidx[:, :, k])
            link(last)
            for k in range(2):
                last = dve.tensor_tensor(one_hot[:, k, :, :], per_expert(exp_no[:, :]), per_token(ef[:, k, :]), ALU.is_equal)
            link(last)
            link(dve.tensor_tensor(both[:, :, :], one_hot[:, 0, :, :], one_hot[:, 1, :, :], ALU.add))
            for i in range(NT):
                link(dve.tensor_tensor(prefix[:, i + 1, :], prefix[:, i, :], both[:, i, :], ALU.add))
            counted["prefix"] = chain.n
            dve.wait_ge(aexp, 2)
            link(dve.tensor_reduce(gsum[:, :], gsub[:, :, :], AX.X, ALU.add))
            link(dve.reciprocal(pg[:, :], gsum[:, :]))
            link(dve.tensor_scalar_add(den[:, :], diff[:, :], 1.0))
            link(dve.reciprocal(den[:, :], den[:, :]))
            link(dve.tensor_tensor(weights[:, 0, :], pg[:, :], den[:, :], ALU.mult))
            link(dve.tensor_tensor(weights[:, 1, :], weights[:, 0, :], diff[:, :], ALU.mult))
            dve.wait_ge(ranked, 1)
            link(dve.tensor_copy(rank_all[:, :, :], R[:, :].rearrange("p (t e) -> p t e", e=E)))
            for k in range(2):
                last = dve.tensor_tensor(picked[:, k, :, :], one_hot[:, k, :, :], rank_all[:, :, :], ALU.mult)
            link(last)
            link(dve.tensor_reduce(rank[:, :, :], picked[:, :, :, :], AX.X, ALU.add))
            link(dve.tensor_scalar(n_over[:, :], C[:, :], float(P), None, ALU.is_gt))
            for m in range(2, S // P):
                link(dve.scalar_tensor_tensor(out=n_over[:, :], in0=C[:, :], scalar=float(m * P), in1=n_over[:, :],
                                              op0=ALU.is_gt, op1=ALU.add))
            link(dve.tensor_tensor_scan(over_end[:, :], n_over[:, :], zero[:, :], 0.0, ALU.add, ALU.add))
            link(dve.tensor_tensor(over_beg[:, :], over_end[:, :], n_over[:, :], ALU.subtract))
            for k in range(2):
                last = dve.tensor_tensor(picked[:, k, :, :], one_hot[:, k, :, :], per_expert(over_beg[:, :]), ALU.mult)
            link(last)
            link(dve.tensor_reduce(start[:, :, :], picked[:, :, :, :], AX.X, ALU.add))
            link(dve.tensor_scalar(over[:, :, :], rank[:, :, :], float(P), None, ALU.is_ge))
            for m in range(2, S // P):
                link(dve.scalar_tensor_tensor(out=over[:, :, :], in0=rank[:, :, :], scalar=float(m * P),
                                              in1=over[:, :, :], op0=ALU.is_ge, op1=ALU.add))
            link(dve.scalar_tensor_tensor(out=place[:, :, :], in0=over[:, :, :], scalar=-float(P), in1=rank[:, :, :],
                                          op0=ALU.mult, op1=ALU.add))
            link(dve.scalar_tensor_tensor(out=tmp[:, :, :], in0=over[:, :, :], scalar=float(E - 1), in1=start[:, :, :],
                                          op0=ALU.add, op1=ALU.add))
            link(dve.tensor_tensor(tmp[:, :, :], tmp[:, :, :], ef[:, :, :], ALU.subtract))
            link(dve.scalar_tensor_tensor(out=tmp[:, :, :], in0=over[:, :, :], scalar=1.0, in1=tmp[:, :, :],
                                          op0=ALU.min, op1=ALU.mult))
            link(dve.tensor_tensor(col[:, :, :], tmp[:, :, :], ef[:, :, :], ALU.add))
            link(dve.tensor_tensor(at_slot[:, :, :], slot_no[:, :].unsqueeze(1).to_broadcast([P, T2, P]),
                                   place[:, :, :].rearrange("p k t -> p (k t)").unsqueeze(2).to_broadcast([P, T2, P]),
                                   ALU.is_equal))
            link(dve.tensor_tensor(at_block[:, :, :], col_no[:, :].unsqueeze(1).to_broadcast([P, T2, N_COL]),
                                   col[:, :, :].rearrange("p k t -> p (k t)").unsqueeze(2).to_broadcast([P, T2, N_COL]),
                                   ALU.is_equal))
            for k in range(2):
                last = dve.tensor_tensor(at_block[:, k * NT:(k + 1) * NT, :], at_block[:, k * NT:(k + 1) * NT, :],
                                         token[:, :].unsqueeze(2).to_broadcast([P, NT, N_COL]), ALU.mult)
            link(last)
            counted["slots"] = chain.n
            link(dve.scalar_tensor_tensor(out=rows[:, :, :], in0=col[:, :, :], scalar=float(P), in1=place[:, :, :],
                                          op0=ALU.mult, op1=ALU.add))
            link(dve.tensor_tensor(cmpb[:, :, :], over_end[:, :].unsqueeze(1).to_broadcast([P, N_OVF + 1, E]),
                                   block_no[:, :].unsqueeze(2).to_broadcast([P, N_OVF + 1, E]), ALU.is_le))
            link(dve.tensor_reduce(bexp[:, :], cmpb[:, :, :], AX.X, ALU.add))
            link(dve.tensor_scalar(overflow[:, 1:], bexp[:, :], float(E - 1), None, ALU.min))
            link(dve.tensor_copy(overflow[:, 0:1], over_end[:, E - 1:E]))
            dve.wait_ge(ranked, 2)
            link(dve.tensor_copy(ids[:, :], ID[:, :]))

        @block.scalar
        def _(act):
            act.wait_ge(step, counted["gsub"])
            act.activation(gsub[:, :, :], gsub[:, :, :], ACT.Exp).then_inc(aexp, 1)
            act.wait_ge(step, counted["diff"])
            act.activation(diff[:, :], diff[:, :], ACT.Exp).then_inc(aexp, 1)

        @block.tensor
        def _(pe):
            pe.wait_ge(step, counted["prefix"])
            pe.wait_ge(made, 11)
            pe.matmul(R[:, :], before[:, :], both[:, :, :].rearrange("p t e -> p (t e)"), start=True, stop=False)
            pe.matmul(R[:, :], g.ones[:, :], prefix[:, 0:NT, :].rearrange("p t e -> p (t e)"), start=False, stop=True)
            pe.matmul(C[:, :], g.ones[:, :], prefix[:, NT, :], start=True, stop=True).then_inc(ranked, 1)
            pe.wait_ge(step, counted["slots"])
            for n in range(T2):
                last = pe.matmul(ID[:, :], at_slot[:, n, :], at_block[:, n, :], start=(n == 0), stop=(n == T2 - 1))
            last.then_inc(ranked, 1)

        @block.gpsimd
        def _(pool):
            flt = dict(allow_small_or_imprecise_dtypes=True)
            pool.memset(gpad[:, :, :], -BIG).then_inc(made, 1)
            pool.memset(prefix[:, 0, :], 0.0).then_inc(made, 1)
            pool.memset(zero[:, :], 0.0).then_inc(made, 1)
            pool.memset(before[:, :], 1.0).then_inc(made, 1)
            pool.iota(grp_of[:, :], pattern=[[1, N_GRP], [0, PER_GRP]], base=0, channel_multiplier=0, **flt).then_inc(made, 1)
            pool.iota(exp_no[:, :], pattern=[[1, E]], base=0, channel_multiplier=0, **flt).then_inc(made, 1)
            pool.iota(block_no[:, :], pattern=[[1, N_OVF + 1]], base=0, channel_multiplier=0, **flt).then_inc(made, 1)
            pool.iota(token[:, :], pattern=[[P, NT]], base=0, channel_multiplier=1, **flt).then_inc(made, 1)
            pool.iota(slot_no[:, :], pattern=[[1, P]], base=0, channel_multiplier=0, **flt).then_inc(made, 1)
            pool.iota(col_no[:, :], pattern=[[1, N_COL]], base=0, channel_multiplier=0, **flt).then_inc(made, 1)
            pool.wait_ge(made, 10)
            pool.affine_select(out=before[:, :], in_=before[:, :], compare_op=ALU.is_gt, fill=0.0, base=0,
                               pattern=[[1, P]], channel_multiplier=-1).then_inc(made, 1)



class ExpertWeights:

    def __init__(self, sb, sem, room):
        KD = D_EXP // P
        self.gate, self.up = [], []
        self.add_slot(sb)
        self.down = [room[:, s * KD * D:(s + 1) * KD * D].rearrange("p (k n) -> p k n", n=D) for s in range(2)]
        self.gu_loaded = [sem(f"e_gu_loaded{s}") for s in range(2)]
        self.d_loaded = [sem(f"e_d_loaded{s}") for s in range(2)]

    def add_slot(self, sb):
        self.gate.append(sb(f"wgate{len(self.gate)}", [P, ND, D_EXP]))
        self.up.append(sb(f"wup{len(self.up)}", [P, ND, D_EXP]))

    def load_gate_up(self, eng, d, e, s):
        for w, source in ((self.gate, d["w_exp_gate"]), (self.up, d["w_exp_up"])):
            eng.dma_start(w[s][:, :, :], source[0, bass.ds(e, 1)].rearrange("a (k p) n -> p (a k) n", p=P)
                          ).then_inc(self.gu_loaded[s], 16)

    def load_down(self, eng, d, e, s):
        eng.dma_start(self.down[s][:, :, :], d["w_exp_down"][0, bass.ds(e, 1)].rearrange("a (k p) n -> p (a k) n", p=P)
                      ).then_inc(self.d_loaded[s], 16)


def experts(nc, g, d, w, ids, overflow, h2_dram, y_dram):
    KD = D_EXP // P
    with ExitStack() as ctx:
        sb, ps, sem = allocator(nc, ctx)
        w.add_slot(sb)
        idx = [sb(f"idx{s}", [P, 1], U32) for s in range(2)]
        xb = [sb(f"xb{s}", [P, D]) for s in range(2)]
        xT = [sb(f"xT{s}", [P, ND, P]) for s in range(2)]
        sig = sb("sig", [P, D_EXP])
        prod = sb("gu", [P, D_EXP])
        aT = sb("aT", [P, KD, P])
        y = [sb(f"yb{s}", [P, D]) for s in range(2)]
        spare = sb("spare", [P, 1])
        carried = sem("e_carried")
        TX = ps("TX", [P, D])
        GP = [ps(f"GP{s}", [P, D_EXP]) for s in range(2)]
        UP = ps("UP", [P, D_EXP])
        TA = ps("TA", [P, D_EXP])
        YP = ps("YP", [P, D])
        x_loaded = [sem(f"e_x_loaded{s}") for s in range(2)]
        y_stored = [sem(f"e_y_stored{s}") for s in range(2)]
        (copied, x_turned, x_out_a, x_out_d, gate_done, gu_done, exped, step, a_turned, a_out, down_done, y_out) = (
            sem(f"e_{n}") for n in ("copied", "x_turned", "x_out_a", "x_out_d", "gate_done", "gu_done", "exped",
                                    "step", "a_turned", "a_out", "down_done", "y_out"))
        block = ctx.enter_context(nc.Block())

        def over_overflow(eng, body):
            used = eng.value_load(overflow[0:1, 0:1], min_val=0, max_val=N_OVF)
            with eng.Fori(0, (N_OVF + 1) // 2) as j:
                for s in range(2):
                    with eng.If(used > j * 2 + s):
                        body(j * 2 + (N_EXP + s), s, j + N_EXP // 2)

        @block.sync
        def _(sp):
            def gate_up(e, b, s):
                sp.wait_ge(gu_done, b + 1)
                w.load_gate_up(sp, d, e, s)

            def down(e, b, s):
                sp.wait_ge(down_done, b + 1)
                w.load_down(sp, d, e, s)

            with sp.Fori(0, N_EXP // 2 - 1) as r:
                for s in range(2):
                    b = r * 2 + s
                    gate_up(b + 1, b + 1, 1 - s)
                    down(b, b, s)
            gate_up(N_EXP - 1, N_EXP - 1, 1)
            down(N_EXP - 2, N_EXP - 2, 0)
            down(N_EXP - 1, N_EXP - 1, 1)

            def more(b, s, r):
                e = sp.value_load(overflow[0:1, bass.ds(b - (N_EXP - 1), 1)], min_val=0, max_val=N_EXP - 1)
                gate_up(e, b, s)
                down(e, b, s)

            over_overflow(sp, more)

        @block.gpsimd
        def _(pool):
            count = pool.alloc_register("e_count")

            def gather(b, s, r):
                pool.reg_mov(count, b + 1)
                pool.wait_ge(x_turned, count)
                pool.tensor_copy(idx[s][:, :], ids[:, bass.ds(b, 1)]).then_inc(copied, 1)
                pool.reg_mov(count, b + 1)
                pool.wait_ge(x_turned, 1)
                pool.wait_ge(copied, count)
                pool.indirect_dma_start(out=xb[s][:, :], out_offset=None, in_=h2_dram,
                                        in_offset=bass.IndirectOffsetOnAxis(ap=idx[s][:, :], axis=0)
                                        ).then_inc(x_loaded[s], 16)

            with pool.Fori(0, N_EXP // 2) as r:
                gather(r * 2, 0, r)
                gather(r * 2 + 1, 1, r)
            over_overflow(pool, gather)

        @block.tensor
        def _(pe):
            def turn_x(b, s, r):
                pe.wait_ge(x_loaded[s], r * 16 + 16)
                pe.wait_ge(x_out_a, b + 1)
                pe.wait_ge(x_out_d, b + 1)
                for k in range(ND):
                    last = pe.transpose(TX[:, k * P:(k + 1) * P], xb[s][:, k * P:(k + 1) * P], g.ident[:, :])
                last.then_inc(x_turned, 1)

            def gate_up(b, s, r):
                pe.wait_ge(w.gu_loaded[s], r * 32 + 32)
                pe.wait_ge(x_out_a, b + 2)
                pe.wait_ge(x_out_d, b + 2)
                pe.wait_ge(step, b * 4 + 4)
                for k in range(ND):
                    last = pe.matmul(GP[s][:, :], xT[s][:, k, :], w.gate[s][:, k, :], start=(k == 0), stop=(k == ND - 1))
                last.then_inc(gate_done, 1)
                pe.wait_ge(step, b * 4 + 8)
                for k in range(ND):
                    last = pe.matmul(UP[:, :], xT[s][:, k, :], w.up[s][:, k, :], start=(k == 0), stop=(k == ND - 1))
                last.then_inc(gu_done, 1)

            def turn_product(b):
                pe.wait_ge(step, b * 4 + 12)
                pe.wait_ge(a_out, b + 1)
                for k in range(KD):
                    last = pe.transpose(TA[:, k * P:(k + 1) * P], prod[:, k * P:(k + 1) * P], g.ident[:, :])
                last.then_inc(a_turned, 1)

            def down(b, s, r):
                pe.wait_ge(a_out, b + 2)
                pe.wait_ge(w.d_loaded[s], r * 16 + 16)
                pe.wait_ge(y_out, b + 1)
                for half in range(2):
                    cols = slice(half * 512, (half + 1) * 512)
                    for k in range(KD):
                        last = pe.matmul(YP[:, cols], aT[:, k, :], w.down[s][:, k, cols], start=(k == 0), stop=(k == KD - 1))
                last.then_inc(down_done, 1)

            pe.sem_inc(gu_done, 2)
            pe.sem_inc(down_done, 2)
            pe.sem_inc(x_turned, 2)
            turn_x(0, 0, 0)
            gate_up(0, 0, 0)
            turn_x(1, 1, 0)

            def round_(b, s, r, next_x=True):
                gate_up(b, s, r)
                turn_product(b - 1)
                if next_x:
                    turn_x(b + 1, 1 - s, r + s)
                down(b - 1, 1 - s, r - (1 - s))

            with pe.Fori(0, N_EXP // 2 - 1) as r:
                round_(r * 2 + 1, 1, r)
                round_(r * 2 + 2, 0, r + 1)
            round_(N_EXP - 1, 1, N_EXP // 2 - 1, next_x=False)
            turn_product(N_EXP - 1)
            down(N_EXP - 1, 1, N_EXP // 2 - 1)

            def more(b, s, r):
                turn_x(b, s, r)
                gate_up(b, s, r)
                turn_product(b)
                down(b, s, r)

            over_overflow(pe, more)

        @block.scalar
        def _(act):
            def x_out(b, s):
                act.wait_ge(x_turned, b + 3)
                act.wait_ge(gu_done, b + 1)
                act.activation(xT[s][:, 0:4, :], TX[:, 0:512].rearrange("p (k t) -> p k t", t=P), ACT.Copy
                               ).then_inc(x_out_a, 1)

            def exp(b, s):
                act.wait_ge(gate_done, b + 1)
                act.wait_ge(step, b * 4 + 8)
                act.activation(sig[:, :], GP[s][:, :], ACT.Exp, scale=-1.0).then_inc(exped, 1)

            def store(b, s, r):
                act.wait_ge(down_done, b + 3)
                act.wait_ge(y_stored[s], r * 16 + 16)
                act.activation(y[s][:, :], YP[:, :], ACT.Copy).then_inc(y_out, 1)
                act.wait_ge(y_out, b + 2)
                act.dma_start(y_dram[bass.ds(b * P, P), :], y[s][:, :]).then_inc(y_stored[s], 16)

            for s in range(2):
                act.sem_inc(y_stored[s], 16)
            act.sem_inc(x_out_a, 1)
            act.sem_inc(y_out, 1)
            x_out(0, 0)
            exp(0, 0)
            x_out(1, 1)

            def round_(b, s, r, next_x=True):
                exp(b, s)
                if next_x:
                    x_out(b + 1, 1 - s)
                store(b - 1, 1 - s, r - (1 - s))

            with act.Fori(0, N_EXP // 2 - 1) as r:
                round_(r * 2 + 1, 1, r)
                round_(r * 2 + 2, 0, r + 1)
            round_(N_EXP - 1, 1, N_EXP // 2 - 1, next_x=False)
            store(N_EXP - 1, 1, N_EXP // 2 - 1)

            def more(b, s, r):
                x_out(b, s)
                exp(b, s)
                store(b, s, r)
                act.wait_ge(y_stored[s], r * 16 + 32)
                act.wait_ge(carried, b - (N_EXP - 1))
                act.activation(spare[:, :], g.eps[:, :], ACT.Copy).then_inc(carried, 1)

            act.sem_inc(carried, 1)
            over_overflow(act, more)
            for s in range(2):
                act.wait_ge(y_stored[s], (N_EXP // 2 + 1) * 16)

        @block.vector
        def _(dve):
            def x_out(b, s):
                dve.wait_ge(x_turned, b + 3)
                dve.wait_ge(gu_done, b + 1)
                dve.tensor_copy(xT[s][:, 4:8, :], TX[:, 512:D].rearrange("p (k t) -> p k t", t=P)).then_inc(x_out_d, 1)

            def sigmoid(b):
                dve.wait_ge(exped, b + 1)
                chain = Chain(dve, step, b * 4 + 8)
                chain.link(dve.tensor_scalar_add(sig[:, :], sig[:, :], 1.0))
                chain.link(dve.reciprocal(sig[:, :], sig[:, :]))

            def multiply(b, s):
                dve.wait_ge(gu_done, b + 3)
                dve.wait_ge(a_turned, b + 1)
                chain = Chain(dve, step, b * 4 + 10)
                chain.link(dve.tensor_tensor(prod[:, :], sig[:, :], GP[s][:, :], ALU.mult))
                chain.link(dve.tensor_tensor(prod[:, :], prod[:, :], UP[:, :], ALU.mult))

            def product_out(b):
                dve.wait_ge(a_turned, b + 2)
                dve.wait_ge(down_done, b + 2)
                dve.tensor_copy(aT[:, :, :], TA[:, :].rearrange("p (k t) -> p k t", t=P)).then_inc(a_out, 1)

            dve.sem_inc(x_out_d, 1)
            dve.sem_inc(step, 8)
            dve.sem_inc(a_out, 1)
            dve.sem_inc(a_turned, 1)
            x_out(0, 0)
            sigmoid(0)
            x_out(1, 1)
            multiply(0, 0)

            def round_(b, s, r, next_x=True):
                sigmoid(b)
                product_out(b - 1)
                if next_x:
                    x_out(b + 1, 1 - s)
                multiply(b, s)

            with dve.Fori(0, N_EXP // 2 - 1) as r:
                round_(r * 2 + 1, 1, r)
                round_(r * 2 + 2, 0, r + 1)
            round_(N_EXP - 1, 1, N_EXP // 2 - 1, next_x=False)
            product_out(N_EXP - 1)

            def more(b, s, r):
                x_out(b, s)
                sigmoid(b)
                multiply(b, s)
                product_out(b)

            over_overflow(dve, more)


def combine(nc, g, d, rows, weights, x1, mod, y_dram, out):
    GT_F = slice(3 * D, 4 * D)
    with ExitStack() as ctx:
        sb, ps, sem = allocator(nc, ctx)
        idx = [[sb(f"c_idx{s}{k}", [P, 1], U32) for k in range(2)] for s in range(2)]
        yk = [[sb(f"c_y{s}{k}", [P, D]) for k in range(2)] for s in range(2)]
        wk = [sb(f"c_w{s}", [P, 2]) for s in range(2)]
        total = [sb(f"c_sum{s}", [P, D]) for s in range(2)]
        ms = [sb(f"c_ms{s}", [P, 1]) for s in range(2)]
        rstd = [sb(f"c_rstd{s}", [P, 1]) for s in range(2)]
        junk = sb("c_junk", [P, D])
        loaded = [sem(f"c_loaded{s}") for s in range(2)]
        stored = [sem(f"c_stored{s}") for s in range(2)]
        copied, step, astep, weighed = (sem(f"c_{n}") for n in ("copied", "step", "astep", "weighed"))
        D_STEPS, CREDIT = 5, 10
        block = ctx.enter_context(nc.Block())

        @block.gpsimd
        def _(pool):
            count = pool.alloc_register("c_count")
            with pool.Fori(0, NT // 2) as r:
                for s in range(2):
                    i = r * 2 + s
                    pool.reg_mov(count, i * D_STEPS + 2)
                    pool.wait_ge(step, count)
                    pool.tensor_copy(wk[s][:, :], weights[:, :, bass.ds(i, 1)].rearrange("p k a -> p (k a)")
                                     ).then_inc(weighed, 1)
                    for k in range(2):
                        pool.tensor_copy(idx[s][k][:, :], rows[:, k, bass.ds(i, 1)]).then_inc(copied, 1)
                    pool.reg_mov(count, i * 2 + 2)
                    for k in range(2):
                        pool.wait_ge(step, CREDIT)
                        pool.wait_ge(copied, count)
                        pool.indirect_dma_start(out=yk[s][k][:, :], out_offset=None, in_=y_dram,
                                                in_offset=bass.IndirectOffsetOnAxis(ap=idx[s][k][:, :], axis=0)
                                                ).then_inc(loaded[s], 16)

        @block.vector
        def _(dve):
            dve.sem_inc(step, CREDIT)
            with dve.Fori(0, NT // 2) as r:
                for s in range(2):
                    i = r * 2 + s
                    chain = Chain(dve, step, i * D_STEPS + CREDIT)
                    dve.wait_ge(loaded[s], r * 32 + 32)
                    dve.wait_ge(weighed, i + 1)
                    dve.wait_ge(stored[s], r * 16 + 16)
                    chain.link(dve.tensor_scalar(total[s][:, :], yk[s][0][:, :], wk[s][:, 0:1], None, ALU.mult))
                    chain.link(dve.scalar_tensor_tensor(out=total[s][:, :], in0=yk[s][1][:, :], scalar=wk[s][:, 1:2],
                                                        in1=total[s][:, :], op0=ALU.mult, op1=ALU.add))
                    dve.wait_ge(astep, i * 2 + 2)
                    chain.link(dve.reciprocal(rstd[s][:, :], ms[s][:, :]))
                    chain.link(dve.scalar_tensor_tensor(out=total[s][:, :], in0=total[s][:, :], scalar=rstd[s][:, :],
                                                        in1=mod[:, GT_F], op0=ALU.mult, op1=ALU.mult))
                    chain.link(dve.tensor_tensor(total[s][:, :], total[s][:, :],
                                                 x1[:, bass.ds(i, 1), :].rearrange("p a n -> p (a n)"), ALU.add))

        @block.scalar
        def _(act):
            with act.Fori(0, NT // 2) as r:
                for s in range(2):
                    i = r * 2 + s
                    chain = Chain(act, astep, i * 2)
                    act.wait_ge(step, i * D_STEPS + (CREDIT + 2))
                    chain.link(act.activation(junk[:, :], total[s][:, :], ACT.Square, scale=D ** -0.5, accum_out=ms[s][:, :]))
                    chain.link(act.activation(ms[s][:, :], ms[s][:, :], ACT.Sqrt, bias=g.eps[:, :]))

        @block.sync
        def _(sp):
            for s in range(2):
                sp.sem_inc(stored[s], 16)
            with sp.Fori(0, NT // 2) as r:
                for s in range(2):
                    i = r * 2 + s
                    sp.wait_ge(step, i * D_STEPS + (CREDIT + 5))
                    sp.dma_start(out[0, bass.ds(i * P, P), :], total[s][:, :]).then_inc(stored[s], 16)
            for s in range(2):
                sp.wait_ge(stored[s], (NT // 2 + 1) * 16)


def decoder_block(nc, d, out):
    fsum_dram = nc.dram_tensor("fsum", [FOX_HEADS, S], F32).ap()
    h2_dram = nc.dram_tensor("h2_rows", [S, D], F32).ap()
    y_dram = nc.dram_tensor("expert_rows", [N_COL * P, D], F32).ap()
    with ExitStack() as ctx:
        sb, _, sem = allocator(nc, ctx)
        g = Constants(sb)
        room = sb("room", [P, ND * S])
        mixT = room[:, :].rearrange("p (k t) -> p k t", t=S)
        constants(nc, g, d)
        with ExitStack() as mixers:
            msb, _, _ = allocator(nc, mixers)
            hT = msb("hT", [P, ND, S])
            yaT, ybT = msb("yaT", [P, NSA_HEADS * HD // P, S]), msb("ybT", [P, FOX_HEADS * HD // P, S])
            gates = msb("gates", [P, NT, 3 * NSA_HEADS])
            with ExitStack() as first:
                mod = allocator(nc, first)[0]("mod_mix", [P, 2 * D])
                modulation(nc, g, d, 0, 4, mod)
                normalise_input(nc, g, d, mod, hT)
            gates_and_forget(nc, g, d, hT, gates, fsum_dram)
            fox(nc, g, d, hT, ybT, fsum_dram, y_dram)
            nsa(nc, g, d, hT, yaT, gates, room)
            mod = sb("mod_ffn", [P, 4 * D], side="right")
            late = ctx.enter_context(ExitStack())
            w_out = allocator(nc, late)[0]("w_out_sb", [P, ND, D], side="right")
            w_out_loaded = sem("w_out_loaded")
            merge(nc, g, d, hT, yaT, ybT, mixT, mod, w_out, w_out_loaded)
        x1 = sb("x1", [P, NT, D])
        expert_weights = ExpertWeights(sb, sem, room)
        logits = sb("logits", [P, NT, N_GRP + N_EXP])
        rows, weights = sb("rows", [P, 2, NT], U32), sb("weights", [P, 2, NT])
        ids = sb("ids", [P, N_COL], U32)
        overflow = sb("overflow", [P, 2 + N_OVF], I32)
        project_out(nc, g, d, mixT, mod, w_out, w_out_loaded, x1, logits, h2_dram, expert_weights)
        late.close()
        route(nc, g, logits, rows, weights, ids, overflow)
        experts(nc, g, d, expert_weights, ids, overflow, h2_dram, y_dram)
        combine(nc, g, d, rows, weights, x1, mod, y_dram, out)


_INS = ['x', 'c', 'w_ada', 'b_ada', 'g_pre_mix', 'g_post_mix', 'g_pre_ffn', 'g_post_ffn', 'w_in', 'b_forget',
        'cmp_pe_k', 'cmp_w1_k', 'cmp_w2_k', 'cmp_pe_v', 'cmp_w1_v', 'cmp_w2_v', 'w_o_nsa', 'w_o_fox', 'w_out',
        'w_router_group', 'b_router_group', 'w_router_expert', 'b_router_expert',
        'w_exp_gate', 'w_exp_up', 'w_exp_down']


def kernel(**inputs):
    import numpy as _np
    import concourse.bacc as _bacc
    from concourse import mybir as _mybir
    from concourse.bass_utils import run_bass_kernel_spmd as _run

    nc = _bacc.Bacc("TRN2", target_bir_lowering=False, num_devices=1)
    arrays, d = {}, {}
    for name in _INS:
        a = _np.ascontiguousarray(inputs[name])
        arrays[f"in_{name}_dram"] = a
        d[name] = nc.dram_tensor(f"in_{name}_dram", a.shape, _mybir.dt.from_np(a.dtype),
                                          kind="ExternalInput").ap()
    out = nc.dram_tensor("out_0_dram", (1, S, D), F32, kind="ExternalOutput").ap()
    decoder_block(nc, d, out)
    r = _run(nc, [arrays], core_ids=[0])
    return r.results[0]["out_0_dram"]
```

```python
from contextlib import ExitStack

import concourse.bass as bass
from concourse import mybir

ALU = mybir.AluOpType
ACT = mybir.ActivationFunctionType
AX = mybir.AxisListType
F32 = mybir.dt.float32
F32R = mybir.dt.float32r
I32 = mybir.dt.int32
U32 = mybir.dt.uint32

P = 128
S = 1024
D = 1024
NT = S // P
ND = D // P
HD = 64
NSA_HEADS, NSA_GROUPS, FOX_HEADS = 8, 2, 8
CMP_LEN, CMP_STRIDE = 32, 16
N_CMP = (S - CMP_LEN) // CMP_STRIDE + 1
WINDOW = 512
EPS = 1e-6
BIG = 1e30
N_GRP, PER_GRP = 4, 8
N_EXP = N_GRP * PER_GRP
D_EXP = D // 2
NEG_SCALE = -(HD ** -0.5)

C_QA = 0
C_KCMP, C_VCMP, C_KSLC, C_VSLC, C_KWIN, C_VWIN = (512 + 128 * i for i in range(6))
C_GL = 1280
C_QB, C_KB, C_VB = 1304, 1816, 2328
C_F = 2840
C_MG = 2848

N_OVF = 2 * S // (P + 1)
N_COL = N_EXP + N_OVF + 1


class Chain:

    def __init__(self, eng, sem, base=0):
        self.eng, self.sem, self.base, self.n = eng, sem, base, 0

    def link(self, instruction):
        instruction.then_inc(self.sem, 1)
        self.n += 1
        self.eng.wait_ge(self.sem, self.base + self.n)


def over_tiles(eng, first, tile, slots=2):
    first(0, 0, 0)
    with eng.Fori(0, NT // slots - 1) as r:
        for s in range(slots):
            first(r * slots + (s + 1), (s + 1) % slots, r + (s + 1) // slots)
            tile(r * slots + s, s, r)
    for s in range(slots):
        i = NT - slots + s
        if s + 1 < slots:
            first(i + 1, s + 1, NT // slots - 1)
        tile(i, s, NT // slots - 1)


def allocator(nc, ctx):
    def sb(name, shape, dt=F32, side="left"):
        return ctx.enter_context(nc.sbuf_tensor(name, shape, dt, side=side))

    def ps(name, shape, dt=F32):
        return ctx.enter_context(nc.psum_tensor(name, shape, dt))

    def sem(name):
        return ctx.enter_context(nc.semaphore(name))

    return sb, ps, sem



class Constants:
    def __init__(self, sb):
        self.ident, self.ident_r = sb("ident", [P, P]), sb("ident_r", [P, P], F32R)
        self.ones, self.eps = sb("ones", [P, P]), sb("eps", [P, 1])
        self.csilu = sb("csilu", [P, ND])


def constants(nc, g, d):
    with ExitStack() as ctx:
        sb, ps, sem = allocator(nc, ctx)
        crow = sb("crow", [ND, P])
        ccol = sb("ccol", [P, ND])
        cexp = sb("cexp", [P, ND])
        cden = sb("cden", [P, ND])
        cps = ps("cps", [P, ND])
        loaded, made, turned, copied, exped, step = (
            sem(n) for n in ("c_loaded", "c_made", "c_turned", "c_copied", "c_exped", "c_step"))
        block = ctx.enter_context(nc.Block())

        @block.sync
        def _(sp):
            sp.dma_start(crow[:, :], d["c"].rearrange("a (k p) -> (a k) p", p=P)).then_inc(loaded, 16)

        @block.gpsimd
        def _(pool):
            pool.memset(g.ident[:, :], 0.0).then_inc(step, 1)
            pool.memset(g.ones[:, :], 1.0).then_inc(step, 1)
            pool.memset(g.eps[:, :], EPS).then_inc(step, 1)
            pool.wait_ge(step, 3)
            pool.affine_select(out=g.ident[:, :], in_=g.ident[:, :], compare_op=ALU.not_equal, fill=1.0,
                               base=0, pattern=[[-1, P]], channel_multiplier=1).then_inc(made, 1)

        @block.tensor
        def _(pe):
            pe.wait_ge(loaded, 16)
            pe.wait_ge(made, 1)
            pe.transpose(cps[:, :], crow[:, :], g.ident[0:ND, 0:ND]).then_inc(turned, 1)

        @block.scalar
        def _(act):
            act.wait_ge(turned, 1)
            act.activation(cexp[:, :], cps[:, :], ACT.Exp, scale=-1.0).then_inc(exped, 1)

        @block.vector
        def _(dve):
            dve.wait_ge(exped, 1)
            chain = Chain(dve, copied)
            chain.link(dve.tensor_copy(ccol[:, :], cps[:, :]))
            chain.link(dve.tensor_scalar_add(cden[:, :], cexp[:, :], 1.0))
            chain.link(dve.reciprocal(cexp[:, :], cden[:, :]))
            dve.tensor_tensor(g.csilu[:, :], ccol[:, :], cexp[:, :], ALU.mult).then_inc(copied, 1)


class Early:

    def __init__(self, sb, sem):
        self.w_small = sb("w_small", [P, ND, 3 * NSA_HEADS + FOX_HEADS], side="right")
        self.b_forget = sb("b_forget_all", [P, FOX_HEADS], side="right")
        self.w1 = sb("cmp_w1", [P, CMP_LEN, P], side="right")
        self.w2 = sb("cmp_w2", [P, P], side="right")
        self.pe_rows = sb("pe_rows", [CMP_LEN, P], side="right")
        self.pec = sb("cmp_pec", [P, 1], side="right")
        self.small_loaded, self.cmp_loaded, self.cleared = sem("small_loaded"), sem("cmp_loaded"), sem("cmp_cleared")

    def load(self, eng, d):
        NG = 3 * NSA_HEADS
        for part, c, n in ((slice(0, NG), C_GL, NG), (slice(NG, NG + FOX_HEADS), C_F, FOX_HEADS)):
            eng.dma_start(self.w_small[:, :, part], d["w_in"][0, :, c:c + n].rearrange("(k p) n -> p k n", p=P)
                          ).then_inc(self.small_loaded, 16)
        eng.dma_start(self.b_forget[:, :], d["b_forget"][0:1, :].to_broadcast([P, FOX_HEADS])
                      ).then_inc(self.small_loaded, 16)
        for part, x, y, z in ((LOW, d["cmp_w1_k"], d["cmp_w2_k"], d["cmp_pe_k"]),
                              (HIGH, d["cmp_w1_v"], d["cmp_w2_v"], d["cmp_pe_v"])):
            eng.dma_start(self.w1[part, :, part], x[0].rearrange("l d e -> d l e")).then_inc(self.cmp_loaded, 16)
            eng.dma_start(self.w2[part, part], y[0]).then_inc(self.cmp_loaded, 16)
            eng.dma_start(self.pe_rows[:, part], z[0]).then_inc(self.cmp_loaded, 16)

    def clear(self, pool):
        for w in (self.w1[LOW, :, HIGH], self.w1[HIGH, :, LOW], self.w2[LOW, HIGH], self.w2[HIGH, LOW]):
            pool.memset(w, 0.0).then_inc(self.cleared, 1)



def normalise_input(nc, g, d, hT, early, room):
    W = 512
    CHUNKS = 2 * D // W
    with ExitStack() as ctx:
        sb, ps, sem = allocator(nc, ctx)
        wada = [sb(f"wada{n}", [P, ND, W]) for n in range(2)] + [hT[:, :, n * W:(n + 1) * W] for n in range(2)]
        bias = sb("bada", [P, 2 * D])
        part = [sb(f"mpart{s}", [P, W]) for s in range(2)]
        mod = sb("mod_mix", [P, 2 * D])
        gain = sb("gain_pre", [P, D])
        scale = sb("scale_mix", [P, D])
        x = room[:, :].rearrange("p (t n) -> p t n", n=D)
        h = [sb(f"ht{s}", [P, D]) for s in range(4)]
        junk = sb("junk", [P, D])
        ms = sb("ms", [P, NT])
        rstd = sb("rstd", [P, NT])
        rstd_i = [sb(f"rstd_i{s}", [P, 1]) for s in range(2)]
        total = [ps(f"mtotal{s}", [P, W]) for s in range(2)]
        tps = [[ps(f"tps{s}{b}", [P, 512]) for b in range(2)] for s in range(2)]
        loaded = [sem(f"m_loaded{n}") for n in range(CHUNKS)]
        x_loaded = [sem(f"n_x_loaded{s}") for s in range(2)]
        step, summed, summed_up = (sem(n) for n in ("m_step", "m_summed", "m_summed_up"))
        vectors, squared, rooted, pstep, scaled, shifted_p, shifted_d, turned, copied = (
            sem(n) for n in ("n_vectors", "n_squared", "n_rooted", "n_pstep", "n_scaled", "n_shifted_p",
                             "n_shifted_d", "n_turned", "n_copied"))
        block = ctx.enter_context(nc.Block())

        @block.sync
        def _(sp):
            for n in range(CHUNKS):
                sp.dma_start(wada[n][:, :, :], d["w_ada"][0, :, n * W:(n + 1) * W]
                             .rearrange("(k p) n -> p k n", p=P)).then_inc(loaded[n], 16)
            early.load(sp, d)

        @block.scalar
        def _(act):
            act.dma_start(bias[:, :], d["b_ada"][0:1, 0:2 * D].to_broadcast([P, 2 * D])).then_inc(vectors, 16)
            act.dma_start(gain[:, :], d["g_pre_mix"][0:1, :].to_broadcast([P, D])).then_inc(vectors, 16)
            for half in range(2):
                t = slice(half * NT // 2, (half + 1) * NT // 2)
                act.dma_start(x[:, t, :], d["x"][0].rearrange("(t p) n -> p t n", p=P)[:, t, :]
                              ).then_inc(x_loaded[half], 16)
            act.sem_inc(squared, 1)
            for half in range(2):
                act.wait_ge(x_loaded[half], 16)
                with act.Fori(0, NT // 2) as t:
                    i = t + half * NT // 2
                    act.wait_ge(squared, i + 1)
                    act.activation(junk[:, :], x[:, bass.ds(i, 1), :].rearrange("p a n -> p (a n)"), ACT.Square,
                                   scale=D ** -0.5, accum_out=ms[:, bass.ds(i, 1)]).then_inc(squared, 1)
            act.wait_ge(squared, NT + 1)
            act.activation(ms[:, :], ms[:, :], ACT.Sqrt, bias=g.eps[:, :]).then_inc(rooted, 1)
            with act.Fori(0, NT // 2) as r:
                for s in range(2):
                    i = r * 2 + s
                    act.wait_ge(turned, i + 5)
                    for b in range(2):
                        act.activation(hT[:, 4 * b:4 * b + 4, bass.ds(i * P, P)],
                                       tps[s][b][:, :].rearrange("p (k t) -> p k t", t=P), ACT.Copy).then_inc(copied, 1)

        @block.gpsimd
        def _(pool):
            early.clear(pool)
            pool.wait_ge(early.cleared, 4)
            with pool.Fori(0, NT // 4) as r:
                for s in (0, 2):
                    pool.wait_ge(scaled, r * 4 + s + 3)
                    pool.tensor_tensor(h[s][:, :], h[s][:, :], mod[:, 0:D], ALU.add).then_inc(shifted_p, 1)

        @block.vector
        def _(dve):
            def add_bias(n):
                dve.wait_ge(summed, n + 1)
                dve.tensor_tensor(mod[:, n * W:(n + 1) * W], total[n % 2][:, :], bias[:, n * W:(n + 1) * W], ALU.add
                                  ).then_inc(summed_up, 1)

            dve.wait_ge(vectors, 32)
            chain = Chain(dve, step)
            for n in range(CHUNKS):
                dve.wait_ge(loaded[n], 16)
                if n >= 2:
                    dve.wait_ge(summed, n - 1)
                out = part[n % 2][:, :]
                chain.link(dve.tensor_scalar(out, wada[n][:, 0, :], g.csilu[:, 0:1], None, ALU.mult))
                for k in range(1, ND):
                    chain.link(dve.scalar_tensor_tensor(out=out, in0=wada[n][:, k, :], scalar=g.csilu[:, k:k + 1],
                                                        in1=out, op0=ALU.mult, op1=ALU.add))
                if n >= 1:
                    add_bias(n - 1)
            dve.wait_ge(rooted, 1)
            dve.reciprocal(rstd[:, :], ms[:, :]).then_inc(scaled, 1)
            add_bias(CHUNKS - 1)
            dve.wait_ge(summed_up, CHUNKS)
            dve.scalar_tensor_tensor(out=scale[:, :], in0=mod[:, D:2 * D], scalar=1.0, in1=gain[:, :],
                                     op0=ALU.add, op1=ALU.mult).then_inc(scaled, 1)
            dve.wait_ge(scaled, 2)
            with dve.Fori(0, NT // 4) as r:
                for s in range(4):
                    i = r * 4 + s
                    dve.wait_ge(scaled, i + 1)
                    dve.tensor_copy(rstd_i[s % 2][:, :], rstd[:, bass.ds(i, 1)]).then_inc(pstep, 1)
                    dve.wait_ge(pstep, i + 1)
                    dve.wait_ge(turned, i + 1)
                    dve.scalar_tensor_tensor(out=h[s][:, :], in0=x[:, bass.ds(i, 1), :].rearrange("p a n -> p (a n)"),
                                             scalar=rstd_i[s % 2][:, :], in1=scale[:, :],
                                             op0=ALU.mult, op1=ALU.mult).then_inc(scaled, 1)
                    if s % 2 == 1:
                        dve.wait_ge(scaled, i + 3)
                        dve.tensor_tensor(h[s][:, :], h[s][:, :], mod[:, 0:D], ALU.add).then_inc(shifted_d, 1)

        @block.tensor
        def _(pe):
            pe.sem_inc(turned, 4)
            pe.sem_inc(copied, 4)
            for n in range(CHUNKS):
                pe.wait_ge(step, (n + 1) * ND)
                if n >= 2:
                    pe.wait_ge(summed_up, n - 1)
                pe.matmul(total[n % 2][:, :], g.ones[:, :], part[n % 2][:, :], start=True, stop=True).then_inc(summed, 1)
            with pe.Fori(0, NT // 4) as r:
                for s in range(4):
                    i = r * 4 + s
                    pe.wait_ge((shifted_p, shifted_d)[s % 2], r * 2 + s // 2 + 1)
                    pe.wait_ge(copied, i * 2 + 2)
                    for k in range(ND):
                        last = pe.transpose(tps[s % 2][k // 4][:, (k % 4) * P:(k % 4 + 1) * P],
                                            h[s][:, k * P:(k + 1) * P], g.ident[:, :])
                    last.then_inc(turned, 1)



def gates_and_forget(nc, g, d, w_mix, hT, early, gates, fsum_dram):
    NG = 3 * NSA_HEADS
    with ExitStack() as ctx:
        sb, ps, sem = allocator(nc, ctx)
        w, bf, loaded = early.w_small, early.b_forget, early.small_loaded
        LEVELS = CMP_LEN.bit_length() - 1
        added = sb("cmp_pe_added", [P, CMP_LEN, P])
        pe_cols = sb("pe_cols", [P, CMP_LEN])
        pe_ps = ps("pe_ps", [P, CMP_LEN])
        pec_ps = ps("pec_ps", [P, 1])
        cmp_step = sem("n_cmp_step")
        turned_logits = sb("turned_logits", [NG + FOX_HEADS, S])
        tl = [ps(f"tl{b}", [NG + FOX_HEADS, 512]) for b in range(2)]
        zero = sb("zero_f", [FOX_HEADS, S])
        f = sb("f_logit", [P, NT, FOX_HEADS])
        fneg = sb("f_neg", [P, NT, FOX_HEADS])
        fln = sb("f_ln", [P, NT, FOX_HEADS])
        gexp = sb("gate_exp", [P, NT, NG])
        fT = sb("f_turned", [FOX_HEADS, S])
        valid = sb("cmp_valid", [P, 1])
        logits = ps("small_logits", [P, NT, NG + FOX_HEADS])
        fps = [ps(f"fps{b}", [FOX_HEADS, 512]) for b in range(2)]
        projected, copied, made, multiplied, aexp, step, turned, stored = (
            sem(n) for n in ("g_projected", "g_copied", "g_made", "g_multiplied", "g_exp", "g_step", "g_turned", "g_stored"))
        block = ctx.enter_context(nc.Block())

        @block.sync
        def _(sp):
            w_mix.load_fox(sp, d, 0)
            sp.wait_ge(step, 9)
            sp.dma_start(fsum_dram, fT[:, :]).then_inc(stored, 16)
            sp.wait_ge(stored, 16)

        @block.gpsimd
        def _(pool):
            pool.memset(valid[:, :], 1.0).then_inc(made, 1)
            pool.memset(zero[:, :], 0.0).then_inc(made, 1)
            pool.wait_ge(made, 2)
            pool.affine_select(out=valid[:, :], in_=valid[:, :], compare_op=ALU.is_ge, fill=0.0,
                               base=-(CMP_LEN - 1), pattern=[[0, 1]], channel_multiplier=1).then_inc(made, 1)

        @block.tensor
        def _(pe):
            pe.wait_ge(loaded, 48)
            pe.wait_ge(early.cmp_loaded, 96)
            pe.transpose(pe_ps[:, :], early.pe_rows[:, :], g.ident[0:CMP_LEN, 0:CMP_LEN]).then_inc(cmp_step, 1)
            for half in range(2):
                for k in range(ND):
                    last = pe.matmul(tl[half][:, :], w[:, k, :], hT[:, k, half * 512:(half + 1) * 512],
                                     start=(k == 0), stop=(k == ND - 1))
                last.then_inc(projected, 1)
            pe.wait_ge(copied, 2)
            for i in range(NT):
                last = pe.transpose(logits[:, i, :], turned_logits[:, i * P:(i + 1) * P],
                                    g.ident[0:NG + FOX_HEADS, 0:NG + FOX_HEADS])
            last.then_inc(multiplied, 1)
            pe.wait_ge(step, 7)
            for i in range(NT):
                last = pe.transpose(fps[i // 4][:, (i % 4) * P:(i % 4 + 1) * P], fln[:, i, :], g.ident[:, :])
            last.then_inc(turned, 1)
            pe.wait_ge(cmp_step, 3 + LEVELS)
            pe.matmul(pec_ps[:, :], added[:, 0, :], g.ones[:, 0:1], start=True, stop=True).then_inc(cmp_step, 1)

        @block.scalar
        def _(act):
            act.wait_ge(cmp_step, 1)
            act.activation(pe_cols[:, :], pe_ps[:, :], ACT.Copy).then_inc(cmp_step, 1)
            for half in range(2):
                act.wait_ge(projected, half + 1)
                act.activation(turned_logits[:, half * 512:(half + 1) * 512], tl[half][:, :], ACT.Copy).then_inc(copied, 1)
            act.wait_ge(multiplied, 1)
            act.activation(gexp[:, :, :], logits[:, :, 0:NG], ACT.Exp, scale=-1.0).then_inc(aexp, 1)
            act.wait_ge(step, 3)
            act.activation(fln[:, :, :], fneg[:, :, :], ACT.Exp).then_inc(aexp, 1)
            act.wait_ge(aexp, 2)
            act.activation(fln[:, :, :], fln[:, :, :], ACT.Ln, bias=1.0).then_inc(aexp, 1)
            act.wait_ge(cmp_step, 4 + LEVELS)
            act.activation(early.pec[:, :], pec_ps[:, :], ACT.Copy).then_inc(cmp_step, 1)

        @block.vector
        def _(dve):
            dve.wait_ge(cmp_step, 2)
            dve.wait_ge(early.cleared, 4)
            chain = Chain(dve, cmp_step, 2)
            chain.link(dve.tensor_tensor(added[:, :, :], early.w1[:, :, :],
                                         pe_cols[:, :].unsqueeze(2).to_broadcast([P, CMP_LEN, P]), ALU.mult))
            for level in range(LEVELS):
                n = CMP_LEN >> (level + 1)
                chain.link(dve.tensor_tensor(added[:, 0:n, :], added[:, 0:n, :], added[:, n:2 * n, :], ALU.add))
            dve.wait_ge(loaded, 48)
            dve.wait_ge(aexp, 1)
            chain = Chain(dve, step)
            chain.link(dve.tensor_tensor(f[:, :, :], logits[:, :, NG:],
                                         bf[:, :].unsqueeze(1).to_broadcast([P, NT, FOX_HEADS]), ALU.add))
            chain.link(dve.tensor_scalar(fneg[:, :, :], f[:, :, :], -1.0, None, ALU.mult))
            chain.link(dve.tensor_tensor(fneg[:, :, :], f[:, :, :], fneg[:, :, :], ALU.min))
            chain.link(dve.tensor_scalar_add(gexp[:, :, :], gexp[:, :, :], 1.0))
            chain.link(dve.reciprocal(gates[:, :, :], gexp[:, :, :]))
            dve.wait_ge(aexp, 3)
            chain.link(dve.tensor_scalar(f[:, :, :], f[:, :, :], 0.0, None, ALU.min))
            chain.link(dve.tensor_tensor(fln[:, :, :], f[:, :, :], fln[:, :, :], ALU.subtract))
            dve.wait_ge(made, 3)
            cmp_gates = gates[:, 0, :].rearrange("p (h b) -> p h b", b=3)[:, :, 0]
            chain.link(dve.tensor_scalar(cmp_gates, cmp_gates, valid[:, 0:1], None, ALU.mult))
            dve.wait_ge(turned, 1)
            dve.tensor_tensor_scan(fT[:, 0:512], fps[0][:, :], zero[:, 0:512], 0.0, ALU.add, ALU.add
                                   ).then_inc(turned, 1)
            dve.wait_ge(turned, 2)
            dve.tensor_tensor_scan(fT[:, 512:S], fps[1][:, :], zero[:, 512:S], fT[:, 511:512], ALU.add, ALU.add
                                   ).then_inc(step, 1)


class MixerWeights:

    def __init__(self, sb, sem):
        self.q, self.k, self.v, self.c = (sb(f"mix_w{n}", [P, ND, P]) for n in "qkvc")
        self.fox_loaded, self.group_loaded, self.nsa_q_loaded, self.merge_loaded = (
            sem(n) for n in ("fox_w_loaded", "nsa_group_loaded", "nsa_q_loaded", "mg_loaded0"))
        self.merge_gate = [self.q, self.k]
        self.merge_o = [w[:, 0:NSA_HEADS * HD // P, :] for w in (self.v, self.c)]

    def load_fox(self, eng, d, t):
        for w, c in ((self.q, C_QB), (self.k, C_KB), (self.v, C_VB)):
            eng.dma_start(w[:, :, :], d["w_in"][0, :, bass.ds(t * P + c, P)].rearrange("(k p) n -> p k n", p=P)
                          ).then_inc(self.fox_loaded, 16)

    def load_nsa_group(self, eng, d, grp):
        for w, half, c in ((self.c, LOW, C_KCMP), (self.c, HIGH, C_VCMP), (self.k, LOW, C_KSLC), (self.k, HIGH, C_KWIN),
                           (self.v, LOW, C_VSLC), (self.v, HIGH, C_VWIN)):
            eng.dma_start(w[:, :, half], d["w_in"][0, :, bass.ds(grp * HD + c, HD)].rearrange("(k p) n -> p k n", p=P)
                          ).then_inc(self.group_loaded, 16)

    def load_nsa_q(self, eng, d, t):
        eng.dma_start(self.q[:, :, :], d["w_in"][0, :, bass.ds(t * P + C_QA, P)].rearrange("(k p) n -> p k n", p=P)
                      ).then_inc(self.nsa_q_loaded, 16)



CR_SCORE = 2
CR_TURN = 6
CR_LO = 2
CR_PV = 2
CR_COMB = 4
CR_FAC = 4
Y_CHUNKS = 2


class Unit:

    def __init__(self, h, i, k0, nk, br, first):
        self.h, self.i, self.k0, self.nk, self.br, self.first = h, i, k0, nk, br, first

    @property
    def chunks(self):
        return [(a, min(a + 512, self.nk)) for a in range(0, self.nk, 512)]


def n_chunks(units):
    return sum(len(u.chunks) for u in units)


class AttentionBuffers:

    def __init__(self, nc, ctx, tag):
        sb, ps, sem = allocator(nc, ctx)
        self.tag, self.counts = tag, {}
        self.S = [ps(f"{tag}_S{s}", [P, S]) for s in range(2)]
        self.T = [ps(f"{tag}_T{s}", [P, 512]) for s in range(2)]
        self.O = [ps(f"{tag}_O{s}", [P, 512]) for s in range(2)]
        self.X = [sb(f"{tag}_X{s}", [P, S]) for s in range(3)]
        self.PTh = [sb(f"{tag}_PTh{s}", [P, S], F32R) for s in range(2)]
        self.PTl = [sb(f"{tag}_PTl{s}", [P, S], F32R) for s in range(2)]
        self.low = sb(f"{tag}_low", [P, 4])
        self.rsum = sb(f"{tag}_rsum", [P, 4])
        self.rmax = sb(f"{tag}_rmax", [P, 4])
        self.inv = sb(f"{tag}_inv", [P, 4])
        self.fac = sb(f"{tag}_fac", [P, 4])
        self.y2 = sb(f"{tag}_y2", [P, NT, 2, P])
        self.y = sb(f"{tag}_y", [P, NT, P])
        self.scored, self.score_read = sem(f"{tag}_scored"), sem(f"{tag}_score_read")
        self.probs, self.turned = sem(f"{tag}_probs"), sem(f"{tag}_turned")
        self.hi_done, self.lo_done = sem(f"{tag}_hi_done"), sem(f"{tag}_lo_done")
        self.pv_done, self.sum_used = sem(f"{tag}_pv_done"), sem(f"{tag}_sum_used")
        self.inv_done, self.fac_ready = sem(f"{tag}_inv_done"), sem(f"{tag}_fac_ready")
        self.combined, self.folded = sem(f"{tag}_combined"), sem(f"{tag}_folded")
        self.proj_done, self.proj_a, self.proj_d = (sem(f"{tag}_proj_{n}") for n in ("done", "a", "d"))


def in_register(eng, a, value, n=0):
    key = (eng.engine, n)
    if key not in a.counts:
        a.counts[key] = eng.alloc_register(f"{a.tag}_count{n}")
    eng.reg_mov(a.counts[key], value)
    return a.counts[key]


def attend_pe(pe, g, a, units, t, operands):
    N, C = len(units), n_chunks(units)
    before = [n_chunks(units[:n]) for n in range(N + 1)]
    u0, c0 = t * N, t * (C + Y_CHUNKS)

    def scores(n):
        u = units[n]
        q, ks, _, mask = operands(u)
        pe.wait_ge(a.score_read, u0 + n + 1)
        for lo, hi in u.chunks:
            out = a.S[n % 2][:, lo:hi]
            pe.matmul(out, q, ks[0][:, u.k0 + lo:u.k0 + hi], start=True, stop=False)
            if mask is not None and hi == u.nk:
                pe.matmul(a.S[n % 2][:, hi - P:hi], g.ident_r[:, :], mask, start=False, stop=False)
            last = pe.matmul(out, q, ks[1][:, u.k0 + lo:u.k0 + hi], start=False, stop=True)
        last.then_inc(a.scored, 1)

    def turn(n):
        u = units[n]
        pe.wait_ge(a.probs, u0 + n + 1)
        for j, (lo, hi) in enumerate(u.chunks):
            c = before[n] + j
            pe.wait_ge(a.lo_done, c0 + c + 1)
            for b in range(lo, hi, P):
                last = pe.transpose(a.T[c % 2][:, b - lo:b - lo + P], a.X[n % 3][:, b:b + P], g.ident[:, :])
            last.then_inc(a.turned, 1)

    def weigh(n):
        u = units[n]
        v = operands(u)[2]
        pe.wait_ge(a.lo_done, c0 + before[n + 1] + CR_LO)
        pe.wait_ge(a.combined, u0 + n + CR_COMB - 1)
        out = a.O[n % 2][:, 0:P]
        for b in range(0, u.nk, P):
            w = min(P, u.nk - b)
            pe.matmul(out, a.PTh[n % 2][0:w, b:b + P], v(b // P), start=(b == 0), stop=False)
            last = pe.matmul(out, a.PTl[n % 2][0:w, b:b + P], v(b // P), start=False, stop=(b + P >= u.nk))
        last.then_inc(a.pv_done, 1)

    scores(0)
    scores(1)
    for n in range(N):
        if n + 2 < N:
            scores(n + 2)
        turn(n)
        if n >= 1:
            weigh(n - 1)
    weigh(N - 1)
    pe.wait_ge(a.folded, t * 2 + 2)
    for half in range(2):
        pe.wait_ge(a.lo_done, c0 + C + half + 1)
        for i in range(4):
            last = pe.transpose(a.T[half][:, i * P:(i + 1) * P], a.y[:, 4 * half + i, :], g.ident[:, :])
        last.then_inc(a.turned, 1)


def attend_act(act, a, units, t):
    N, C = len(units), n_chunks(units)
    before = [n_chunks(units[:n]) for n in range(N + 1)]
    u0, c0 = t * N, t * (C + Y_CHUNKS)

    def exps(n):
        u = units[n]
        act.wait_ge(a.score_read, u0 + n + 1 + CR_SCORE)
        act.wait_ge(a.sum_used, u0 + n + 1)
        x = a.X[n % 3][:, 0:u.nk]
        act.activation(x, x, ACT.Exp, bias=a.low[:, n % 4:n % 4 + 1], scale=-1.0,
                       accum_out=a.rsum[:, n % 4:n % 4 + 1]).then_inc(a.probs, 1)

    def hi(n):
        u = units[n]
        act.wait_ge(a.pv_done, u0 + n + 1)
        for j, (lo, end) in enumerate(u.chunks):
            c = before[n] + j
            w = min(P, u.nk)
            cols = max(P, end - lo)
            act.wait_ge(a.turned, c0 + c + 1 + CR_TURN)
            act.activation(a.PTh[n % 2][0:w, lo:lo + cols], a.T[c % 2][0:w, 0:cols], ACT.Copy).then_inc(a.hi_done, 1)

    exps(0)
    for n in range(N):
        if n + 1 < N:
            exps(n + 1)
        hi(n)


def attend_dve(dve, a, units, t, bias_of, gated, yT):
    N, C = len(units), n_chunks(units)
    before = [n_chunks(units[:n]) for n in range(N + 1)]
    u0, c0, h0 = t * N, t * (C + Y_CHUNKS), t * C

    def add_bias(n):
        u = units[n]
        chunks = before[n - 2] if n >= 3 else -Y_CHUNKS
        scored = in_register(dve, a, u0 + n + 1, 1)
        count = in_register(dve, a, c0 + (chunks + CR_TURN))
        dve.wait_ge(a.score_read, CR_SCORE)
        dve.wait_ge(a.scored, scored)
        dve.wait_ge(a.turned, count)
        dve.tensor_tensor_reduce(out=a.X[n % 3][:, 0:u.nk], in0=a.S[n % 2][:, 0:u.nk], in1=bias_of(u),
                                 scale=1.0, scalar=3e38, op0=ALU.add, op1=ALU.min,
                                 accum_out=a.low[:, n % 4:n % 4 + 1]).then_inc(a.score_read, 1)

    def lo(n):
        u = units[n]
        for j, (start, end) in enumerate(u.chunks):
            c = before[n] + j
            w = min(P, u.nk)
            cols = max(P, end - start)
            dve.wait_ge(a.hi_done, h0 + c + 1)
            dve.tensor_tensor(a.PTl[n % 2][0:w, start:start + cols], a.T[c % 2][0:w, 0:cols],
                              a.PTh[n % 2][0:w, start:start + cols].bitcast(F32), ALU.subtract
                              ).then_inc(a.lo_done, 1)

    def invert(n):
        c = slice(n % 4, n % 4 + 1)
        dve.wait_ge(a.sum_used, u0 + n + 1 + CR_FAC)
        dve.wait_ge(a.combined, u0 + n + 1)
        if gated:
            dve.reciprocal(a.inv[:, c], a.rmax[:, c]).then_inc(a.inv_done, 1)
        else:
            dve.reciprocal(a.fac[:, c], a.rmax[:, c]).then_inc(a.inv_done, 1)

    def combine(n):
        u = units[n]
        y = a.y2[:, u.i, u.h, :]
        f = a.fac[:, n % 4:n % 4 + 1]
        dve.wait_ge(a.pv_done, u0 + n + 1 + CR_PV)
        if gated:
            dve.wait_ge(a.fac_ready, u0 + n + 1)
        else:
            dve.wait_ge(a.inv_done, u0 + n + 1 + CR_FAC)
        if u.first:
            dve.tensor_scalar(y, a.O[n % 2][:, 0:P], f, None, ALU.mult).then_inc(a.combined, 1)
        else:
            dve.wait_ge(a.combined, u0 + n + CR_COMB)
            dve.scalar_tensor_tensor(out=y, in0=a.O[n % 2][:, 0:P], scalar=f, in1=y,
                                     op0=ALU.mult, op1=ALU.add).then_inc(a.combined, 1)

    add_bias(0)
    add_bias(1)
    for n in range(N):
        if n + 2 < N:
            add_bias(n + 2)
        lo(n)
        invert(n)
        if n >= 1:
            combine(n - 1)
    combine(N - 1)
    dve.wait_ge(a.combined, u0 + N + CR_COMB)
    fold(dve, a, 1)
    for half in range(2):
        dve.wait_ge(a.turned, c0 + C + half + 1 + CR_TURN)
        dve.tensor_copy(yT[:, bass.ds(t, 1), half * 512:(half + 1) * 512], a.T[half][:, :].unsqueeze(1)
                        ).then_inc(a.lo_done, 1)


def fold(eng, a, h):
    eng.tensor_tensor(a.y[:, :, h * HD:(h + 1) * HD], a.y2[:, :, h, 0:HD], a.y2[:, :, h, HD:P], ALU.add
                      ).then_inc(a.folded, 1)


def attend_pool(pool, a, units, t, gate_of):
    N = len(units)
    u0 = t * N

    def guard(n):
        c = slice(n % 4, n % 4 + 1)
        count = in_register(pool, a, u0 + n + 1)
        pool.wait_ge(a.sum_used, CR_FAC)
        pool.wait_ge(a.probs, count)
        pool.wait_ge(a.inv_done, count)
        pool.tensor_scalar(a.rmax[:, c], a.rsum[:, c], 1e-30, None, ALU.max).then_inc(a.sum_used, 1)

    def gate(n):
        c = slice(n % 4, n % 4 + 1)
        pool.wait_ge(a.inv_done, u0 + n + 1 + CR_FAC)
        pool.wait_ge(a.combined, u0 + n + 1)
        pool.tensor_tensor(a.fac[:, c], a.inv[:, c], gate_of(units[n]), ALU.mult).then_inc(a.fac_ready, 1)

    for n in range(N):
        guard(n)
        if gate_of is not None:
            gate(n)
        if n == N // 2 + 3:
            pool.wait_ge(a.combined, u0 + N // 2 + CR_COMB)
            fold(pool, a, 0)


def project_columns(pe, a, slot, w, hT):
    for half in range(2):
        for k in range(ND):
            last = pe.matmul(a.S[slot][:, half * 512:(half + 1) * 512], w[:, k, :],
                             hT[:, k, half * 512:(half + 1) * 512], start=(k == 0), stop=(k == ND - 1))
    last.then_inc(a.proj_done, 1)


def project_rows(pe, a, slot, w, hT):
    for i in range(NT):
        for k in range(ND):
            last = pe.matmul(a.S[slot][:, i * P:(i + 1) * P], hT[:, k, i * P:(i + 1) * P], w[:, k, :],
                             start=(k == 0), stop=(k == ND - 1))
    last.then_inc(a.proj_done, 1)


LOW, HIGH = slice(0, HD), slice(HD, P)


def queries_act(act, ps, q):
    act.activation(q[0][LOW, :], ps[LOW, :], ACT.Copy, scale=NEG_SCALE)
    return act.activation(q[1][LOW, :], ps[HIGH, :], ACT.Copy, scale=NEG_SCALE)


def queries_dve(dve, ps, q):
    for h, part in enumerate((LOW, HIGH)):
        last = dve.scalar_tensor_tensor(out=q[h][HIGH, :], in0=ps[part, :], scalar=NEG_SCALE,
                                        in1=q[h][LOW, :].bitcast(F32), op0=ALU.mult, op1=ALU.subtract)
    return last


def keys_act(act, ps, k_hi):
    for h, part in enumerate((LOW, HIGH)):
        act.activation(k_hi[h][LOW, :], ps[part, :], ACT.Copy)
        last = act.activation(k_hi[h][HIGH, :], ps[part, :], ACT.Copy)
    return last


def keys_dve(dve, ps, k_hi, k_lo):
    for h, part in enumerate((LOW, HIGH)):
        dve.tensor_tensor(k_lo[h][LOW, :], ps[part, :], k_hi[h][LOW, :].bitcast(F32), ALU.subtract)
        last = dve.tensor_tensor(k_lo[h][HIGH, :], ps[part, :], k_hi[h][LOW, :].bitcast(F32), ALU.subtract)
    return last


def values_act(act, ps, v):
    return act.activation(v[:, :, 0:HD], ps[:, :].rearrange("p (n e) -> p n e", e=HD), ACT.Copy)


def values_dve(dve, ps, v):
    return dve.tensor_tensor(v[:, :, HD:P], ps[:, :].rearrange("p (n e) -> p n e", e=HD),
                             v[:, :, 0:HD].bitcast(F32), ALU.subtract)


def fox(nc, g, d, w, hT, yT, fsum_dram, y_dram, room):
    units = [Unit(h=h, i=i, k0=0, nk=(i + 1) * P, br=0, first=True) for h in range(2) for i in range(NT)]
    N = len(units)
    PAIRS = FOX_HEADS // 2
    with ExitStack() as ctx:
        sb, ps, sem = allocator(nc, ctx)
        a = AttentionBuffers(nc, ctx, "fox")
        q = [sb(f"fox_q{h}", [P, S], F32R) for h in range(2)]
        k_hi = [sb(f"fox_kh{h}", [P, S], F32R) for h in range(2)]
        k_lo = [sb(f"fox_kl{h}", [P, S], F32R) for h in range(2)]
        v = sb("fox_v", [P, NT * 2, P], F32R)
        decay = room[:, D:D + 2 * S].rearrange("p (h n) -> p h n", n=S)
        mask_f = sb("fox_mask_f", [P, P])
        mask = sb("fox_mask", [P, P], F32R)
        zero = room[:, 0:D]
        masked, decayed, blank, blanked = (sem(f"fox_{n}") for n in ("masked", "decayed", "blank", "blanked"))
        block = ctx.enter_context(nc.Block())

        @block.sync
        def _(sp):
            def load_decay(t):
                for h in range(2):
                    sp.dma_start(decay[:, h, :], fsum_dram[bass.ds(t * 2 + h, 1), :].to_broadcast([P, S])
                                 ).then_inc(decayed, 16)

            load_decay(0)
            with sp.Fori(0, PAIRS - 1) as t:
                sp.wait_ge(a.proj_d, t * 3 + 4)
                w.load_fox(sp, d, t + 1)
                sp.wait_ge(a.score_read, t * N + (N + CR_SCORE))
                load_decay(t + 1)
            sp.wait_ge(a.proj_d, (PAIRS - 1) * 3 + 4)
            w.load_nsa_group(sp, d, 0)
            w.load_nsa_q(sp, d, 0)
            sp.wait_ge(blank, 1)
            for j in range(N_COL - N_EXP):
                sp.dma_start(y_dram[(N_EXP + j) * P:(N_EXP + j + 1) * P, :], zero[:, :]).then_inc(blanked, 16)
            sp.wait_ge(blanked, (N_COL - N_EXP) * 16)

        def operands(u):
            return (q[u.h][:, u.i * P:(u.i + 1) * P], (k_hi[u.h], k_lo[u.h]),
                    lambda b: v[:, 2 * b + u.h, :], mask[:, :])

        @block.tensor
        def _(pe):
            with pe.Fori(0, PAIRS) as t:
                pe.wait_ge(a.score_read, t * N + CR_SCORE)
                pe.wait_ge(w.fox_loaded, t * 48 + 48)
                project_columns(pe, a, 0, w.q, hT)
                project_columns(pe, a, 1, w.k, hT)
                pe.wait_ge(a.proj_d, t * 3 + 2)
                project_rows(pe, a, 0, w.v, hT)
                pe.wait_ge(a.proj_d, t * 3 + 4)
                pe.wait_ge(masked, 4)
                attend_pe(pe, g, a, units, t, operands)

        @block.scalar
        def _(act):
            with act.Fori(0, PAIRS) as t:
                act.wait_ge(a.proj_done, t * 3 + 1)
                queries_act(act, a.S[0], q).then_inc(a.proj_a, 1)
                act.wait_ge(a.proj_done, t * 3 + 2)
                keys_act(act, a.S[1], k_hi).then_inc(a.proj_a, 1)
                act.wait_ge(a.proj_done, t * 3 + 3)
                values_act(act, a.S[0], v).then_inc(a.proj_a, 1)
                attend_act(act, a, units, t)

        @block.gpsimd
        def _(pool):
            pool.sem_inc(a.sum_used, CR_FAC)
            pool.memset(mask_f[:, :], 0.0).then_inc(masked, 1)
            pool.memset(zero[:, :], 0.0).then_inc(blank, 1)
            pool.wait_ge(masked, 1)
            pool.affine_select(out=mask_f[:, :], in_=mask_f[:, :], compare_op=ALU.is_ge, fill=2.0 ** 99, base=0,
                               pattern=[[-1, P]], channel_multiplier=1).then_inc(masked, 1)
            with pool.Fori(0, PAIRS) as t:
                attend_pool(pool, a, units, t, None)

        @block.vector
        def _(dve):
            dve.sem_inc(a.score_read, CR_SCORE)
            dve.sem_inc(a.lo_done, CR_LO)
            dve.sem_inc(a.combined, CR_COMB)
            dve.sem_inc(a.pv_done, CR_PV)
            dve.sem_inc(a.turned, CR_TURN)
            dve.sem_inc(a.proj_d, 1)
            dve.sem_inc(a.inv_done, CR_FAC)
            dve.wait_ge(masked, 2)
            dve.tensor_copy(mask[:, :], mask_f[:, :]).then_inc(masked, 1)
            dve.tensor_copy(g.ident_r[:, :], g.ident[:, :]).then_inc(masked, 1)
            with dve.Fori(0, PAIRS) as t:
                dve.wait_ge(a.proj_a, t * 3 + 1)
                queries_dve(dve, a.S[0], q).then_inc(a.proj_d, 1)
                dve.wait_ge(a.proj_a, t * 3 + 2)
                keys_dve(dve, a.S[1], k_hi, k_lo).then_inc(a.proj_d, 1)
                dve.wait_ge(a.proj_a, t * 3 + 3)
                values_dve(dve, a.S[0], v).then_inc(a.proj_d, 1)
                dve.wait_ge(decayed, t * 32 + 32)
                attend_dve(dve, a, units, t, lambda u: decay[:, u.h, 0:u.nk], False, yT)


def nsa(nc, g, d, w, early, hT, yT, gates, room):
    CMP, SEL, WIN = range(3)
    units = []
    for h in range(2):
        for i in range(NT):
            k0 = max(0, i * P - WINDOW)
            units += [Unit(h=h, i=i, br=CMP, k0=0, nk=HD, first=True),
                      Unit(h=h, i=i, br=SEL, k0=0, nk=(i + 1) * P, first=False),
                      Unit(h=h, i=i, br=WIN, k0=k0, nk=(i + 1) * P - k0, first=False)]
    N = len(units)
    W_CMP = NT * HD
    W_WIN = WINDOW + P
    X_SEL, X_WIN, X_CMP = 0, S, S + W_WIN
    W_TAB = S + W_WIN + W_CMP
    PPG = NSA_HEADS // NSA_GROUPS // 2
    G_TILES = 3 + PPG
    GELU_A, GELU_B = 0.044715, 2 * (2 / 3.141592653589793) ** 0.5
    with ExitStack() as ctx:
        sb, ps, sem = allocator(nc, ctx)
        w1, w2, pec = early.w1, early.w2, early.pec
        a = AttentionBuffers(nc, ctx, "nsa")
        q = [sb(f"nsa_q{h}", [P, S], F32R) for h in range(2)]
        k_hi = [sb(f"nsa_kh{b}", [P, S], F32R) for b in range(2)]
        k_lo = [sb(f"nsa_kl{b}", [P, S], F32R) for b in range(2)]
        v = sb("nsa_v", [P, NT * 2, P], F32R)
        kc_hi = sb("cmp_kh", [P, HD], F32R)
        kc_lo = sb("cmp_kl", [P, HD], F32R)
        vc = sb("cmp_v", [HD, P], F32R)
        dist = room[:, 0:W_TAB]
        bias = room[:, W_TAB:3 * W_TAB].rearrange("p (h n) -> p h n", h=2)
        kvc = room[:, 3 * W_TAB:3 * W_TAB + S]
        rest = room[:, 3 * W_TAB + S:]
        hid, cube, act_out = (rest[:, n * HD:n * HD + N_CMP] for n in range(3))
        hidT = rest[:, 3 * HD:4 * HD]
        pair_gates = sb("pair_gates", [P, NT, 6])
        cleared, cmp_pe, cmp_act, cmp_dve, tables, gated, made = (
            sem(n) for n in ("nsa_cleared", "cmp_pe", "cmp_act", "cmp_dve", "tables", "pair_gated", "dist_made"))
        C_DVE, C_ACT, C_PE = 9, 4, 2
        block = ctx.enter_context(nc.Block())

        @block.sync
        def _(sp):
            def load_q(grp, pr):
                sp.wait_ge(a.proj_d, grp * G_TILES + (pr + 4))
                w.load_nsa_q(sp, d, grp * PPG + pr)

            with sp.Fori(0, NSA_GROUPS - 1) as grp:
                sp.wait_ge(a.proj_d, grp * G_TILES + 4)
                w.load_nsa_group(sp, d, grp + 1)
                for pr in range(1, PPG):
                    load_q(grp, pr + 0)
                load_q(grp, PPG)
            for pr in range(1, PPG):
                load_q(NSA_GROUPS - 1, pr)
            sp.wait_ge(a.proj_d, (NSA_GROUPS - 1) * G_TILES + (PPG + 4))
            load_merge_weights(sp, d, w.merge_gate, w.merge_o, 0, w.merge_loaded)

        def operands(u):
            tile = slice(u.i * P, (u.i + 1) * P)
            if u.br == CMP:
                return q[u.h][:, tile], (kc_hi, kc_lo), lambda b: vc[:, :], None
            b = u.br - SEL
            return (q[u.h][:, tile], (k_hi[b], k_lo[b]),
                    lambda n: v[:, 2 * (u.k0 // P + n) + b, :], None)

        def bias_of(u):
            if u.br == CMP:
                lo = X_CMP + u.i * HD
            elif u.br == SEL:
                lo = X_SEL + S - u.nk
            else:
                lo = X_WIN + W_WIN - u.nk
            return bias[:, u.h, lo:lo + u.nk]

        @block.tensor
        def _(pe):
            with pe.Fori(0, NSA_GROUPS) as grp:
                pe.wait_ge(a.score_read, grp * (PPG * N) + CR_SCORE)
                pe.wait_ge(w.group_loaded, grp * 96 + 96)
                project_columns(pe, a, 0, w.c, hT)
                project_columns(pe, a, 1, w.k, hT)
                pe.wait_ge(a.proj_d, grp * G_TILES + 2)
                project_rows(pe, a, 0, w.v, hT)
                pe.wait_ge(a.combined, grp * (PPG * N) + CR_COMB)
                for l in range(CMP_LEN):
                    last = pe.matmul(a.O[0][:, 0:N_CMP], w1[:, l, :],
                                     kvc[:, l:l + CMP_STRIDE * (N_CMP - 1) + 1:CMP_STRIDE],
                                     start=(l == 0), stop=(l == CMP_LEN - 1))
                last.then_inc(cmp_pe, 1)
                pe.wait_ge(cmp_dve, grp * C_DVE + 7)
                pe.matmul(a.O[1][:, 0:HD], w2[:, :], hidT[:, :], start=True, stop=True)
                pe.matmul(a.O[1][0:HD, HD:P], hidT[:, :], w2[:, HIGH], start=True, stop=True).then_inc(cmp_pe, 1)
                with pe.Fori(0, PPG) as pr:
                    t = grp * PPG + pr
                    pe.wait_ge(cmp_dve, grp * C_DVE + C_DVE)
                    pe.wait_ge(a.score_read, t * N + CR_SCORE)
                    pe.wait_ge(a.proj_d, grp * G_TILES + pr + 4)
                    pe.wait_ge(w.nsa_q_loaded, t * 16 + 16)
                    project_columns(pe, a, 1, w.q, hT)
                    pe.wait_ge(a.proj_d, grp * G_TILES + pr + 5)
                    attend_pe(pe, g, a, units, t, operands)

        @block.scalar
        def _(act):
            act.wait_ge(made, 8)
            with act.Fori(0, NSA_GROUPS) as grp:
                act.wait_ge(a.proj_done, grp * G_TILES + 1)
                act.activation(kvc[:, 0:512], a.S[0][:, 0:512], ACT.Copy).then_inc(a.proj_a, 1)
                act.wait_ge(a.proj_done, grp * G_TILES + 2)
                keys_act(act, a.S[1], k_hi).then_inc(a.proj_a, 1)
                act.wait_ge(a.proj_done, grp * G_TILES + 3)
                values_act(act, a.S[0], v).then_inc(a.proj_a, 1)
                act.wait_ge(cmp_dve, grp * C_DVE + 4)
                act.activation(act_out[:, :], cube[:, :], ACT.Exp, scale=-GELU_B).then_inc(cmp_act, 1)
                act.wait_ge(cmp_pe, grp * C_PE + 2)
                act.activation(kc_hi[LOW, :], a.O[1][LOW, 0:HD], ACT.Copy).then_inc(cmp_act, 1)
                act.activation(kc_hi[HIGH, :], a.O[1][LOW, 0:HD], ACT.Copy).then_inc(cmp_act, 1)
                act.activation(vc[:, 0:HD], a.O[1][LOW, HD:P], ACT.Copy).then_inc(cmp_act, 1)
                with act.Fori(0, PPG) as pr:
                    t = grp * PPG + pr
                    act.wait_ge(a.score_read, t * N + CR_SCORE)
                    act.activation(bias[:, 0, :], dist[:, :], ACT.Copy, scale=0.5).then_inc(tables, 1)
                    act.activation(bias[:, 1, :], dist[:, :], ACT.Copy, scale=0.25).then_inc(tables, 1)
                    act.wait_ge(tables, t * 3 + 2)
                    act.activation(dist[:, :], dist[:, :], ACT.Copy, scale=0.25).then_inc(tables, 1)
                    act.wait_ge(tables, t * 3 + 3)
                    act.wait_ge(a.proj_done, grp * G_TILES + pr + 4)
                    queries_act(act, a.S[1], q).then_inc(a.proj_a, 1)
                    attend_act(act, a, units, t)

        @block.gpsimd
        def _(pool):
            pool.sem_inc(a.sum_used, CR_FAC)
            for s in range(3):
                pool.memset(a.X[s][:, 0:P], 0.0).then_inc(cleared, 1)
            pool.memset(hidT[:, :], 0.0).then_inc(made, 1)
            tab = dict(allow_small_or_imprecise_dtypes=True, channel_multiplier=1)
            pool.iota(dist[:, X_SEL:X_SEL + S], pattern=[[-1, S]], base=S - P, **tab).then_inc(made, 1)
            pool.iota(dist[:, X_WIN:X_WIN + W_WIN], pattern=[[-1, W_WIN]], base=WINDOW, **tab).then_inc(made, 1)
            pool.iota(dist[:, X_CMP:], pattern=[[P, NT], [-CMP_STRIDE, HD]], base=1 - CMP_LEN, **tab).then_inc(made, 1)
            pool.wait_ge(made, 4)

            def keep(lo, hi, pattern, base, mult):
                pool.affine_select(out=dist[:, lo:hi], in_=dist[:, lo:hi], compare_op=ALU.is_ge, fill=BIG,
                                   base=base, pattern=pattern, channel_multiplier=mult).then_inc(made, 1)

            keep(X_SEL, X_SEL + S, [[-1, S]], S - P, 1)
            keep(X_WIN, X_WIN + W_WIN, [[-1, W_WIN]], WINDOW, 1)
            keep(X_CMP, W_TAB, [[P, NT], [-CMP_STRIDE, HD]], 1 - CMP_LEN, 1)
            pool.wait_ge(made, 6)
            keep(X_WIN, X_WIN + W_WIN, [[1, W_WIN]], -1, -1)
            pool.wait_ge(made, 8)
            with pool.Fori(0, NSA_GROUPS) as grp:
                with pool.Fori(0, PPG) as pr:
                    t = grp * PPG + pr
                    pool.wait_ge(a.combined, t * N + CR_COMB)
                    pool.tensor_copy(pair_gates[:, :, :], gates[:, :, bass.ds(t * 6, 6)]).then_inc(gated, 1)
                    pool.wait_ge(gated, t * 1 + 1)
                    attend_pool(pool, a, units, t, lambda u: pair_gates[:, u.i, 3 * u.h + u.br:3 * u.h + u.br + 1])

        @block.vector
        def _(dve):
            dve.sem_inc(a.score_read, CR_SCORE)
            dve.sem_inc(a.lo_done, CR_LO)
            dve.sem_inc(a.combined, CR_COMB)
            dve.sem_inc(a.pv_done, CR_PV)
            dve.sem_inc(a.turned, CR_TURN)
            dve.sem_inc(a.proj_d, 1)
            dve.sem_inc(a.inv_done, CR_FAC)
            dve.wait_ge(cleared, 3)
            dve.wait_ge(made, 1)
            with dve.Fori(0, NSA_GROUPS) as grp:
                dve.wait_ge(a.proj_done, grp * G_TILES + 1)
                dve.wait_ge(a.proj_a, grp * G_TILES + 1)
                dve.tensor_copy(kvc[:, 512:S], a.S[0][:, 512:S]).then_inc(a.proj_d, 1)
                dve.wait_ge(a.proj_a, grp * G_TILES + 2)
                keys_dve(dve, a.S[1], k_hi, k_lo).then_inc(a.proj_d, 1)
                dve.wait_ge(a.proj_a, grp * G_TILES + 3)
                values_dve(dve, a.S[0], v).then_inc(a.proj_d, 1)
                dve.wait_ge(cmp_pe, grp * C_PE + 1)
                chain = Chain(dve, cmp_dve, grp * C_DVE)
                chain.link(dve.tensor_scalar(hid[:, :], a.O[0][:, 0:N_CMP], pec[:, 0:1], None, ALU.add))
                chain.link(dve.tensor_tensor(cube[:, :], hid[:, :], hid[:, :], ALU.mult))
                chain.link(dve.tensor_scalar(cube[:, :], cube[:, :], GELU_A, 1.0, ALU.mult, ALU.add))
                chain.link(dve.tensor_tensor(cube[:, :], cube[:, :], hid[:, :], ALU.mult))
                dve.wait_ge(cmp_act, grp * C_ACT + 1)
                chain.link(dve.tensor_scalar_add(act_out[:, :], act_out[:, :], 1.0))
                chain.link(dve.reciprocal(act_out[:, :], act_out[:, :]))
                chain.link(dve.tensor_tensor(hidT[:, 0:N_CMP], hid[:, :], act_out[:, :], ALU.mult))
                dve.wait_ge(cmp_act, grp * C_ACT + 4)
                dve.tensor_tensor(kc_lo[LOW, :], a.O[1][LOW, 0:HD], kc_hi[LOW, :].bitcast(F32), ALU.subtract)
                chain.link(dve.tensor_tensor(kc_lo[HIGH, :], a.O[1][LOW, 0:HD], kc_hi[LOW, :].bitcast(F32), ALU.subtract))
                dve.tensor_tensor(vc[:, HD:P], a.O[1][LOW, HD:P], vc[:, 0:HD].bitcast(F32), ALU.subtract
                                  ).then_inc(cmp_dve, 1)
                with dve.Fori(0, PPG) as pr:
                    t = grp * PPG + pr
                    dve.wait_ge(a.proj_a, grp * G_TILES + pr + 4)
                    queries_dve(dve, a.S[1], q).then_inc(a.proj_d, 1)
                    dve.wait_ge(tables, t * 3 + 2)
                    attend_dve(dve, a, units, t, bias_of, True, yT)



def load_merge_weights(eng, d, w_gate, w_o, c, loaded):
    for m, w in enumerate((d["w_o_nsa"], d["w_o_fox"])):
        eng.dma_start(w_gate[m][:, :, :], d["w_in"][0, :, bass.ds(c * P + (C_MG + m * D), P)]
                      .rearrange("(k p) n -> p k n", p=P)).then_inc(loaded, 16)
        eng.dma_start(w_o[m][:, :, :], w[0, :, bass.ds(c * P, P)].rearrange("(k p) n -> p k n", p=P)
                      ).then_inc(loaded, 16)


def merge(nc, g, d, w_mix, hT, yaT, ybT, mixT, mod, w_router, b_router, out_loaded):
    NY = yaT.shape[1]
    W_ADA, CREDIT = 128, 2 * ND
    with ExitStack() as ctx:
        sb, ps, sem = allocator(nc, ctx)
        w_gate = [w_mix.merge_gate, [sb(f"w_mg1{m}", [P, ND, P]) for m in range(2)]]
        w_o = [w_mix.merge_o, [sb(f"w_o1{m}", [P, NY, P]) for m in range(2)]]
        e = [sb(f"mg_e{s}", [P, 2, 512]) for s in range(2)]
        w_ada = [sb(f"mg_wada{q}", [P, ND, W_ADA]) for q in range(2)]
        h_hi, h_lo = (sb(f"mg_h_{n}", [P, ND, 512], F32R) for n in ("hi", "lo"))
        w_hi, w_lo = ([sb(f"mg_w_{n}{m}", [P, ND, P], F32R) for m in range(2)] for n in ("hi", "lo"))
        bank = [[ps(f"mg_ps{s}{m}", [P, 512]) for m in range(4)] for s in range(2)]
        loaded = [w_mix.merge_loaded, sem("mg_loaded1")]
        ada_loaded = [sem(f"mg_ada_loaded{q}") for q in range(2)]
        weighed, cleared, b_loaded = (sem(f"mg_{n}") for n in ("weighed", "cleared", "b_loaded"))
        multiplied, exped, step, used, mixed, h_hi_done, h_lo_done, w_hi_done, w_lo_done = (
            sem(f"mg_{n}") for n in ("multiplied", "exped", "step", "used", "mixed", "h_hi_done",
                                     "h_lo_done", "w_hi_done", "w_lo_done"))
        block = ctx.enter_context(nc.Block())
        halves = [slice(0, 512), slice(512, S)]
        ROUNDS = ND // 2

        def over_columns(eng, body):
            for h in range(2):
                with eng.Fori(0, ROUNDS - 1) as r:
                    for s in range(2):
                        body(r * 2 + s, s, r + h * ROUNDS, h, False)
                for s in range(2):
                    body(ND - 2 + s, s, (h + 1) * ROUNDS - 1, h, s == 1)

        @block.sync
        def _(sp):
            sp.wait_ge(cleared, 1)
            sp.dma_start(mod[0:1, :], d["b_ada"][0:1, 2 * D:]).then_inc(b_loaded, 16)

            def load(c, s, h, first=False):
                n = c + h * ND
                if not first:
                    sp.wait_ge(multiplied, n + 1)
                    load_merge_weights(sp, d, w_gate[s], w_o[s], c, loaded[s])
                for q in range(2):
                    j = n * 2 + q
                    sp.wait_ge(weighed, j * ND + ND)
                    sp.dma_start(w_ada[q][:, :, :], d["w_ada"][0, :, bass.ds(j * W_ADA + 2 * D, W_ADA)]
                                 .rearrange("(k p) n -> p k n", p=P)).then_inc(ada_loaded[q], 16)

            load(0, 0, 0, first=True)
            load(1, 1, 0)
            with sp.Fori(0, ROUNDS - 1) as r:
                for s in range(2):
                    load(r * 2 + (2 + s), s, 0)
            with sp.Fori(0, ROUNDS) as r:
                for s in range(2):
                    load(r * 2 + s, s, 1)
            for part, wr, br in ((slice(0, N_GRP), d["w_router_group"], d["b_router_group"]),
                                 (slice(N_GRP, N_GRP + N_EXP), d["w_router_expert"], d["b_router_expert"])):
                sp.dma_start(w_router[:, :, part], wr[0].rearrange("(k p) n -> p k n", p=P)).then_inc(out_loaded, 16)
                sp.dma_start(b_router[:, part], br[0:1, :].to_broadcast([P, part.stop - part.start])).then_inc(out_loaded, 16)

        @block.tensor
        def _(pe):
            def body(c, s, r, h, ends):
                n = c + h * ND
                pe.wait_ge(loaded[s], r * 64 + 64)
                pe.wait_ge(used, n + 1)
                for m, y in enumerate((yaT, ybT)):
                    for k in range(NY):
                        pe.matmul(bank[s][2 + m][:, :], w_o[s][m][:, k, :], y[:, k, halves[h]],
                                  start=(k == 0), stop=(k == NY - 1))
                pe.wait_ge(h_lo_done, (h + 1) * ND)
                pe.wait_ge(w_lo_done, n + 1)
                for m in range(2):
                    for k in range(ND):
                        out = bank[s][m][:, :]
                        pe.matmul(out, w_hi[m][:, k, :], h_hi[:, k, :], start=(k == 0), stop=False)
                        pe.matmul(out, w_hi[m][:, k, :], h_lo[:, k, :], start=False, stop=False)
                        end = pe.matmul(out, w_lo[m][:, k, :], h_hi[:, k, :], start=False, stop=(k == ND - 1))
                end.then_inc(multiplied, 1)

            pe.sem_inc(multiplied, 2)
            over_columns(pe, body)

        @block.scalar
        def _(act):
            def split(s):
                act.activation(w_hi[0][:, :, :], w_gate[s][0][:, :, :], ACT.Copy)
                act.activation(w_hi[1][:, :, :], w_gate[s][1][:, :, :], ACT.Copy).then_inc(w_hi_done, 1)

            def split_h(h):
                act.wait_ge(multiplied, h * ND + 2)
                with act.Fori(0, ND) as k:
                    act.activation(h_hi[:, bass.ds(k, 1), :], hT[:, bass.ds(k, 1), halves[h]], ACT.Copy
                                   ).then_inc(h_hi_done, 1)

            def body(c, s, r, h, ends):
                n = c + h * ND
                act.wait_ge(multiplied, n + 3)
                if not (ends and h == 1):
                    act.wait_ge(loaded[1 - s], r * 64 + (64 + 64 * s))
                    split(1 - s)
                if ends and h == 0:
                    split_h(1)
                act.wait_ge(mixed, n + 1)
                act.activation(e[s][:, 0, :], bank[s][0][:, :], ACT.Exp, scale=-1.0)
                act.activation(e[s][:, 1, :], bank[s][1][:, :], ACT.Exp, scale=-1.0).then_inc(exped, 1)

            act.wait_ge(loaded[0], 64)
            split(0)
            split_h(0)
            over_columns(act, body)

        @block.vector
        def _(dve):
            def split_w(s, n):
                dve.wait_ge(w_hi_done, n + 1)
                for m in range(2):
                    last = dve.tensor_tensor(w_lo[m][:, :, :], w_gate[s][m][:, :, :], w_hi[m][:, :, :].bitcast(F32), ALU.subtract)
                last.then_inc(w_lo_done, 1)

            def split_h(h):
                with dve.Fori(0, ND) as k:
                    dve.wait_ge(h_hi_done, k + (h * ND + 1))
                    dve.tensor_tensor(h_lo[:, bass.ds(k, 1), :], hT[:, bass.ds(k, 1), halves[h]],
                                      h_hi[:, bass.ds(k, 1), :].bitcast(F32), ALU.subtract).then_inc(h_lo_done, 1)

            def body(c, s, r, h, ends):
                n = c + h * ND
                for q in range(2):
                    j = n * 2 + q
                    dve.wait_ge(ada_loaded[q], n * 16 + 16)
                    part = mod[:, bass.ds(j * W_ADA, W_ADA)]
                    chain = Chain(dve, weighed, j * ND + CREDIT)
                    for k in range(ND):
                        chain.link(dve.scalar_tensor_tensor(out=part, in0=w_ada[q][:, k, :], scalar=g.csilu[:, k:k + 1],
                                                            in1=part, op0=ALU.mult, op1=ALU.add))
                if not (ends and h == 1):
                    split_w(1 - s, n + 1)
                if ends and h == 0:
                    split_h(1)
                dve.wait_ge(exped, n + 1)
                chain = Chain(dve, step, n * 2)
                chain.link(dve.tensor_scalar_add(e[s][:, :, :], e[s][:, :, :], 1.0))
                chain.link(dve.reciprocal(e[s][:, :, :], e[s][:, :, :]))
                dve.tensor_tensor(e[s][:, 0, :], e[s][:, 0, :], bank[s][2][:, :], ALU.mult)
                dve.tensor_tensor(e[s][:, 1, :], e[s][:, 1, :], bank[s][3][:, :], ALU.mult).then_inc(used, 1)

            dve.sem_inc(used, 2)
            dve.sem_inc(weighed, CREDIT)
            split_w(0, 0)
            split_h(0)
            dve.wait_ge(b_loaded, 16)
            over_columns(dve, body)

        @block.gpsimd
        def _(pool):
            pool.sem_inc(mixed, 2)
            pool.memset(mod[:, :], 0.0).then_inc(cleared, 1)
            pool.wait_ge(cleared, 1)
            for h in range(2):
                with pool.Fori(0, ROUNDS) as r:
                    for s in range(2):
                        c = r * 2 + s
                        pool.wait_ge(used, c + (h * ND + 3))
                        pool.tensor_tensor(mixT[:, bass.ds(c, 1), halves[h]], e[s][:, 0, :].unsqueeze(1),
                                           e[s][:, 1, :].unsqueeze(1), ALU.add).then_inc(mixed, 1)



def project_out(nc, g, d, mixT, mod, wr, br, out_loaded, x1, logits, h2_dram, expert_weights):
    GT_M, SH_F, SC_F, GT_F = (slice(i * D, (i + 1) * D) for i in range(4))
    NL = N_GRP + N_EXP
    with ExitStack() as ctx:
        sb, ps, sem = allocator(nc, ctx)
        w = sb("w_out_sb", [P, ND, D])
        w_loaded = sem("o_w_loaded")
        gain = [sb(f"gain{n}", [P, D]) for n in range(3)]
        mt = [sb(f"mt{s}", [P, ND, P]) for s in range(2)]
        x = [sb(f"xo{s}", [P, D]) for s in range(2)]
        scaled = [sb(f"scaled{s}", [P, D]) for s in range(2)]
        h2 = [sb(f"h2{s}", [P, D]) for s in range(2)]
        h2T = sb("h2T", [P, ND, P])
        ms = [sb(f"oms{s}", [P, 2]) for s in range(2)]
        rstd = [sb(f"orstd{s}", [P, 2]) for s in range(2)]
        junk = sb("ojunk", [P, D])
        M = [ps(f"oM{s}", [P, D]) for s in range(2)]
        TP = ps("oT", [P, D])
        LG = ps("oL", [P, NL])
        SUM = [TP[:, 0:512], TP[:, 512:D]]
        summed, added = sem("o_summed"), sem("o_added")
        x_loaded = [sem(f"o_x_loaded{s}") for s in range(2)]
        stored = [sem(f"o_stored{s}") for s in range(2)]
        gains, staged, mixed, astep, dstep, shifted, turned, out_a, out_d, routed, logit = (
            sem(f"o_{n}") for n in ("gains", "staged", "mixed", "astep", "dstep", "shifted",
                                    "turned", "out_a", "out_d", "routed", "logit"))
        A_STEPS, D_STEPS, CREDIT = 4, 5, 10
        block = ctx.enter_context(nc.Block())

        @block.sync
        def _(sp):
            sp.dma_start(w[:, :, :], d["w_out"][0].rearrange("(k p) n -> p k n", p=P)).then_inc(w_loaded, 16)
            for n, gd in enumerate((d["g_post_mix"], d["g_pre_ffn"], d["g_post_ffn"])):
                sp.dma_start(gain[n][:, :], gd[0:1, :].to_broadcast([P, D])).then_inc(gains, 16)

            def load(i, s, r):
                sp.wait_ge(dstep, i * D_STEPS + 3)
                sp.dma_start(x[s][:, :], d["x"][0, bass.ds(i * P, P), :]).then_inc(x_loaded[s], 16)

            def store(i, s, r):
                sp.wait_ge(shifted, i + 1)
                sp.dma_start(h2_dram[bass.ds(i * P, P), :], h2[s][:, :]).then_inc(stored[s], 16)

            for s in range(2):
                sp.sem_inc(stored[s], 16)
            expert_weights.load_gate_up(sp, d, 0, 0)
            over_tiles(sp, load, store)
            for s in range(2):
                sp.wait_ge(stored[s], (NT // 2 + 1) * 16)

        @block.tensor
        def _(pe):
            def project(i, s, r):
                pe.wait_ge(staged, i + 1)
                pe.wait_ge(dstep, i * D_STEPS + 2)
                for half in range(2):
                    cols = slice(half * 512, (half + 1) * 512)
                    for k in range(ND):
                        last = pe.matmul(M[s][:, cols], mt[s][:, k, :], w[:, k, cols], start=(k == 0), stop=(k == ND - 1))
                last.then_inc(mixed, 1)

            def route(i, s, r):
                pe.wait_ge(shifted, i + 1)
                pe.wait_ge(out_a, i + 1)
                pe.wait_ge(out_d, i + 1)
                for k in range(ND):
                    last = pe.transpose(TP[:, k * P:(k + 1) * P], h2[s][:, k * P:(k + 1) * P], g.ident[:, :])
                last.then_inc(turned, 1)
                pe.wait_ge(out_a, i + 2)
                pe.wait_ge(out_d, i + 2)
                pe.wait_ge(logit, i + 1)
                for k in range(ND):
                    last = pe.matmul(LG[:, :], h2T[:, k, :], wr[:, k, :], start=(k == 0), stop=(k == ND - 1))
                last.then_inc(routed, 1)

            with pe.Fori(0, 4 * D // 1024) as r:
                for b in range(2):
                    n = r * 2 + b
                    pe.wait_ge(added, n + 1)
                    pe.matmul(SUM[b], g.ones[:, :], mod[:, bass.ds(n * 512, 512)], start=True, stop=True
                              ).then_inc(summed, 1)
            pe.wait_ge(w_loaded, 16)
            project(0, 0, 0)
            pe.wait_ge(out_loaded, 64)
            pe.wait_ge(added, 2 + 4 * D // 512)
            with pe.Fori(0, NT // 2 - 1) as r:
                for s in range(2):
                    project(r * 2 + s + 1, 1 - s, r + s)
                    route(r * 2 + s, s, r)
            project(NT - 1, 1, NT // 2 - 1)
            route(NT - 2, 0, NT // 2 - 1)
            route(NT - 1, 1, NT // 2 - 1)

        @block.scalar
        def _(act):
            def stage(i, s, r):
                act.wait_ge(mixed, i + 1)
                act.activation(mt[s][:, :, :], mixT[:, :, bass.ds(i * P, P)], ACT.Copy).then_inc(staged, 1)

            def norms(i, s, r):
                chain = Chain(act, astep, i * A_STEPS)
                act.wait_ge(mixed, i + 3)
                act.wait_ge(dstep, i * D_STEPS + 4)
                chain.link(act.activation(junk[:, :], M[s][:, :], ACT.Square, scale=D ** -0.5, accum_out=ms[s][:, 0:1]))
                chain.link(act.activation(ms[s][:, 0:1], ms[s][:, 0:1], ACT.Sqrt, bias=g.eps[:, :]))
                act.wait_ge(dstep, i * D_STEPS + (CREDIT + 3))
                chain.link(act.activation(junk[:, :], x1[:, bass.ds(i, 1), :].rearrange("p a n -> p (a n)"), ACT.Square,
                                          scale=D ** -0.5, accum_out=ms[s][:, 1:2]))
                chain.link(act.activation(ms[s][:, 1:2], ms[s][:, 1:2], ACT.Sqrt, bias=g.eps[:, :]))
                act.wait_ge(turned, i + 1)
                act.wait_ge(routed, i + 1)
                act.activation(h2T[:, 0:4, :], TP[:, 0:512].rearrange("p (k t) -> p k t", t=P), ACT.Copy).then_inc(out_a, 1)

            act.sem_inc(mixed, 2)
            over_tiles(act, stage, norms)

        @block.gpsimd
        def _(pool):
            with pool.Fori(0, NT // 2) as r:
                for s in range(2):
                    i = r * 2 + s
                    pool.wait_ge(dstep, i * D_STEPS + (CREDIT + 5))
                    pool.tensor_tensor(h2[s][:, :], h2[s][:, :], mod[:, SH_F], ALU.add).then_inc(shifted, 1)

        @block.vector
        def _(dve):
            dve.sem_inc(dstep, CREDIT)
            dve.sem_inc(out_d, 1)
            dve.sem_inc(out_a, 1)
            dve.sem_inc(logit, 1)
            dve.sem_inc(routed, 1)
            dve.sem_inc(added, 2)
            with dve.Fori(0, 4 * D // 1024) as r:
                for b in range(2):
                    n = r * 2 + b
                    dve.wait_ge(summed, n + 1)
                    dve.tensor_copy(mod[:, bass.ds(n * 512, 512)], SUM[b]).then_inc(added, 1)
            dve.wait_ge(added, 2 + 4 * D // 512)
            dve.wait_ge(gains, 48)
            for n, (part, plus) in enumerate(((GT_M, 0.0), (SC_F, 1.0), (GT_F, 0.0))):
                dve.scalar_tensor_tensor(out=mod[:, part], in0=mod[:, part], scalar=plus, in1=gain[n][:, :],
                                         op0=ALU.add, op1=ALU.mult).then_inc(added, 1)
            dve.wait_ge(added, 2 + 4 * D // 512 + 3)
            dve.wait_ge(out_loaded, 64)
            with dve.Fori(0, NT // 2) as r:
                for s in range(2):
                    i = r * 2 + s
                    x1_i = x1[:, bass.ds(i, 1), :].rearrange("p a n -> p (a n)")
                    chain = Chain(dve, dstep, i * D_STEPS + CREDIT)
                    dve.wait_ge(astep, i * A_STEPS + 2)
                    chain.link(dve.reciprocal(rstd[s][:, 0:1], ms[s][:, 0:1]))
                    chain.link(dve.scalar_tensor_tensor(out=scaled[s][:, :], in0=M[s][:, :], scalar=rstd[s][:, 0:1],
                                                        in1=mod[:, GT_M], op0=ALU.mult, op1=ALU.mult))
                    dve.wait_ge(x_loaded[s], r * 16 + 16)
                    chain.link(dve.tensor_tensor(x1_i, scaled[s][:, :], x[s][:, :], ALU.add))
                    dve.wait_ge(astep, i * A_STEPS + 4)
                    chain.link(dve.reciprocal(rstd[s][:, 1:2], ms[s][:, 1:2]))
                    dve.wait_ge(stored[s], r * 16 + 16)
                    chain.link(dve.scalar_tensor_tensor(out=h2[s][:, :], in0=x1_i, scalar=rstd[s][:, 1:2],
                                                        in1=mod[:, SC_F], op0=ALU.mult, op1=ALU.mult))
                    dve.wait_ge(turned, i + 1)
                    dve.wait_ge(routed, i + 1)
                    dve.tensor_copy(h2T[:, 4:8, :], TP[:, 512:D].rearrange("p (k t) -> p k t", t=P)).then_inc(out_d, 1)
                    dve.wait_ge(routed, i + 2)
                    dve.tensor_tensor(logits[:, bass.ds(i, 1), :], LG[:, :].unsqueeze(1), br[:, :].unsqueeze(1), ALU.add
                                      ).then_inc(logit, 1)



def route(nc, g, d, expert_weights, logits, rows, weights, ids, overflow):
    with ExitStack() as ctx:
        sb, ps, sem = allocator(nc, ctx)
        E, T2 = N_EXP, 2 * NT
        gpad = sb("gpad", [P, NT, 8])
        gtop = sb("gtop", [P, NT, 8])
        gidx = sb("gidx", [P, NT, 8], U32)
        gsub = sb("gsub", [P, NT, N_GRP])
        gsum = sb("gsum", [P, NT])
        pg = sb("pg", [P, NT])
        gif = sb("gif", [P, NT])
        grp_of = sb("grp_of", [P, E])
        exp_no = sb("exp_no", [P, E])
        in_grp = sb("in_grp", [P, NT, E])
        outside = sb("outside", [P, NT, E])
        masked = sb("masked", [P, NT, E])
        etop = sb("etop", [P, NT, 8])
        eidx = sb("eidx", [P, NT, 8], U32)
        ef = sb("ef", [P, 2, NT])
        diff = sb("diff", [P, NT])
        den = sb("den", [P, NT])
        one_hot = sb("one_hot", [P, 2, NT, E])
        prefix = sb("prefix", [P, NT + 1, E])
        both = sb("both", [P, NT, E])
        before = sb("before_me", [P, P])
        rank_all = sb("rank_all", [P, NT, E])
        picked = sb("picked", [P, 2, NT, E])
        rank = sb("rank", [P, 2, NT])
        over = sb("over_no", [P, 2, NT])
        start = sb("over_start", [P, 2, NT])
        n_over = sb("n_over", [P, E])
        over_end = sb("over_end", [P, E])
        over_beg = sb("over_beg", [P, E])
        zero = sb("rzero", [P, E])
        place = sb("place", [P, 2, NT])
        col = sb("colno", [P, 2, NT])
        tmp = sb("rtmp", [P, 2, NT])
        block_no = sb("block_no", [P, N_OVF + 1])
        cmpb = sb("cmpb", [P, N_OVF + 1, E])
        bexp = sb("bexp", [P, N_OVF + 1])
        token = sb("token_no", [P, NT])
        slot_no = sb("slot_no", [P, P])
        col_no = sb("col_no", [P, N_COL])
        at_slot = sb("at_slot", [P, T2, P])
        at_block = sb("at_block", [P, T2, N_COL])
        R = ps("rank_ps", [P, NT * E])
        C = ps("count_ps", [P, E])
        ID = ps("ids_ps", [P, N_COL])
        made, step, ranked, aexp = (sem(f"r_{n}") for n in ("made", "step", "ranked", "aexp"))
        counted = {}
        block = ctx.enter_context(nc.Block())

        def per_token(ap):
            return ap.unsqueeze(2).to_broadcast([P, NT, E])

        def per_expert(ap):
            return ap.unsqueeze(1).to_broadcast([P, NT, E])

        @block.vector
        def _(dve):
            chain = Chain(dve, step)
            link = chain.link
            dve.wait_ge(made, 11)
            link(dve.tensor_copy(gpad[:, :, 0:N_GRP], logits[:, :, 0:N_GRP]))
            for i in range(NT):
                last = dve.max(gtop[:, i, :], gpad[:, i, :])
            link(last)
            for i in range(NT):
                last = dve.max_index(gidx[:, i, :], gtop[:, i, :], gpad[:, i, :])
            link(last)
            link(dve.tensor_tensor(gsub[:, :, :], logits[:, :, 0:N_GRP],
                                   gtop[:, :, 0:1].to_broadcast([P, NT, N_GRP]), ALU.subtract))
            counted["gsub"] = chain.n
            link(dve.tensor_copy(gif[:, :], gidx[:, :, 0]))
            link(dve.tensor_tensor(in_grp[:, :, :], per_expert(grp_of[:, :]), per_token(gif[:, :]), ALU.is_equal))
            link(dve.tensor_scalar(outside[:, :, :], in_grp[:, :, :], BIG, -BIG, ALU.mult, ALU.add))
            link(dve.tensor_tensor(masked[:, :, :], logits[:, :, N_GRP:], in_grp[:, :, :], ALU.mult))
            link(dve.tensor_tensor(masked[:, :, :], masked[:, :, :], outside[:, :, :], ALU.add))
            for i in range(NT):
                last = dve.max(etop[:, i, :], masked[:, i, :])
            link(last)
            for i in range(NT):
                last = dve.max_index(eidx[:, i, :], etop[:, i, :], masked[:, i, :])
            link(last)
            link(dve.tensor_tensor(diff[:, :], etop[:, :, 1], etop[:, :, 0], ALU.subtract))
            counted["diff"] = chain.n
            for k in range(2):
                last = dve.tensor_copy(ef[:, k, :], eidx[:, :, k])
            link(last)
            for k in range(2):
                last = dve.tensor_tensor(one_hot[:, k, :, :], per_expert(exp_no[:, :]), per_token(ef[:, k, :]), ALU.is_equal)
            link(last)
            link(dve.tensor_tensor(both[:, :, :], one_hot[:, 0, :, :], one_hot[:, 1, :, :], ALU.add))
            for i in range(NT):
                link(dve.tensor_tensor(prefix[:, i + 1, :], prefix[:, i, :], both[:, i, :], ALU.add))
            counted["prefix"] = chain.n
            dve.wait_ge(aexp, 2)
            link(dve.tensor_reduce(gsum[:, :], gsub[:, :, :], AX.X, ALU.add))
            link(dve.reciprocal(pg[:, :], gsum[:, :]))
            link(dve.tensor_scalar_add(den[:, :], diff[:, :], 1.0))
            link(dve.reciprocal(den[:, :], den[:, :]))
            link(dve.tensor_tensor(weights[:, 0, :], pg[:, :], den[:, :], ALU.mult))
            link(dve.tensor_tensor(weights[:, 1, :], weights[:, 0, :], diff[:, :], ALU.mult))
            dve.wait_ge(ranked, 1)
            link(dve.tensor_copy(rank_all[:, :, :], R[:, :].rearrange("p (t e) -> p t e", e=E)))
            for k in range(2):
                last = dve.tensor_tensor(picked[:, k, :, :], one_hot[:, k, :, :], rank_all[:, :, :], ALU.mult)
            link(last)
            link(dve.tensor_reduce(rank[:, :, :], picked[:, :, :, :], AX.X, ALU.add))
            link(dve.tensor_scalar(n_over[:, :], C[:, :], float(P), None, ALU.is_gt))
            for m in range(2, S // P):
                link(dve.scalar_tensor_tensor(out=n_over[:, :], in0=C[:, :], scalar=float(m * P), in1=n_over[:, :],
                                              op0=ALU.is_gt, op1=ALU.add))
            link(dve.tensor_tensor_scan(over_end[:, :], n_over[:, :], zero[:, :], 0.0, ALU.add, ALU.add))
            link(dve.tensor_tensor(over_beg[:, :], over_end[:, :], n_over[:, :], ALU.subtract))
            for k in range(2):
                last = dve.tensor_tensor(picked[:, k, :, :], one_hot[:, k, :, :], per_expert(over_beg[:, :]), ALU.mult)
            link(last)
            link(dve.tensor_reduce(start[:, :, :], picked[:, :, :, :], AX.X, ALU.add))
            link(dve.tensor_scalar(over[:, :, :], rank[:, :, :], float(P), None, ALU.is_ge))
            for m in range(2, S // P):
                link(dve.scalar_tensor_tensor(out=over[:, :, :], in0=rank[:, :, :], scalar=float(m * P),
                                              in1=over[:, :, :], op0=ALU.is_ge, op1=ALU.add))
            link(dve.scalar_tensor_tensor(out=place[:, :, :], in0=over[:, :, :], scalar=-float(P), in1=rank[:, :, :],
                                          op0=ALU.mult, op1=ALU.add))
            link(dve.scalar_tensor_tensor(out=tmp[:, :, :], in0=over[:, :, :], scalar=float(E - 1), in1=start[:, :, :],
                                          op0=ALU.add, op1=ALU.add))
            link(dve.tensor_tensor(tmp[:, :, :], tmp[:, :, :], ef[:, :, :], ALU.subtract))
            link(dve.scalar_tensor_tensor(out=tmp[:, :, :], in0=over[:, :, :], scalar=1.0, in1=tmp[:, :, :],
                                          op0=ALU.min, op1=ALU.mult))
            link(dve.tensor_tensor(col[:, :, :], tmp[:, :, :], ef[:, :, :], ALU.add))
            link(dve.tensor_tensor(at_slot[:, :, :], slot_no[:, :].unsqueeze(1).to_broadcast([P, T2, P]),
                                   place[:, :, :].rearrange("p k t -> p (k t)").unsqueeze(2).to_broadcast([P, T2, P]),
                                   ALU.is_equal))
            link(dve.tensor_tensor(at_block[:, :, :], col_no[:, :].unsqueeze(1).to_broadcast([P, T2, N_COL]),
                                   col[:, :, :].rearrange("p k t -> p (k t)").unsqueeze(2).to_broadcast([P, T2, N_COL]),
                                   ALU.is_equal))
            for k in range(2):
                last = dve.tensor_tensor(at_block[:, k * NT:(k + 1) * NT, :], at_block[:, k * NT:(k + 1) * NT, :],
                                         token[:, :].unsqueeze(2).to_broadcast([P, NT, N_COL]), ALU.mult)
            link(last)
            counted["slots"] = chain.n
            link(dve.scalar_tensor_tensor(out=rows[:, :, :], in0=col[:, :, :], scalar=float(P), in1=place[:, :, :],
                                          op0=ALU.mult, op1=ALU.add))
            link(dve.tensor_tensor(cmpb[:, :, :], over_end[:, :].unsqueeze(1).to_broadcast([P, N_OVF + 1, E]),
                                   block_no[:, :].unsqueeze(2).to_broadcast([P, N_OVF + 1, E]), ALU.is_le))
            link(dve.tensor_reduce(bexp[:, :], cmpb[:, :, :], AX.X, ALU.add))
            link(dve.tensor_scalar(overflow[:, 1:], bexp[:, :], float(E - 1), None, ALU.min))
            link(dve.tensor_copy(overflow[:, 0:1], over_end[:, E - 1:E]))
            dve.wait_ge(ranked, 2)
            link(dve.tensor_copy(ids[:, :], ID[:, :]))

        @block.scalar
        def _(act):
            act.wait_ge(step, counted["gsub"])
            act.activation(gsub[:, :, :], gsub[:, :, :], ACT.Exp).then_inc(aexp, 1)
            act.wait_ge(step, counted["diff"])
            act.activation(diff[:, :], diff[:, :], ACT.Exp).then_inc(aexp, 1)

        @block.tensor
        def _(pe):
            pe.wait_ge(step, counted["prefix"])
            pe.wait_ge(made, 11)
            pe.matmul(R[:, :], before[:, :], both[:, :, :].rearrange("p t e -> p (t e)"), start=True, stop=False)
            pe.matmul(R[:, :], g.ones[:, :], prefix[:, 0:NT, :].rearrange("p t e -> p (t e)"), start=False, stop=True)
            pe.matmul(C[:, :], g.ones[:, :], prefix[:, NT, :], start=True, stop=True).then_inc(ranked, 1)
            pe.wait_ge(step, counted["slots"])
            for n in range(T2):
                last = pe.matmul(ID[:, :], at_slot[:, n, :], at_block[:, n, :], start=(n == 0), stop=(n == T2 - 1))
            last.then_inc(ranked, 1)

        @block.sync
        def _(sp):
            expert_weights.load_gate_up(sp, d, 1, 1)
            expert_weights.load_down(sp, d, 0, 0)

        @block.gpsimd
        def _(pool):
            flt = dict(allow_small_or_imprecise_dtypes=True)
            pool.memset(gpad[:, :, :], -BIG).then_inc(made, 1)
            pool.memset(prefix[:, 0, :], 0.0).then_inc(made, 1)
            pool.memset(zero[:, :], 0.0).then_inc(made, 1)
            pool.memset(before[:, :], 1.0).then_inc(made, 1)
            pool.iota(grp_of[:, :], pattern=[[1, N_GRP], [0, PER_GRP]], base=0, channel_multiplier=0, **flt).then_inc(made, 1)
            pool.iota(exp_no[:, :], pattern=[[1, E]], base=0, channel_multiplier=0, **flt).then_inc(made, 1)
            pool.iota(block_no[:, :], pattern=[[1, N_OVF + 1]], base=0, channel_multiplier=0, **flt).then_inc(made, 1)
            pool.iota(token[:, :], pattern=[[P, NT]], base=0, channel_multiplier=1, **flt).then_inc(made, 1)
            pool.iota(slot_no[:, :], pattern=[[1, P]], base=0, channel_multiplier=0, **flt).then_inc(made, 1)
            pool.iota(col_no[:, :], pattern=[[1, N_COL]], base=0, channel_multiplier=0, **flt).then_inc(made, 1)
            pool.wait_ge(made, 10)
            pool.affine_select(out=before[:, :], in_=before[:, :], compare_op=ALU.is_gt, fill=0.0, base=0,
                               pattern=[[1, P]], channel_multiplier=-1).then_inc(made, 1)



class ExpertWeights:

    def __init__(self, sb, sem, room):
        KD = D_EXP // P
        self.gate, self.up = [], []
        self.add_slot(sb)
        self.down = [room[:, s * KD * D:(s + 1) * KD * D].rearrange("p (k n) -> p k n", n=D) for s in range(2)]
        self.gu_loaded = [sem(f"e_gu_loaded{s}") for s in range(2)]
        self.d_loaded = [sem(f"e_d_loaded{s}") for s in range(2)]

    def add_slot(self, sb):
        self.gate.append(sb(f"wgate{len(self.gate)}", [P, ND, D_EXP]))
        self.up.append(sb(f"wup{len(self.up)}", [P, ND, D_EXP]))

    def load_gate_up(self, eng, d, e, s):
        for w, source in ((self.gate, d["w_exp_gate"]), (self.up, d["w_exp_up"])):
            eng.dma_start(w[s][:, :, :], source[0, bass.ds(e, 1)].rearrange("a (k p) n -> p (a k) n", p=P)
                          ).then_inc(self.gu_loaded[s], 16)

    def load_down(self, eng, d, e, s):
        eng.dma_start(self.down[s][:, :, :], d["w_exp_down"][0, bass.ds(e, 1)].rearrange("a (k p) n -> p (a k) n", p=P)
                      ).then_inc(self.d_loaded[s], 16)


def experts(nc, g, d, w, ids, overflow, h2_dram, y_dram, mod):
    KD = D_EXP // P
    with ExitStack() as ctx:
        sb, ps, sem = allocator(nc, ctx)
        idx = [sb(f"idx{s}", [P, 1], U32) for s in range(2)]
        xb = [sb(f"xb{s}", [P, D]) for s in range(2)]
        xT = [sb(f"xT{s}", [P, ND, P]) for s in range(2)]
        sig = sb("sig", [P, D_EXP])
        prod = sb("gu", [P, D_EXP])
        aT_hi, aT_lo = (sb(f"aT_{n}", [P, KD, P], F32R) for n in ("hi", "lo"))
        d_hi, d_lo = (sb(f"w_down_{n}", [P, KD, D], F32R) for n in ("hi", "lo"))
        y = [mod[:, s * D:(s + 1) * D] for s in range(2)]
        spare = sb("spare", [P, 1])
        carried = sem("e_carried")
        TX = ps("TX", [P, D])
        GP = [ps(f"GP{s}", [P, D_EXP]) for s in range(2)]
        UP = ps("UP", [P, D_EXP])
        TA = ps("TA", [P, D_EXP])
        YP = ps("YP", [P, D])
        d_hi_done, d_lo_done, a_hi_done = (sem(f"e_{n}") for n in ("d_hi_done", "d_lo_done", "a_hi_done"))
        PARTS = (slice(0, KD // 2), slice(KD // 2, KD))
        x_loaded = [sem(f"e_x_loaded{s}") for s in range(2)]
        y_stored = [sem(f"e_y_stored{s}") for s in range(2)]
        (copied, x_turned, x_out_a, x_out_d, gate_done, gu_done, exped, step, a_turned, a_out, down_done, y_out) = (
            sem(f"e_{n}") for n in ("copied", "x_turned", "x_out_a", "x_out_d", "gate_done", "gu_done", "exped",
                                    "step", "a_turned", "a_out", "down_done", "y_out"))
        block = ctx.enter_context(nc.Block())

        def over_overflow(eng, body):
            used = eng.value_load(overflow[0:1, 0:1], min_val=0, max_val=N_OVF)
            with eng.Fori(0, (N_OVF + 1) // 4) as q:
                with eng.If(used > q * 4):
                    with eng.Fori(0, 2) as half:
                        j = q * 2 + half
                        for s in range(2):
                            with eng.If(used > j * 2 + s):
                                body(j * 2 + (N_EXP + s), s, j + N_EXP // 2)

        @block.sync
        def _(sp):
            def gate_up(e, b, s):
                sp.wait_ge(gu_done, b + 1)
                w.load_gate_up(sp, d, e, s)

            def down(e, b, s):
                sp.wait_ge(down_done, b + 1)
                w.load_down(sp, d, e, s)

            with sp.Fori(0, N_EXP // 2 - 1) as r:
                down(r * 2 + 1, r * 2 + 1, 1)
                gate_up(r * 2 + 2, r * 2 + 2, 0)
                down(r * 2 + 2, r * 2 + 2, 0)
                gate_up(r * 2 + 3, r * 2 + 3, 1)
            down(N_EXP - 1, N_EXP - 1, 1)

            def more(b, s, r):
                e = sp.value_load(overflow[0:1, bass.ds(b - (N_EXP - 1), 1)], min_val=0, max_val=N_EXP - 1)
                gate_up(e, b, s)
                down(e, b, s)

            over_overflow(sp, more)

        @block.gpsimd
        def _(pool):
            count = pool.alloc_register("e_count")

            def gather(b, s, r):
                pool.reg_mov(count, b + 1)
                pool.wait_ge(x_turned, count)
                pool.tensor_copy(idx[s][:, :], ids[:, bass.ds(b, 1)]).then_inc(copied, 1)
                pool.reg_mov(count, b + 1)
                pool.wait_ge(x_turned, 1)
                pool.wait_ge(copied, count)
                pool.indirect_dma_start(out=xb[s][:, :], out_offset=None, in_=h2_dram,
                                        in_offset=bass.IndirectOffsetOnAxis(ap=idx[s][:, :], axis=0)
                                        ).then_inc(x_loaded[s], 16)

            with pool.Fori(0, N_EXP // 2) as r:
                gather(r * 2, 0, r)
                gather(r * 2 + 1, 1, r)
            over_overflow(pool, gather)

        @block.tensor
        def _(pe):
            def turn_x(b, s, r):
                pe.wait_ge(x_loaded[s], r * 16 + 16)
                pe.wait_ge(x_out_a, b + 1)
                pe.wait_ge(x_out_d, b + 1)
                for k in range(ND):
                    last = pe.transpose(TX[:, k * P:(k + 1) * P], xb[s][:, k * P:(k + 1) * P], g.ident[:, :])
                last.then_inc(x_turned, 1)

            def gate_up(b, s, r, between=None):
                pe.wait_ge(w.gu_loaded[s], r * 32 + 32)
                pe.wait_ge(x_out_a, b + 2)
                pe.wait_ge(x_out_d, b + 2)
                pe.wait_ge(step, b * 4 + 4)
                for k in range(ND):
                    last = pe.matmul(GP[s][:, :], xT[s][:, k, :], w.gate[s][:, k, :], start=(k == 0), stop=(k == ND - 1))
                last.then_inc(gate_done, 1)
                if between is not None:
                    between()
                pe.wait_ge(step, b * 4 + 8)
                for k in range(ND):
                    last = pe.matmul(UP[:, :], xT[s][:, k, :], w.up[s][:, k, :], start=(k == 0), stop=(k == ND - 1))
                last.then_inc(gu_done, 1)

            def turn_product(b):
                pe.wait_ge(step, b * 4 + 12)
                pe.wait_ge(a_out, b + 1)
                for k in range(KD):
                    last = pe.transpose(TA[:, k * P:(k + 1) * P], prod[:, k * P:(k + 1) * P], g.ident[:, :])
                last.then_inc(a_turned, 1)

            def down(b, s, r):
                pe.wait_ge(a_out, b + 2)
                pe.wait_ge(d_lo_done, b * 2 + 2)
                pe.wait_ge(y_out, b + 1)
                for half in range(2):
                    cols = slice(half * 512, (half + 1) * 512)
                    for k in range(KD):
                        pe.matmul(YP[:, cols], aT_hi[:, k, :], d_hi[:, k, cols], start=(k == 0), stop=False)
                        pe.matmul(YP[:, cols], aT_hi[:, k, :], d_lo[:, k, cols], start=False, stop=False)
                        last = pe.matmul(YP[:, cols], aT_lo[:, k, :], d_hi[:, k, cols], start=False, stop=(k == KD - 1))
                last.then_inc(down_done, 1)

            pe.sem_inc(gu_done, 2)
            pe.sem_inc(down_done, 2)
            pe.sem_inc(x_turned, 2)
            turn_x(0, 0, 0)
            gate_up(0, 0, 0)
            turn_x(1, 1, 0)

            def round_(b, s, r, next_x=True):
                gate_up(b, s, r, between=lambda: turn_product(b - 1))
                if next_x:
                    turn_x(b + 1, 1 - s, r + s)
                down(b - 1, 1 - s, r - (1 - s))

            with pe.Fori(0, N_EXP // 2 - 1) as r:
                round_(r * 2 + 1, 1, r)
                round_(r * 2 + 2, 0, r + 1)
            round_(N_EXP - 1, 1, N_EXP // 2 - 1, next_x=False)
            turn_product(N_EXP - 1)
            down(N_EXP - 1, 1, N_EXP // 2 - 1)

            def more(b, s, r):
                turn_x(b, s, r)
                gate_up(b, s, r)
                turn_product(b)
                down(b, s, r)

            over_overflow(pe, more)

        @block.scalar
        def _(act):
            def x_out(b, s):
                act.wait_ge(x_turned, b + 3)
                act.wait_ge(gu_done, b + 1)
                act.activation(xT[s][:, 0:4, :], TX[:, 0:512].rearrange("p (k t) -> p k t", t=P), ACT.Copy
                               ).then_inc(x_out_a, 1)

            def exp(b, s):
                act.wait_ge(gate_done, b + 1)
                act.wait_ge(step, b * 4 + 8)
                act.activation(sig[:, :], GP[s][:, :], ACT.Exp, scale=-1.0).then_inc(exped, 1)

            def split_down(b, s, r):
                act.wait_ge(w.d_loaded[s], r * 16 + 16)
                act.wait_ge(down_done, b + 2)
                for ks in PARTS:
                    act.activation(d_hi[:, ks, :], w.down[s][:, ks, :], ACT.Copy).then_inc(d_hi_done, 1)

            def product_hi(b):
                act.wait_ge(a_turned, b + 2)
                act.wait_ge(down_done, b + 2)
                act.activation(aT_hi[:, :, :], TA[:, :].rearrange("p (k t) -> p k t", t=P), ACT.Copy).then_inc(a_hi_done, 1)

            def store(b, s, r):
                act.wait_ge(down_done, b + 3)
                act.wait_ge(y_stored[s], r * 16 + 16)
                act.activation(y[s][:, :], YP[:, :], ACT.Copy).then_inc(y_out, 1)
                act.wait_ge(y_out, b + 2)
                act.dma_start(y_dram[bass.ds(b * P, P), :], y[s][:, :]).then_inc(y_stored[s], 16)

            for s in range(2):
                act.sem_inc(y_stored[s], 16)
            act.sem_inc(x_out_a, 1)
            act.sem_inc(y_out, 1)
            x_out(0, 0)
            exp(0, 0)
            x_out(1, 1)

            def round_(b, s, r, next_x=True):
                split_down(b - 1, 1 - s, r - (1 - s))
                exp(b, s)
                product_hi(b - 1)
                if next_x:
                    x_out(b + 1, 1 - s)
                store(b - 1, 1 - s, r - (1 - s))

            with act.Fori(0, N_EXP // 2 - 1) as r:
                round_(r * 2 + 1, 1, r)
                round_(r * 2 + 2, 0, r + 1)
            round_(N_EXP - 1, 1, N_EXP // 2 - 1, next_x=False)
            split_down(N_EXP - 1, 1, N_EXP // 2 - 1)
            product_hi(N_EXP - 1)
            store(N_EXP - 1, 1, N_EXP // 2 - 1)

            def more(b, s, r):
                x_out(b, s)
                exp(b, s)
                split_down(b, s, r)
                product_hi(b)
                store(b, s, r)
                act.wait_ge(y_stored[s], r * 16 + 32)
                act.wait_ge(carried, b - (N_EXP - 1))
                act.activation(spare[:, :], g.eps[:, :], ACT.Copy).then_inc(carried, 1)

            act.sem_inc(carried, 1)
            over_overflow(act, more)
            for s in range(2):
                act.wait_ge(y_stored[s], (N_EXP // 2 + 1) * 16)

        @block.vector
        def _(dve):
            def x_out(b, s):
                dve.wait_ge(x_turned, b + 3)
                dve.wait_ge(gu_done, b + 1)
                dve.tensor_copy(xT[s][:, 4:8, :], TX[:, 512:D].rearrange("p (k t) -> p k t", t=P)).then_inc(x_out_d, 1)

            def sigmoid(b):
                dve.wait_ge(exped, b + 1)
                chain = Chain(dve, step, b * 4 + 8)
                chain.link(dve.tensor_scalar_add(sig[:, :], sig[:, :], 1.0))
                chain.link(dve.reciprocal(sig[:, :], sig[:, :]))

            def multiply(b, s):
                dve.wait_ge(gu_done, b + 3)
                dve.wait_ge(a_turned, b + 1)
                chain = Chain(dve, step, b * 4 + 10)
                chain.link(dve.tensor_tensor(prod[:, :], sig[:, :], GP[s][:, :], ALU.mult))
                chain.link(dve.tensor_tensor(prod[:, :], prod[:, :], UP[:, :], ALU.mult))

            def split_down(b, s):
                for p, ks in enumerate(PARTS):
                    dve.wait_ge(d_hi_done, b * 2 + (p + 1))
                    dve.tensor_tensor(d_lo[:, ks, :], w.down[s][:, ks, :], d_hi[:, ks, :].bitcast(F32), ALU.subtract
                                      ).then_inc(d_lo_done, 1)

            def product_out(b):
                dve.wait_ge(a_hi_done, b + 1)
                dve.tensor_tensor(aT_lo[:, :, :], TA[:, :].rearrange("p (k t) -> p k t", t=P),
                                  aT_hi[:, :, :].bitcast(F32), ALU.subtract).then_inc(a_out, 1)

            dve.sem_inc(x_out_d, 1)
            dve.sem_inc(step, 8)
            dve.sem_inc(a_out, 1)
            dve.sem_inc(a_turned, 1)
            x_out(0, 0)
            sigmoid(0)
            x_out(1, 1)
            multiply(0, 0)

            def round_(b, s, r, next_x=True):
                split_down(b - 1, 1 - s)
                sigmoid(b)
                product_out(b - 1)
                if next_x:
                    x_out(b + 1, 1 - s)
                multiply(b, s)

            with dve.Fori(0, N_EXP // 2 - 1) as r:
                round_(r * 2 + 1, 1, r)
                round_(r * 2 + 2, 0, r + 1)
            round_(N_EXP - 1, 1, N_EXP // 2 - 1, next_x=False)
            split_down(N_EXP - 1, 1)
            product_out(N_EXP - 1)

            def more(b, s, r):
                x_out(b, s)
                sigmoid(b)
                split_down(b, s)
                multiply(b, s)
                product_out(b)

            over_overflow(dve, more)


def combine(nc, g, d, rows, weights, x1, mod, y_dram, out):
    GT_F = slice(3 * D, 4 * D)
    SLOTS = 4
    with ExitStack() as ctx:
        sb, ps, sem = allocator(nc, ctx)
        idx = [[sb(f"c_idx{s}{k}", [P, 1], U32) for k in range(2)] for s in range(SLOTS)]
        yk = [[sb(f"c_y{s}{k}", [P, D]) for k in range(2)] for s in range(SLOTS)]
        wk = [sb(f"c_w{s}", [P, 2]) for s in range(SLOTS)]
        total = [sb(f"c_sum{s}", [P, D]) for s in range(SLOTS)]
        ms = [sb(f"c_ms{s}", [P, 1]) for s in range(SLOTS)]
        rstd = [sb(f"c_rstd{s}", [P, 1]) for s in range(SLOTS)]
        junk = sb("c_junk", [P, D])
        loaded = [sem(f"c_loaded{s}") for s in range(SLOTS)]
        stored = [sem(f"c_stored{s}") for s in range(SLOTS)]
        copied, weighed, summed, normed, finish = (
            sem(f"c_{n}") for n in ("copied", "weighed", "summed", "normed", "finish"))
        D_STEPS, CREDIT = 3, 3 * SLOTS
        block = ctx.enter_context(nc.Block())

        @block.gpsimd
        def _(pool):
            count = pool.alloc_register("c_count")
            with pool.Fori(0, NT // SLOTS) as r:
                for s in range(SLOTS):
                    i = r * SLOTS + s
                    pool.reg_mov(count, i + 1)
                    pool.wait_ge(summed, count)
                    pool.tensor_copy(wk[s][:, :], weights[:, :, bass.ds(i, 1)].rearrange("p k a -> p (k a)")
                                     ).then_inc(copied, 1)
                    for k in range(2):
                        pool.tensor_copy(idx[s][k][:, :], rows[:, k, bass.ds(i, 1)]).then_inc(copied, 1)
                    pool.reg_mov(count, i * 3 + 3)
                    for k in range(2):
                        pool.wait_ge(summed, 1)
                        pool.wait_ge(copied, count)
                        pool.indirect_dma_start(out=yk[s][k][:, :], out_offset=None, in_=y_dram,
                                                in_offset=bass.IndirectOffsetOnAxis(ap=idx[s][k][:, :], axis=0)
                                                ).then_inc(loaded[s], 16)

        @block.vector
        def _(dve):
            def add(i, s, r):
                dve.wait_ge(weighed, i + 1)
                dve.scalar_tensor_tensor(out=total[s][:, :], in0=yk[s][1][:, :], scalar=wk[s][:, 1:2],
                                         in1=total[s][:, :], op0=ALU.mult, op1=ALU.add).then_inc(summed, 1)

            def norm(i, s, r):
                chain = Chain(dve, finish, i * D_STEPS + CREDIT)
                dve.wait_ge(normed, i * 2 + 2)
                chain.link(dve.reciprocal(rstd[s][:, :], ms[s][:, :]))
                chain.link(dve.scalar_tensor_tensor(out=total[s][:, :], in0=total[s][:, :], scalar=rstd[s][:, :],
                                                    in1=mod[:, GT_F], op0=ALU.mult, op1=ALU.mult))
                chain.link(dve.tensor_tensor(total[s][:, :], total[s][:, :],
                                             x1[:, bass.ds(i, 1), :].rearrange("p a n -> p (a n)"), ALU.add))

            dve.sem_inc(finish, CREDIT)
            dve.sem_inc(summed, SLOTS)
            over_tiles(dve, add, norm, SLOTS)

        @block.scalar
        def _(act):
            def weigh(i, s, r):
                act.wait_ge(loaded[s], r * 32 + 32)
                act.wait_ge(copied, i * 3 + 1)
                act.wait_ge(stored[s], r * 16 + 16)
                act.activation(total[s][:, :], yk[s][0][:, :], ACT.Copy, scale=wk[s][:, 0:1]).then_inc(weighed, 1)

            def square(i, s, r):
                chain = Chain(act, normed, i * 2)
                act.wait_ge(summed, i + (SLOTS + 1))
                act.wait_ge(finish, i * D_STEPS + 1)
                chain.link(act.activation(junk[:, :], total[s][:, :], ACT.Square, scale=D ** -0.5, accum_out=ms[s][:, :]))
                chain.link(act.activation(ms[s][:, :], ms[s][:, :], ACT.Sqrt, bias=g.eps[:, :]))

            over_tiles(act, weigh, square, SLOTS)

        @block.sync
        def _(sp):
            for s in range(SLOTS):
                sp.sem_inc(stored[s], 16)
            with sp.Fori(0, NT // SLOTS) as r:
                for s in range(SLOTS):
                    i = r * SLOTS + s
                    sp.wait_ge(finish, i * D_STEPS + (CREDIT + 3))
                    sp.dma_start(out[0, bass.ds(i * P, P), :], total[s][:, :]).then_inc(stored[s], 16)
            for s in range(SLOTS):
                sp.wait_ge(stored[s], (NT // SLOTS + 1) * 16)


def decoder_block(nc, d, out):
    fsum_dram = nc.dram_tensor("fsum", [FOX_HEADS, S], F32).ap()
    h2_dram = nc.dram_tensor("h2_rows", [S, D], F32).ap()
    y_dram = nc.dram_tensor("expert_rows", [N_COL * P, D], F32).ap()
    with ExitStack() as ctx:
        sb, _, sem = allocator(nc, ctx)
        g = Constants(sb)
        room = sb("room", [P, ND * S])
        mixT = room[:, :].rearrange("p (k t) -> p k t", t=S)
        constants(nc, g, d)
        with ExitStack() as mixers:
            msb, _, _ = allocator(nc, mixers)
            hT = msb("hT", [P, ND, S])
            yaT, ybT = msb("yaT", [P, NSA_HEADS * HD // P, S]), msb("ybT", [P, FOX_HEADS * HD // P, S])
            gates = msb("gates", [P, NT, 3 * NSA_HEADS])
            with ExitStack() as first:
                early = Early(allocator(nc, first)[0], sem)
                normalise_input(nc, g, d, hT, early, room)
                mixer_weights = MixerWeights(msb, sem)
                gates_and_forget(nc, g, d, mixer_weights, hT, early, gates, fsum_dram)
                fox(nc, g, d, mixer_weights, hT, ybT, fsum_dram, y_dram, room)
                nsa(nc, g, d, mixer_weights, early, hT, yaT, gates, room)
            mod = sb("mod_ffn", [P, 4 * D], side="right")
            late = ctx.enter_context(ExitStack())
            w_router = allocator(nc, late)[0]("w_router", [P, ND, N_GRP + N_EXP], side="right")
            b_router = allocator(nc, late)[0]("b_router", [P, N_GRP + N_EXP], side="right")
            out_loaded = sem("out_loaded")
            merge(nc, g, d, mixer_weights, hT, yaT, ybT, mixT, mod, w_router, b_router, out_loaded)
        x1 = sb("x1", [P, NT, D])
        expert_weights = ExpertWeights(sb, sem, room)
        logits = sb("logits", [P, NT, N_GRP + N_EXP])
        rows, weights = sb("rows", [P, 2, NT], U32), sb("weights", [P, 2, NT])
        ids = sb("ids", [P, N_COL], U32)
        overflow = sb("overflow", [P, 2 + N_OVF], I32)
        project_out(nc, g, d, mixT, mod, w_router, b_router, out_loaded, x1, logits, h2_dram, expert_weights)
        late.close()
        expert_weights.add_slot(sb)
        route(nc, g, d, expert_weights, logits, rows, weights, ids, overflow)
        experts(nc, g, d, expert_weights, ids, overflow, h2_dram, y_dram, mod)
        combine(nc, g, d, rows, weights, x1, mod, y_dram, out)


_INS = ['x', 'c', 'w_ada', 'b_ada', 'g_pre_mix', 'g_post_mix', 'g_pre_ffn', 'g_post_ffn', 'w_in', 'b_forget',
        'cmp_pe_k', 'cmp_w1_k', 'cmp_w2_k', 'cmp_pe_v', 'cmp_w1_v', 'cmp_w2_v', 'w_o_nsa', 'w_o_fox', 'w_out',
        'w_router_group', 'b_router_group', 'w_router_expert', 'b_router_expert',
        'w_exp_gate', 'w_exp_up', 'w_exp_down']


def kernel(**inputs):
    import numpy as _np
    import concourse.bacc as _bacc
    from concourse import mybir as _mybir
    from concourse.bass_utils import run_bass_kernel_spmd as _run

    nc = _bacc.Bacc("TRN2", target_bir_lowering=False, num_devices=1)
    arrays, d = {}, {}
    for name in _INS:
        a = _np.ascontiguousarray(inputs[name])
        arrays[f"in_{name}_dram"] = a
        d[name] = nc.dram_tensor(f"in_{name}_dram", a.shape, _mybir.dt.from_np(a.dtype),
                                          kind="ExternalInput").ap()
    out = nc.dram_tensor("out_0_dram", (1, S, D), F32, kind="ExternalOutput").ap()
    decoder_block(nc, d, out)
    r = _run(nc, [arrays], core_ids=[0])
    return r.results[0]["out_0_dram"]
```
